# Optimizing a Trainium2 kernel written in Bass

```python
import math
import jax, jax.numpy as jnp
from jax import lax
import numpy as np

D_MODEL = 1024
BATCH = 1
SEQ = 512
DEPTH = 1

MLA_HEADS = 8
MLA_NOPE = 64
MLA_ROPE = 32
MLA_V = 64
MLA_QK = MLA_NOPE + MLA_ROPE
MLA_Q_RANK = 384
MLA_KV_RANK = 256
ROPE_THETA = 10000.0
NSA_HEADS = 8
NSA_KV_HEADS = 2
NSA_GROUP = NSA_HEADS // NSA_KV_HEADS
NSA_HEAD_DIM = 64
N_BRANCH = 3
CMP_BLOCK = 32
CMP_STRIDE = 16
CMP_HIDDEN = 128
SEL_BLOCK = 64
SEL_TOP_N = 16
WINDOW = 512
FORCE_SCORE = 1e4
REL_BUCKETS = 32
REL_MAX_DIST = 128
D_FF = 4 * D_MODEL
Q_BLOCK = 128
SEL_Q_BLOCK = 64
EPS = 1e-6

MLA_OUT = MLA_HEADS * MLA_V
NSA_OUT = NSA_HEADS * NSA_HEAD_DIM
MIX_WIDTH = MLA_OUT + NSA_OUT
IN_SPLIT_SIZES = (MLA_Q_RANK, MLA_KV_RANK, MLA_ROPE, NSA_HEADS * NSA_HEAD_DIM,
                  2 * N_BRANCH * NSA_KV_HEADS * NSA_HEAD_DIM, N_BRANCH * NSA_HEADS)
D_IN = sum(IN_SPLIT_SIZES)

kernel_name = "hymba_mla_nsa_hybrid_block"

def rms_norm(x, g):
    xf = x.astype(jnp.float32)
    y = xf * lax.rsqrt(jnp.mean(xf * xf, axis=-1, keepdims=True) + EPS)
    return (y * g.astype(jnp.float32)).astype(x.dtype)

def rope(x, pos):
    half = x.shape[-1] // 2
    inv = 1.0 / (ROPE_THETA ** (jnp.arange(half, dtype=jnp.float32) / half))
    ang = pos.astype(jnp.float32)[:, None] * inv[None, :]
    cos = jnp.cos(ang)[None, :, None, :]
    sin = jnp.sin(ang)[None, :, None, :]
    xf = x.astype(jnp.float32)
    x1, x2 = xf[..., :half], xf[..., half:]
    return jnp.concatenate([x1 * cos - x2 * sin, x2 * cos + x1 * sin], axis=-1).astype(x.dtype)

def t5_bucket(dist):
    n = jnp.maximum(dist, 0)
    max_exact = REL_BUCKETS // 2
    large = max_exact + (jnp.log(jnp.maximum(n, 1).astype(jnp.float32) / max_exact)
                         / math.log(REL_MAX_DIST / max_exact)
                         * (REL_BUCKETS - max_exact)).astype(jnp.int32)
    large = jnp.minimum(large, REL_BUCKETS - 1)
    return jnp.where(n < max_exact, n, large)

def masked_softmax(s, mask):
    s = jnp.where(mask, s.astype(jnp.float32), -jnp.inf)
    m = jnp.max(s, axis=-1, keepdims=True)
    m = jnp.where(jnp.isfinite(m), m, 0.0)
    p = jnp.exp(s - m)
    return p / jnp.maximum(jnp.sum(p, axis=-1, keepdims=True), 1e-30)

def mla_mixer(h_q, h_kv, h_kr, cq_g, ckv_g, w_uq, w_ukv, q_gain, k_gain):
    B, S, _ = h_q.shape
    pos = jnp.arange(S)
    q = (rms_norm(h_q, cq_g) @ w_uq).reshape(B, S, MLA_HEADS, MLA_QK)
    kv = (rms_norm(h_kv, ckv_g) @ w_ukv).reshape(B, S, MLA_HEADS, MLA_NOPE + MLA_V)
    k_nope, v = kv[..., :MLA_NOPE], kv[..., MLA_NOPE:]
    k_r = jnp.broadcast_to(h_kr[:, :, None, :], (B, S, MLA_HEADS, MLA_ROPE))
    k = jnp.concatenate([k_nope, k_r], axis=-1)
    q = rms_norm(q, q_gain)
    k = rms_norm(k, k_gain)
    q = jnp.concatenate([q[..., :MLA_NOPE], rope(q[..., MLA_NOPE:], pos)], axis=-1)
    k = jnp.concatenate([k[..., :MLA_NOPE], rope(k[..., MLA_NOPE:], pos)], axis=-1)
    scale = MLA_QK ** -0.5
    nb = S // Q_BLOCK
    qb = q.reshape(B, nb, Q_BLOCK, MLA_HEADS, MLA_QK).transpose(1, 0, 2, 3, 4)

    def block(args):
        qi, i = args
        s = jnp.einsum('bqhd,bkhd->bhqk', qi, k).astype(jnp.float32) * scale
        qpos = i * Q_BLOCK + jnp.arange(Q_BLOCK)
        p = masked_softmax(s, pos[None, :] <= qpos[:, None])
        return jnp.einsum('bhqk,bkhd->bqhd', p.astype(v.dtype), v)

    o = lax.map(block, (qb, jnp.arange(nb)))
    return o.transpose(1, 0, 2, 3, 4).reshape(B, S, MLA_OUT)

def nsa_mixer(q_in, kv_in, gate_logits, q_gain, k_gain, cmp_pe, cmp_w1, cmp_w2, rel_bias):
    B, S, _ = q_in.shape
    H, G, R, Dh = NSA_HEADS, NSA_KV_HEADS, NSA_GROUP, NSA_HEAD_DIM
    pos = jnp.arange(S)
    scale = Dh ** -0.5
    qg = rms_norm(q_in.reshape(B, S, H, Dh), q_gain).reshape(B, S, G, R, Dh)
    kv = kv_in.reshape(B, S, N_BRANCH, 2, G, Dh)

    n_chunk = S // CMP_STRIDE
    n_cmp = n_chunk - 1

    def compress(t, pe, w1, w2):
        c = t.reshape(B, n_chunk, CMP_STRIDE, G, Dh)
        blocks = jnp.concatenate([c[:, :-1], c[:, 1:]], axis=2)
        blocks = blocks + pe[None, None, :, None, :]
        flat = blocks.transpose(0, 1, 3, 2, 4).reshape(B, n_cmp, G, CMP_BLOCK * Dh)
        return jax.nn.silu(flat @ w1) @ w2

    k_cmp = rms_norm(compress(kv[:, :, 0, 0], cmp_pe[0], cmp_w1[0], cmp_w2[0]), k_gain[0])
    v_cmp = compress(kv[:, :, 0, 1], cmp_pe[1], cmp_w1[1], cmp_w2[1])
    cmp_start = jnp.arange(n_cmp) * CMP_STRIDE
    dist_c = pos[:, None] - (cmp_start + CMP_BLOCK - 1)[None, :]
    bias_c = rel_bias[t5_bucket(dist_c)].reshape(S, n_cmp, G, R).transpose(2, 3, 0, 1)
    s_c = jnp.einsum('bsgrd,bcgd->bgrsc', qg, k_cmp).astype(jnp.float32) * scale + bias_c
    p_c = masked_softmax(s_c, dist_c >= 0)
    o_cmp = jnp.einsum('bgrsc,bcgd->bsgrd', p_c.astype(v_cmp.dtype), v_cmp)

    n_sel = S // SEL_BLOCK
    sel_start = jnp.arange(n_sel) * SEL_BLOCK
    overlap = jnp.clip(jnp.minimum(cmp_start[:, None] + CMP_BLOCK, sel_start[None, :] + SEL_BLOCK)
                       - jnp.maximum(cmp_start[:, None], sel_start[None, :]), 0, None)
    overlap = overlap.astype(jnp.float32) / CMP_BLOCK
    imp = jnp.einsum('bgrsc,cj->bgsj', p_c, overlap)
    blk_t = pos // SEL_BLOCK
    j = jnp.arange(n_sel)[None, :]
    valid = j <= blk_t[:, None]
    forced = valid & ((j == 0) | (j == blk_t[:, None]) | (j == blk_t[:, None] - 1))
    score = jnp.where(forced, FORCE_SCORE, jnp.where(valid, imp, -jnp.inf))
    n_top = min(SEL_TOP_N, n_sel)
    _, sel_idx = lax.top_k(score, n_top)

    k_sel = rms_norm(kv[:, :, 1, 0], k_gain[1])
    v_sel = kv[:, :, 1, 1]
    ksb = k_sel.reshape(B, n_sel, SEL_BLOCK, G, Dh).transpose(0, 3, 1, 2, 4)
    vsb = v_sel.reshape(B, n_sel, SEL_BLOCK, G, Dh).transpose(0, 3, 1, 2, 4)
    table_g = rel_bias.reshape(REL_BUCKETS, G, R).transpose(1, 0, 2)
    n_qc = S // SEL_Q_BLOCK
    q_c = qg.reshape(B, n_qc, SEL_Q_BLOCK, G, R, Dh).transpose(1, 0, 2, 3, 4, 5)
    idx_c = sel_idx.reshape(B, G, n_qc, SEL_Q_BLOCK, n_top).transpose(2, 0, 1, 3, 4)
    pos_c = pos.reshape(n_qc, SEL_Q_BLOCK)
    bi = jnp.arange(B)[:, None, None, None]
    gi = jnp.arange(G)[None, :, None, None]
    m_sel = n_top * SEL_BLOCK

    def sel_block(args):
        qi, idx, qpos = args
        kb = ksb[bi, gi, idx]
        vb = vsb[bi, gi, idx].reshape(B, G, SEL_Q_BLOCK, m_sel, Dh)
        key_pos = idx[..., None] * SEL_BLOCK + jnp.arange(SEL_BLOCK)
        dist = qpos[None, None, :, None, None] - key_pos
        bias = table_g[gi[..., None], t5_bucket(dist)]
        s = jnp.einsum('bqgrd,bgqnkd->bgrqnk', qi, kb).astype(jnp.float32) * scale \
            + jnp.moveaxis(bias, -1, 2)
        s = s.reshape(B, G, R, SEL_Q_BLOCK, m_sel)
        mask = (dist >= 0).reshape(B, G, 1, SEL_Q_BLOCK, m_sel)
        p = masked_softmax(s, mask)
        return jnp.einsum('bgrqm,bgqmd->bqgrd', p.astype(vb.dtype), vb)

    o_sel = lax.map(sel_block, (q_c, idx_c, pos_c))
    o_sel = o_sel.transpose(1, 0, 2, 3, 4, 5).reshape(B, S, G, R, Dh)

    k_win = rms_norm(kv[:, :, 2, 0], k_gain[2])
    v_win = kv[:, :, 2, 1]
    kp = jnp.pad(k_win, ((0, 0), (WINDOW, 0), (0, 0), (0, 0)))
    vp = jnp.pad(v_win, ((0, 0), (WINDOW, 0), (0, 0), (0, 0)))
    span = Q_BLOCK + WINDOW
    n_wb = S // Q_BLOCK
    off = WINDOW + jnp.arange(Q_BLOCK)[:, None] - jnp.arange(span)[None, :]
    band = (off >= 0) & (off < WINDOW)
    bias_w = rel_bias[t5_bucket(off)].reshape(Q_BLOCK, span, G, R).transpose(2, 3, 0, 1)
    q_w = qg.reshape(B, n_wb, Q_BLOCK, G, R, Dh).transpose(1, 0, 2, 3, 4, 5)

    def win_block(args):
        qi, i = args
        start = i * Q_BLOCK
        kb = lax.dynamic_slice_in_dim(kp, start, span, axis=1)
        vb = lax.dynamic_slice_in_dim(vp, start, span, axis=1)
        key_pos = start - WINDOW + jnp.arange(span)
        mask = band & (key_pos >= 0)[None, :]
        s = jnp.einsum('bqgrd,bkgd->bgrqk', qi, kb).astype(jnp.float32) * scale + bias_w
        p = masked_softmax(s, mask)
        return jnp.einsum('bgrqk,bkgd->bqgrd', p.astype(vb.dtype), vb)

    o_win = lax.map(win_block, (q_w, jnp.arange(n_wb)))
    o_win = o_win.transpose(1, 0, 2, 3, 4, 5).reshape(B, S, G, R, Dh)

    g = jax.nn.sigmoid(gate_logits.astype(jnp.float32)).reshape(B, S, N_BRANCH, G, R, 1)
    o = g[:, :, 0] * o_cmp + g[:, :, 1] * o_sel + g[:, :, 2] * o_win
    return o.astype(q_in.dtype).reshape(B, S, NSA_OUT)

def setup_inputs(seed: int = 0) -> dict:
    key = jax.random.key(seed)
    ks = jax.random.split(key, 21)
    L = DEPTH

    def nrm(k, shape, scale):
        return jax.random.normal(k, shape, jnp.float32) * scale

    def gain(k, shape):
        return 1.0 + 0.01 * jax.random.normal(k, shape, jnp.float32)

    return {
        "x": nrm(ks[0], (BATCH, SEQ, D_MODEL), 1.0),
        "ln1_g": gain(ks[1], (L, D_MODEL)),
        "w_in": nrm(ks[2], (L, D_MODEL, D_IN), D_MODEL ** -0.5),
        "mla_cq_norm_g": gain(ks[3], (L, MLA_Q_RANK)),
        "mla_ckv_norm_g": gain(ks[4], (L, MLA_KV_RANK)),
        "mla_w_uq": nrm(ks[5], (L, MLA_Q_RANK, MLA_HEADS * MLA_QK), MLA_Q_RANK ** -0.5),
        "mla_w_ukv": nrm(ks[6], (L, MLA_KV_RANK, MLA_HEADS * (MLA_NOPE + MLA_V)), MLA_KV_RANK ** -0.5),
        "mla_q_gain": gain(ks[7], (L, MLA_QK)),
        "mla_k_gain": gain(ks[8], (L, MLA_QK)),
        "nsa_q_gain": gain(ks[9], (L, NSA_HEAD_DIM)),
        "nsa_k_gain": gain(ks[10], (L, N_BRANCH, NSA_HEAD_DIM)),
        "nsa_cmp_pe": nrm(ks[11], (L, 2, CMP_BLOCK, NSA_HEAD_DIM), 0.1),
        "nsa_cmp_w1": nrm(ks[12], (L, 2, CMP_BLOCK * NSA_HEAD_DIM, CMP_HIDDEN), (CMP_BLOCK * NSA_HEAD_DIM) ** -0.5),
        "nsa_cmp_w2": nrm(ks[13], (L, 2, CMP_HIDDEN, NSA_HEAD_DIM), CMP_HIDDEN ** -0.5),
        "rel_bias": nrm(ks[14], (REL_BUCKETS, NSA_HEADS), 0.5),
        "grp_norm_mla": gain(ks[15], (L, MLA_OUT)),
        "grp_norm_nsa": gain(ks[16], (L, NSA_OUT)),
        "w_o": nrm(ks[17], (L, MIX_WIDTH, D_MODEL), MIX_WIDTH ** -0.5),
        "ln2_g": gain(ks[18], (L, D_MODEL)),
        "w_up": nrm(ks[19], (L, D_MODEL, D_FF), D_MODEL ** -0.5),
        "w_down": nrm(ks[20], (L, D_FF, D_MODEL), D_FF ** -0.5),
    }

def reference(x, ln1_g, w_in, mla_cq_norm_g, mla_ckv_norm_g, mla_w_uq, mla_w_ukv, mla_q_gain,
              mla_k_gain, nsa_q_gain, nsa_k_gain, nsa_cmp_pe, nsa_cmp_w1, nsa_cmp_w2, rel_bias,
              grp_norm_mla, grp_norm_nsa, w_o, ln2_g, w_up, w_down):
    offsets = []
    acc = 0
    for size in IN_SPLIT_SIZES[:-1]:
        acc += size
        offsets.append(acc)
    for l in range(DEPTH):
        h = rms_norm(x, ln1_g[l])
        proj = h @ w_in[l]
        h_q, h_kv, h_kr, q_b, kv_b, gate_b = jnp.split(proj, offsets, axis=-1)
        o_a = mla_mixer(h_q, h_kv, h_kr, mla_cq_norm_g[l], mla_ckv_norm_g[l], mla_w_uq[l],
                        mla_w_ukv[l], mla_q_gain[l], mla_k_gain[l])
        o_b = nsa_mixer(q_b, kv_b, gate_b, nsa_q_gain[l], nsa_k_gain[l], nsa_cmp_pe[l],
                        nsa_cmp_w1[l], nsa_cmp_w2[l], rel_bias)
        mix = jnp.concatenate([rms_norm(o_a, grp_norm_mla[l]), rms_norm(o_b, grp_norm_nsa[l])], axis=-1)
        x = x + mix @ w_o[l]
        h2 = rms_norm(x, ln2_g[l])
        x = x + jnp.square(jax.nn.relu(h2 @ w_up[l])) @ w_down[l]
    return x


_drawn_inputs = setup_inputs


def setup_inputs(seed=0):
    import zlib

    import numpy as np

    out = dict(_drawn_inputs(seed))
    spreads = {}
    factors = {'ln1_g': 4.749,
     'mla_cq_norm_g': 8.0,
     'mla_ckv_norm_g': 7.623,
     'mla_q_gain': 8.0,
     'mla_k_gain': 8.0,
     'nsa_q_gain': 8.0,
     'nsa_k_gain': 8.0,
     'grp_norm_mla': 8.0,
     'grp_norm_nsa': 8.0,
     'ln2_g': 7.643}
    for name, (base, spread) in spreads.items():
        noise = np.random.default_rng([zlib.crc32(name.encode()), seed]).standard_normal(out[name].shape)
        drawn = base * np.exp(spread * noise) if base else spread * noise
        out[name] = __import__('jax').numpy.asarray(drawn.astype(out[name].dtype))
    for name, factor in factors.items():
        out[name] = (out[name] * factor).astype(out[name].dtype)
    return out
```

```python
from contextlib import ExitStack

import concourse.bass as bass
import numpy as np
from concourse import mybir

F32 = mybir.dt.float32
F32R = mybir.dt.float32r
ALU = mybir.AluOpType
ACT = mybir.ActivationFunctionType
AX = mybir.AxisListType

P = 128
D_MODEL, SEQ, D_FF = 1024, 512, 4096
NT = SEQ // P
KD = D_MODEL // P
HEADS = 8
NOPE, ROPE, QK, VD = 64, 32, 96, 64
Q_RANK, KV_RANK = 384, 256
HD = 64
CMP_BLOCK, CMP_STRIDE, CMP_HIDDEN = 32, 16, 128
N_CMP = SEQ // CMP_STRIDE - 1
NC = 32
BUCKETS, MAX_DIST = 32, 128
EPS = 1e-6
MASKED = 1e30
LEAST = 1e29

_KV = Q_RANK + KV_RANK + ROPE + HEADS * HD
IN_BLOCKS = {
    "cq": [(0, Q_RANK)],
    "ckv": [(Q_RANK, KV_RANK + ROPE)],
    "nq": [(Q_RANK + KV_RANK + ROPE, HEADS * HD)],
    "nkv": [(_KV + 256, 512)],
    "cmp": [(_KV, 256), (_KV + 768, 24)],
}
BLOCK_COLS = {b: sum(n for _, n in cols) for b, cols in IN_BLOCKS.items()}
UP_HALF = D_FF // P // 2


def weight_pieces():
    out = []

    def add(what, count, width, split=True):
        out.extend((what, i, width, split) for i in range(count))

    add("cq", 4, 2 * BLOCK_COLS["cq"])
    add("ckv", 4, 2 * BLOCK_COLS["ckv"])
    add("uq", Q_RANK // P, HEADS * QK)
    add("ukv", KV_RANK // P, HEADS * (NOPE + VD))
    add("nq", 4, 2 * BLOCK_COLS["nq"])
    add("nkv", 4, 2 * BLOCK_COLS["nkv"])
    add("cmp", 4, 2 * BLOCK_COLS["cmp"])
    add("w1", 4, 1024, False)
    add("wo", 8, 1024)
    for half in range(2):
        add(("up", half), UP_HALF, 1024)
        for c in range(2):
            add(("down", half, c), UP_HALF // 2, 1024)
    return out


PIECES = weight_pieces()
PIECE_AT = {(what, i): n for n, (what, i, _, _) in enumerate(PIECES)}
SPLIT_AT = {n: m for m, n in enumerate(n for n, p in enumerate(PIECES) if p[3])}
SPLITS = list(SPLIT_AT)
RAW, RING = 3, 5

NEAR = 640
FAR = SEQ + SEQ - CMP_STRIDE
FAR_LEAST = CMP_STRIDE * (NC - 1) + CMP_BLOCK - 1
VEC = NEAR + FAR


class Signal:

    def __init__(self, nc, ctx, name, known, step=1):
        self.sem = ctx.enter_context(nc.semaphore(name))
        self.name, self.known, self.step, self.count = name, known, step, 0

    def mark(self, key=0):
        self.count += self.step
        self.known[self.name, key] = self.count
        return self.sem, self.step

    def at(self, key=0):
        return self.sem, self.known.get((self.name, key), self.step)


UNITS = [("mla", t, h) for t in range(NT) for h in range(HEADS)]
N_MLA = len(UNITS)
for _t in range(NT):
    UNITS += [("sel", _t, h) for h in range(HEADS)]
    UNITS += [("win", _t, h) for h in range(HEADS)]
    UNITS += [("cmp", _t, 0)]
OUTS = [("mla", t) for t in range(NT)] + [(b, t) for t in range(NT) for b in ("sel", "win", "cmp")]

DENSE = [("cq", t) for t in range(NT)] + [("ckv", t) for t in range(NT)]
DENSE += [("uq", t, c) for t in range(NT) for c in range(2)]
DENSE += [("ukv", t, c) for t in range(NT) for c in range(2)]
DENSE += [("nq", t) for t in range(NT)] + [("nkv", t) for t in range(NT)] + [("cmp", t) for t in range(NT)]
DENSE += [("wo", c, t) for c in range(2) for t in range(NT)]
for _h in range(2):
    DENSE += [("up", _h, f) for f in range(UP_HALF)]
    DENSE += [("down", _h, c, i) for c in range(2) for i in range(UP_HALF // 2)]


def last_user(piece):
    what, i, _, _ = PIECES[piece]
    if what in ("uq", "ukv"):
        return (what, NT - 1, 1)
    if what == "wo":
        return ("wo", i // 4, NT - 1)
    if what[0] == "up":
        return (*what, i)
    if what[0] == "down":
        return (*what, i)
    return (what, NT - 1)


SPLIT_AFTER, SPLIT_AT_UNIT = {}, {}
_early = (("cq", NT - 1), ("ckv", NT - 1), ("uq", NT - 1, 1), ("ukv", NT - 1, 1), ("wo", 0, NT - 1))
for _m, _n in enumerate(SPLITS[RING:]):
    _g = last_user(SPLITS[_m])
    _what = PIECES[_n][0]
    if _what == "wo" and PIECES[_n][1] < RING:
        SPLIT_AT_UNIT.setdefault(N_MLA + 5 + 3 * PIECES[_n][1], []).append(_n)
    elif _g in (("nq", NT - 1), ("nkv", NT - 1)):
        SPLIT_AT_UNIT.setdefault(4 * (3 if _g[0] == "nq" else 7) + 1 + PIECES[SPLITS[_m]][1], []).append(_n)
    elif _g in _early:
        SPLIT_AFTER.setdefault(DENSE[DENSE.index(_g) - 1], []).append(_n)
    else:
        SPLIT_AFTER.setdefault(_g, []).append(_n)


def out_of(n):
    return OUTS.index(UNITS[n][0:2])


CONST_AT, _at = {}, 0
for _name, _n in (("ident", P), ("mask", SEQ), ("rope", NT * 64), ("g_q", QK), ("g_k", QK), ("g_nq", HD), ("g_nk", 3 * HD),
                  ("pe", 2 * CMP_BLOCK // 2), ("w2", 2 * HD), ("rel", HEADS)):
    if _name == "rel":
        CONST_LOADED = _at
    CONST_AT[_name] = (_at, _n)
    _at += _n
CONST_COLS = _at


def build(nc, a, out, known):
    with ExitStack() as ctx:
        base = (nc.sbuf_base + 63) // 64 * 64
        top = [base]

        def place(name, cols, dt=F32, at=None, parts=P):
            off = top[0] if at is None else at
            if at is None:
                top[0] += cols * 4
            assert off + cols * 4 <= nc.sbuf_usable_end, (name, off)
            return nc.alloc_sbuf_tensor_at(name, [parts, cols], dt, offset=off)[:, :]

        def psum(name):
            return ctx.enter_context(nc.psum_tensor(name, [P, 512], F32))[:, :]

        def signal(name, step=1):
            return Signal(nc, ctx, name, known, step)

        x = place("x", NT * D_MODEL).rearrange("p (t d) -> p t d", t=NT)
        raw = place("raw", RAW * 1024).rearrange("p (s n) -> p s n", s=RAW)
        w_hi = place("w_hi", RING * 1024, F32R).rearrange("p (s n) -> p s n", s=RING)
        w_lo = place("w_lo", RING * 1024, F32R).rearrange("p (s n) -> p s n", s=RING)
        act_hi = place("act_hi", KD * SEQ, F32R).rearrange("p (k s) -> p k s", k=KD)
        act_lo = place("act_lo", KD * SEQ, F32R).rearrange("p (k s) -> p k s", k=KD)
        r_mla = top[0]
        m_q = place("m_q", NT * HEADS * P).rearrange("p (t h s) -> p t h s", t=NT, h=HEADS)
        m_k = place("m_k", HEADS * SEQ).rearrange("p (h s) -> p h s", h=HEADS)
        m_v = place("m_v", NT * HEADS * VD).rearrange("p (t n) -> p t n", t=NT)
        n_q = place("n_q", 4 * SEQ).rearrange("p (r s) -> p r s", r=4)
        n_k = place("n_k", 2 * SEQ).rearrange("p (b s) -> p b s", b=2)
        n_v = place("n_v", NT * 2 * P).rearrange("p (t b n) -> p t b n", t=NT, b=2)
        r_bias = top[0]
        bias = place("bias", HEADS * SEQ).rearrange("p (h s) -> p h s", h=HEADS)
        bias_c = place("bias_c", NT * 2 * P).rearrange("p (t g n) -> p t g n", t=NT, g=2)
        r_work = top[0]
        s_buf = place("s_buf", 2 * 512).rearrange("p (b n) -> p b n", b=2)
        p_buf = place("p_buf", 2 * 512).rearrange("p (b n) -> p b n", b=2)
        pt_buf = place("pt_buf", 2 * 512).rearrange("p (b n) -> p b n", b=2)
        r_temp = top[0]
        raw_row = place("raw_row", 2 * 512).rearrange("p (b n) -> p b n", b=2)
        square = place("square", 512)
        r_onsa = top[0]
        o_nsa = place("o_nsa", 2 * 512).rearrange("p (b n) -> p b n", b=2)
        consts = place("consts", CONST_COLS)
        kr = place("kr", NT * ROPE).rearrange("p (t n) -> p t n", t=NT)
        gates = place("gates", NT * 24).rearrange("p (t n) -> p t n", t=NT)
        stats = place("stats", 384)
        tab_q = place("tab_q", NT * 128, at=r_onsa).rearrange("p (t n) -> p t n", t=NT)
        tab_k = place("tab_k", NT * 128, at=r_onsa + 2048).rearrange("p (t n) -> p t n", t=NT)
        o_mla = place("o_mla", NT * 512, at=r_mla).rearrange("p (t n) -> p t n", t=NT)
        gain_ln1 = place("gain_ln1", D_MODEL, at=r_mla)
        c_row = place("c_row", NT * (Q_RANK + KV_RANK), at=r_mla + 4096).rearrange("p (t n) -> p t n", t=NT)
        r_mk = r_mla + NT * HEADS * P * 4
        gain_c = place("gain_c", Q_RANK + KV_RANK, at=r_mk)
        onehot = place("onehot", VEC, at=r_mk + 2560, parts=33)
        bias_vec = place("bias_vec", VEC, at=r_mk + 2560 + VEC * 4, parts=8)
        c_hi = place("c_hi", 5 * SEQ, F32R, at=r_bias).rearrange("p (k s) -> p k s", k=5)
        c_lo = place("c_lo", 5 * SEQ, F32R, at=r_bias + 5 * SEQ * 4).rearrange("p (k s) -> p k s", k=5)
        ln_row = place("ln_row", 2 * D_MODEL, at=r_work).rearrange("p (b n) -> p b n", b=2)
        ln_sq = place("ln_sq", D_MODEL, at=r_work + 8192)
        qk_row = place("qk_row", 2 * HEADS * QK, at=r_work).rearrange("p (b n) -> p b n", b=2)
        qk_out = place("qk_out", HEADS * QK, at=r_work + 6144)
        qk_sq = place("qk_sq", HEADS * QK, at=r_work + 9216)
        rope_t = place("rope_t", HEADS * ROPE, at=r_temp)
        taps = place("taps", 4 * SEQ, at=r_mk).rearrange("p (j s) -> p j s", j=4)
        bias_ct = place("bias_ct", 2 * SEQ, at=r_mk + 8192).rearrange("p (g s) -> p g s", g=2)
        v_diag = place("v_diag", 2 * 256, at=r_mk + 12288).rearrange("p (g n) -> p g n", g=2)
        hid_v = place("hid_v", 2 * P, at=r_mk + 14336).rearrange("p (g h c) -> p g h c", g=2, h=4)
        k_cmp = place("k_cmp", NC, at=r_mk + 15360)
        hid_k = place("hid_k", 2 * NC, at=r_mk + 15488)
        kc_row = place("kc_row", HD, at=r_mk + 15744, parts=64)
        kc_sq = place("kc_sq", HD, at=r_mk + 16000, parts=64)
        r_mv = r_mk + 16384
        gain_grp = place("gain_grp", D_MODEL, at=r_mv)
        gain_ln2 = place("gain_ln2", D_MODEL, at=r_mv + 4096)
        mix_row = place("mix_row", 2 * 512, at=r_mla + 8192).rearrange("p (b n) -> p b n", b=2)
        gate_t = place("gate_t", SEQ, at=r_mla + 13824, parts=24)
        z_buf = place("z_buf", 3 * 2 * 2 * N_CMP, at=r_mla + 12288).rearrange("p (a b n) -> p a b n", a=3, b=2)
        a_hi = place("a_hi", UP_HALF * SEQ, F32R, at=r_mla).rearrange("p (f s) -> p f s", f=UP_HALF)
        a_lo = place("a_lo", UP_HALF * SEQ, F32R, at=r_mla + UP_HALF * SEQ * 4).rearrange("p (f s) -> p f s", f=UP_HALF)
        relu_b = place("relu_b", 2 * 512, at=r_work).rearrange("p (b n) -> p b n", b=2)
        sq_b = place("sq_b", 2 * 512, at=r_work + 4096).rearrange("p (b n) -> p b n", b=2)

        def const(name, parts=P):
            at, n = CONST_AT[name]
            return consts[0:parts, at:at + n]

        ident = const("ident")
        rope = const("rope").rearrange("p (t n) -> p t n", t=NT)
        stat_at = [0]

        def stat(n):
            stat_at[0] += n
            assert stat_at[0] <= 384
            return stats[:, stat_at[0] - n:stat_at[0]]

        ss_ln, rs_ln = stat(NT), stat(NT)
        ss_c, rs_c, ss_kr = stat(2 * NT), stat(2 * NT), stat(NT)
        ss_row, rs_row = stat(16), stat(16)
        neg_max = stat(8 * 2)
        den, rden = stat(8 * 3), stat(8 * 3)
        half_neg = stat(8)
        ss_mix, rs_mix = stat(2 * NT), stat(2 * NT)
        pe_col, kc_ss, kc_rs = stat(2), stat(1), stat(1)

        banks = [psum(f"bank{i}") for i in range(8)]
        D, T, S, O = banks[0:2], banks[2:4], banks[4:6], banks[6:8]
        TD = T + D

        x_in = [signal(f"x_in{t}", 16) for t in range(NT)]
        raw_in = [signal(f"raw_in{s}", 16) for s in range(RAW)]
        consts_in, gain1_in, gainc_in = signal("consts_in", 16), signal("gain1_in", 16), signal("gainc_in", 16)
        onehot_in, vec_out = signal("onehot_in", 16), signal("vec_out", 16)
        bias_in, biasc_in = signal("bias_in", 16), signal("biasc_in", 16)
        gaing_in, gain2_in, y_out = signal("gaing_in", 16), signal("gain2_in", 16), signal("y_out", 16)
        hi_done, lo_done = signal("hi_done"), signal("lo_done")
        piece_used, taps_used = signal("piece_used"), signal("taps_used")
        dense_done, turned = signal("dense_done"), signal("turned")
        scores, half_scored, mixed = signal("scores"), signal("half_scored"), signal("mixed")
        squares, copied, turn_hi = signal("squares"), signal("copied"), signal("turn_hi")
        probs, relu_done, a_hi_done = signal("probs"), signal("relu_done"), signal("a_hi_done")
        act_pt, exp_small = signal("act_pt"), signal("exp_small")
        summed, scaled, turn_lo = signal("summed"), signal("scaled"), signal("turn_lo")
        lows, dve_pt, o_used = signal("lows"), signal("dve_pt"), signal("o_used")
        dve_step, x2_done, sq_done, a_lo_done = signal("dve_step"), signal("x2_done"), signal("sq_done"), signal("a_lo_done")
        y_done = signal("y_done")
        rsqrt_done, pool_step, roped = signal("rsqrt_done"), signal("pool_step"), signal("roped")

        vec_dram = nc.dram_tensor("bias_by_distance", [HEADS, VEC], F32, kind="Internal").ap()

        def bank_of(kind, key):
            return known.get(("bank", kind, key), 0)

        def raw_free(n):
            what, i, _, split = PIECES[n]
            if split:
                return lo_done.at(n)
            return turned.at(("hid", i // 2)) if i % 2 else taps_used.at(n)

        def used_by(n):
            what, i, _, _ = PIECES[n]
            last = {"uq": Q_RANK // P, "ukv": KV_RANK // P}.get(what, 4)
            if what[0] == "up":
                return dense_done.at((*what, i))
            if what[0] == "down":
                return mixed.at((*what, NT - 1)) if i == UP_HALF // 2 - 1 else piece_used.at(n)
            if i % last < last - 1:
                return piece_used.at(n)
            return dense_done.at(last_user(n))

        def up_bank(half, f):
            return ((S + O) if half == 0 else (D + T))[f % 4]

        def down_banks(half, c):
            return (D + T) if (half + c) % 2 == 0 else (S + O)

        def backwards(tiles):
            return tiles[:, :, ::-1]

        nsa_rows = [(b, t) for b in ("nq", "nkv") for t in range(NT)]

        block = ctx.enter_context(nc.Block())

        @block.sync
        def _(sp):
            for t in range(NT):
                sp.dma_start(x[:, t, :], a["x"][t * P:(t + 1) * P, :]).then_inc(*x_in[t].mark())
            for n, (what, i, width, split) in enumerate(PIECES):
                if n >= RAW:
                    sp.wait_ge(*raw_free(n - RAW))
                sp.dma_start(raw[:, n % RAW, 0:width], a["weights"][n, :, 0:width]).then_inc(*raw_in[n % RAW].mark(n))
            for t in range(NT):
                for c in range(2):
                    sp.wait_ge(*y_done.at((t, c)))
                    sp.dma_start(out[t * P:(t + 1) * P, c * 512:(c + 1) * 512],
                                 x[:, t, c * 512:(c + 1) * 512]).then_inc(*y_out.mark((t, c)))
            sp.wait_ge(*y_out.at((NT - 1, 1)))

        @block.gpsimd
        def _(pool):
            pool.memset(half_neg, -0.5).then_inc(*pool_step.mark("half"))
            pool.memset(consts[0:33, CONST_AT["rel"][0]:CONST_AT["rel"][0] + 8], MASKED).then_inc(*pool_step.mark("rel0"))
            pool.wait_ge(*pool_step.at("rel0"))
            pool.dma_start(const("rel", 32), a["rel_bias"]).then_inc(*onehot_in.mark("rel"))
            pool.dma_start(onehot, a["onehot"]).then_inc(*onehot_in.mark("table"))
            pool.wait_ge(*consts_in.at())
            pool.tensor_scalar(const("g_q"), const("g_q"), -float(QK) ** -0.5, 1.0, ALU.mult, ALU.mult).then_inc(*pool_step.mark("gq"))
            pool.tensor_scalar(const("g_nq"), const("g_nq"), -float(HD) ** -0.5, 1.0, ALU.mult, ALU.mult).then_inc(*pool_step.mark("gnq"))
            pool.wait_ge(*pool_step.at("gq"))
            for name, tab in (("g_q", tab_q), ("g_k", tab_k)):
                g = const(name)
                for n, lo, hi in ((0, 0, NOPE), (NOPE, NOPE, QK), (QK, NOPE + 16, QK), (QK + 16, NOPE, NOPE + 16)):
                    w = hi - lo
                    gain = g[:, lo:hi].unsqueeze(1).to_broadcast([P, NT, w])
                    if n == 0:
                        ins = pool.tensor_scalar(tab[:, :, 0:w], gain, 1.0, 1.0, ALU.mult, ALU.mult)
                    else:
                        ins = pool.tensor_tensor(tab[:, :, n:n + w], gain, rope[:, :, n - NOPE:n - NOPE + w], ALU.mult)
                ins.then_inc(*pool_step.mark(name))

            def rsqrt(key, out_, in_, width, after=None):
                pool.tensor_scalar(in_, in_, 1.0 / width, EPS, ALU.mult, ALU.add).then_inc(*pool_step.mark(("ms", key)))
                pool.wait_ge(*pool_step.at(("ms", key)))
                n = in_.shape[1]
                pool.tensor_tensor(out_, in_, half_neg[0:in_.shape[0], 0:n], ALU.pow).then_inc(*rsqrt_done.mark(key))

            pool.wait_ge(*pool_step.at("half"))
            for t in range(NT):
                pool.wait_ge(*squares.at(("ln1", t)))
                rsqrt(("ln1", t), rs_ln[:, t:t + 1], ss_ln[:, t:t + 1], D_MODEL)
            pool.wait_ge(*dve_step.at("vec3"))
            pool.dma_start(vec_dram, bias_vec).then_inc(*vec_out.mark())
            for c, (b, width) in enumerate((("cq", Q_RANK), ("ckv", KV_RANK))):
                for t in range(NT):
                    pool.wait_ge(*squares.at((b, t)))
                    rsqrt((b, t), rs_c[:, c * NT + t:c * NT + t + 1], ss_c[:, c * NT + t:c * NT + t + 1], width)

            for name, tab in (("uq", tab_q), ("ukv", tab_k)):
                for t in range(NT):
                    b = t % 2
                    ss, rs = ss_row[:, 8 * b:8 * b + 8], rs_row[:, 8 * b:8 * b + 8]
                    pool.wait_ge(*summed.at((name, t)))
                    if name == "ukv":
                        pool.tensor_scalar(ss, ss, ss_kr[:, t:t + 1], 1.0, ALU.add, ALU.mult).then_inc(*pool_step.mark(("kr", t)))
                        pool.wait_ge(*pool_step.at(("kr", t)))
                    rsqrt((name, t), rs, ss, QK)
                    row = qk_row[:, b, :].rearrange("p (h n) -> p h n", h=HEADS)
                    fin = qk_out.rearrange("p (h n) -> p h n", h=HEADS)
                    tmp = rope_t.rearrange("p (h n) -> p h n", h=HEADS)
                    pool.wait_ge(*scaled.at((name, t)))
                    for lo, src in ((0, NOPE + 16), (16, NOPE)):
                        sin = tab[:, t, QK + lo:QK + lo + 16].unsqueeze(1).to_broadcast([P, HEADS, 16])
                        ins = pool.tensor_tensor(tmp[:, :, lo:lo + 16], row[:, :, src:src + 16], sin, ALU.mult)
                    ins.then_inc(*pool_step.mark(("rot", name, t)))
                    pool.wait_ge(*pool_step.at(("rot", name, t)))
                    pool.wait_ge(*dve_step.at(("gain", name, t)))
                    pool.tensor_tensor(fin[:, :, NOPE:QK], fin[:, :, NOPE:QK], tmp, ALU.add).then_inc(*roped.mark((name, t)))

            pool.wait_ge(*vec_out.at())
            pool.wait_ge(*dense_done.at(("ukv", NT - 1, 1)))
            pool.dma_start(bias, bass.AP(vec_dram.tensor, 0, [[1, P], [VEC, HEADS], [1, SEQ]])).then_inc(*bias_in.mark())

            for b in ("nq", "nkv"):
                for t in range(NT):
                    j = t % 2
                    n = 8 if b == "nq" else 4
                    pool.wait_ge(*summed.at((b, t)))
                    rsqrt((b, t), rs_row[:, 8 * j:8 * j + n], ss_row[:, 8 * j:8 * j + n], HD)

            pool.wait_ge(*mixed.at(N_MLA - 1))
            for h in range(HEADS):
                pool.dma_start(bias_ct[32 * (h % 4):32 * (h % 4) + 32, h // 4, :],
                               bass.AP(vec_dram.tensor, h * VEC + NEAR, [[CMP_STRIDE, NC], [1, SEQ]])
                               ).then_inc(*biasc_in.mark(h))
            pool.dma_start(gain_grp, a["gain_grp"]).then_inc(*gaing_in.mark())
            pool.dma_start(gain_ln2, a["gain_ln2"]).then_inc(*gain2_in.mark())
            for t in range(NT):
                pool.wait_ge(*squares.at(("mix", 0, t)))
                rsqrt(("mix", 0, t), rs_mix[:, t:t + 1], ss_mix[:, t:t + 1], 512)
            pool.wait_ge(*dve_step.at("kc_ss"))
            rsqrt("kc", kc_rs[0:64, :], kc_ss[0:64, :], HD)
            for t in range(NT):
                pool.wait_ge(*squares.at(("mix", 1, t)))
                rsqrt(("mix", 1, t), rs_mix[:, NT + t:NT + t + 1], ss_mix[:, NT + t:NT + t + 1], 512)
            for t in range(NT):
                pool.wait_ge(*squares.at(("ln2", t)))
                rsqrt(("ln2", t), rs_ln[:, t:t + 1], ss_ln[:, t:t + 1], D_MODEL)

        @block.scalar
        def _(act):
            act.dma_start(gain_ln1, a["gain_ln1"]).then_inc(*gain1_in.mark())
            act.dma_start(consts[:, 0:CONST_LOADED], a["consts"]).then_inc(*consts_in.mark())
            act.dma_start(gain_c, a["gain_c"]).then_inc(*gainc_in.mark())

            def split_hi(n):
                m, width = SPLIT_AT[n], PIECES[n][2]
                act.wait_ge(*raw_in[n % RAW].at(n))
                if m >= RING:
                    act.wait_ge(*used_by(SPLITS[m - RING]))
                act.activation(w_hi[:, m % RING, 0:width], raw[:, n % RAW, 0:width], ACT.Copy).then_inc(*hi_done.mark(n))

            def after(group):
                for n in SPLIT_AFTER.get(group, ()):
                    split_hi(n)

            def to_hi(key, dst, cols, width):
                act.wait_ge(*turned.at(key))
                src = TD[bank_of("T", key)][:, 0:cols * width].rearrange("p (k s) -> p k s", k=cols)
                if key[0] == "mix":
                    src = backwards(src)
                act.activation(dst, src, ACT.Copy).then_inc(*turn_hi.mark(key))

            for t in range(NT):
                act.wait_ge(*x_in[t].at())
                if t:
                    act.wait_ge(*squares.at(("ln1", t - 1)))
                act.activation(ln_sq, x[:, t, :], ACT.Square, accum_out=ss_ln[:, t:t + 1]).then_inc(*squares.mark(("ln1", t)))
            for n in SPLITS[:3]:
                split_hi(n)
            for t in range(NT):
                for half in range(2):
                    to_hi(("ln1", t, half), act_hi[:, 4 * half:4 * half + 4, t * P:(t + 1) * P], 4, P)
            for n in SPLITS[3:RING]:
                split_hi(n)

            for t in range(NT):
                key = ("cq", t)
                act.wait_ge(*dense_done.at(key))
                bank = D[bank_of("D", key)]
                if t:
                    act.wait_ge(*squares.at(("cq", t - 1)))
                act.activation(square[:, 0:Q_RANK], bank[:, 0:Q_RANK], ACT.Square, accum_out=ss_c[:, t:t + 1]).then_inc(*squares.mark(key))
                act.activation(c_row[:, t, 0:Q_RANK], bank[:, 0:Q_RANK], ACT.Copy).then_inc(*copied.mark(key))
                after(key)
            for t in range(NT):
                key = ("ckv", t)
                act.wait_ge(*dense_done.at(key))
                bank = D[bank_of("D", key)]
                act.wait_ge(*squares.at(("ckv", t - 1) if t else ("cq", NT - 1)))
                act.activation(square[:, KV_RANK:KV_RANK + ROPE], bank[:, KV_RANK:KV_RANK + ROPE], ACT.Square, accum_out=ss_kr[:, t:t + 1]).then_inc(*squares.mark(("kr", t)))
                act.activation(square[:, 0:KV_RANK], bank[:, 0:KV_RANK], ACT.Square, accum_out=ss_c[:, NT + t:NT + t + 1]).then_inc(*squares.mark(key))
                act.activation(kr[:, t, :], bank[:, KV_RANK:KV_RANK + ROPE], ACT.Copy).then_inc(*copied.mark(("kr", t)))
                act.activation(c_row[:, t, Q_RANK:], bank[:, 0:KV_RANK], ACT.Copy).then_inc(*copied.mark(key))
                after(key)
                to_hi(("cq", t), c_hi[:, 0:3, t * P:(t + 1) * P], 3, P)

            def turned_out(name, t, half):
                key = (name, t, half)
                act.wait_ge(*turned.at(key))
                src = TD[bank_of("T", key)][0:QK, :].rearrange("p (h s) -> p h s", h=4)
                if name == "uq":
                    src = backwards(src)
                dst = m_q[0:QK, t, 4 * half:4 * half + 4, :] if name == "uq" else m_k[0:QK, 4 * half:4 * half + 4, t * P:(t + 1) * P]
                act.activation(dst, src, ACT.Copy).then_inc(*copied.mark(("turned", key)))

            for name, n, w in (("uq", QK, QK), ("ukv", NOPE, NOPE + VD)):
                for t in range(NT):
                    row = qk_row[:, t % 2, :].rearrange("p (h n) -> p h n", h=HEADS)
                    sq = qk_sq[:, 0:HEADS * n].rearrange("p (h n) -> p h n", h=HEADS)
                    if name == "uq":
                        to_hi(("ckv", t), c_hi[:, 3:5, t * P:(t + 1) * P], 2, P)
                    for c in range(2):
                        key = (name, t, c)
                        act.wait_ge(*dense_done.at(key))
                        src = D[bank_of("D", key)][:, 0:4 * w].rearrange("p (h n) -> p h n", h=4)
                        hs = slice(4 * c, 4 * c + 4)
                        before = (name, t - 1) if t else ("uq", NT - 1) if name == "ukv" else None
                        if before:
                            act.wait_ge(*summed.at(before))
                        act.activation(sq[:, hs, :], src[:, :, 0:n], ACT.Square).then_inc(*squares.mark(key))
                        two = (name, t - 2) if t >= 2 else ("uq", NT - 2 + t) if name == "ukv" else None
                        if two:
                            act.wait_ge(*roped.at(two))
                        if name == "ukv":
                            act.activation(m_v[:, t, 4 * c * VD:(4 * c + 4) * VD].rearrange("p (h n) -> p h n", h=4),
                                           src[:, :, NOPE:], ACT.Copy).then_inc(*copied.mark(("v", t, c)))
                        act.activation(row[:, hs, 0:n], src[:, :, 0:n], ACT.Copy).then_inc(*copied.mark(key))
                        after(key)
                    if (name, t) == ("ukv", 1):
                        act.wait_ge(*vec_out.at())
                    if (name, t) != ("uq", 0):
                        pn, pt = (name, t - 1) if t else ("uq", NT - 1)
                        for half in range(2):
                            turned_out(pn, pt, half)
            for half in range(2):
                turned_out("ukv", NT - 1, half)

            def exp_unit(n):
                kind, t, h = UNITS[n]
                nk = 2 * P if kind == "cmp" else (t + 1) * P
                act.wait_ge(*lows.at(n))
                if n >= 2:
                    act.wait_ge(*turned.at(("p", n - 2)))
                if kind == "cmp":
                    act.activation(p_buf[:, n % 2, 0:nk], s_buf[:, n % 2, 0:nk], ACT.Exp, scale=-1.0).then_inc(*probs.mark(n))
                else:
                    m, d = (h + 8 * out_of(n)) % 16, h + 8 * (out_of(n) % 3)
                    act.activation(p_buf[:, n % 2, 0:nk], s_buf[:, n % 2, 0:nk], ACT.Exp, scale=-1.0,
                                   bias=neg_max[:, m:m + 1], accum_out=den[:, d:d + 1]).then_inc(*probs.mark(n))

            def pt_out(n):
                kind, t, h = UNITS[n]
                nk = 2 * P if kind == "cmp" else (t + 1) * P
                act.wait_ge(*turned.at(("p", n)))
                if n >= 2:
                    act.wait_ge(*mixed.at(n - 2))
                act.activation(pt_buf[:, n % 2, 0:nk], TD[bank_of("T", ("p", n))][:, 0:nk], ACT.Copy).then_inc(*act_pt.mark(n))

            def row_in(key):
                b, t = key
                act.wait_ge(*dense_done.at(key))
                bank = D[bank_of("D", key)]
                j = t % 2
                before = (b, t - 1) if t else ("nq", NT - 1) if b == "nkv" else None
                if before:
                    act.wait_ge(*summed.at(before))
                two = (b, t - 2) if t >= 2 else ("nq", NT - 2 + t) if b == "nkv" else None
                if two:
                    act.wait_ge(*scaled.at(two))
                if b == "nq":
                    act.activation(square, bank, ACT.Square).then_inc(*squares.mark(key))
                    act.activation(raw_row[:, j, :], bank, ACT.Copy).then_inc(*copied.mark(key))
                else:
                    src = bank.rearrange("p (b v n) -> p b v n", b=2, v=2)
                    two_b = lambda r: r[:, 0:256].rearrange("p (b n) -> p b n", b=2)
                    act.activation(two_b(square), src[:, :, 0, :], ACT.Square).then_inc(*squares.mark(key))
                    act.activation(n_v[:, t, :, :], src[:, :, 1, :], ACT.Copy).then_inc(*copied.mark(("nv", t)))
                    act.activation(two_b(raw_row[:, j, :]), src[:, :, 0, :], ACT.Copy).then_inc(*copied.mark(key))
                after(key)

            def unit_step(n, last):
                if n - 3 >= 0 and (n - 3) % 2 == 0:
                    pt_out(n - 3)
                if n - 1 >= 0 and n - 1 < last:
                    exp_unit(n - 1)

            for n in range(N_MLA):
                unit_step(n, N_MLA)
                if n % 4 == 0 and n:
                    row_in(nsa_rows[n // 4 - 1])
                for m in SPLIT_AT_UNIT.get(n, ()):
                    split_hi(m)

            def top_taps(t):
                act.wait_ge(*turned.at(("taps", t)))
                act.activation(taps[0:HD, :, t * P:(t + 1) * P],
                               TD[bank_of("T", ("taps", t))][0:HD, :].rearrange("p (j s) -> p j s", j=4), ACT.Copy).then_inc(*copied.mark(("taps", t)))

            def mix_square(g, t):
                src = o_mla[:, t, :] if g == 0 else o_nsa[:, t % 2, :]
                i = g * NT + t - 1
                if i >= 0:
                    act.wait_ge(*squares.at(("mix", i // NT, i % NT)))
                act.activation(square, src, ACT.Square, accum_out=ss_mix[:, g * NT + t:g * NT + t + 1]).then_inc(*squares.mark(("mix", g, t)))

            for n in range(N_MLA, N_MLA + 3):
                if (n - 3) % 2 == 0:
                    pt_out(n - 3)
                if n - 1 < N_MLA:
                    exp_unit(n - 1)
                if n == N_MLA:
                    row_in(nsa_rows[-1])
            for t in range(NT):
                key = ("cmp", t)
                act.wait_ge(*dense_done.at(key))
                bank = D[bank_of("D", key)]
                if t >= 2:
                    act.wait_ge(*turned.at(("taps", t - 2)))
                src = bank[:, 0:256].rearrange("p (j n) -> p j n", j=4).unsqueeze(2).to_broadcast([P, 4, 2, HD])
                act.activation(raw_row[:, t % 2, :].rearrange("p (j d n) -> p j d n", j=4, d=2), src, ACT.Copy).then_inc(*copied.mark(("dup", t)))
                act.activation(gates[:, t, :], bank[:, 256:280], ACT.Exp, scale=-1.0).then_inc(*copied.mark(key))
                after(key)
                if t:
                    top_taps(t - 1)
            top_taps(NT - 1)
            for t in range(NT):
                act.wait_ge(*o_used.at(("mla", t)))
                mix_square(0, t)
            for kv in range(2):
                act.wait_ge(*dve_step.at(("z", kv)))
                act.activation(z_buf[:, 1, kv, :], z_buf[:, 0, kv, :], ACT.Exp, scale=-1.0).then_inc(*exp_small.mark(kv))
            for t in range(NT):
                to_hi(("mix", 0, t), act_hi[:, 0:4, t * P:(t + 1) * P], 4, P)

            last = len(UNITS)
            for n in range(N_MLA, last + 3):
                if n - 3 >= N_MLA and (n - 3) % 2 == 0:
                    pt_out(n - 3)
                if n - 1 >= N_MLA and n - 1 < last:
                    exp_unit(n - 1)
                done = n - 5
                if done >= N_MLA and (done < last) and UNITS[done][0] == "cmp" and UNITS[done][1] < NT - 1:
                    t = UNITS[done][1]
                    act.wait_ge(*o_used.at(("cmp", t)))
                    mix_square(1, t)
                done = n - 10
                if done >= N_MLA and UNITS[done][0] == "cmp":
                    t = UNITS[done][1]
                    to_hi(("mix", 1, t), act_hi[:, 4:8, t * P:(t + 1) * P], 4, P)
                for m in SPLIT_AT_UNIT.get(n, ()):
                    split_hi(m)
            act.wait_ge(*o_used.at(("cmp", NT - 1)))
            mix_square(1, NT - 1)
            to_hi(("mix", 1, NT - 1), act_hi[:, 4:8, (NT - 1) * P:], 4, P)

            for t in range(NT):
                after(("wo", 0, t))
            for t in range(NT):
                act.wait_ge(*x2_done.at((1, t)))
                if t:
                    act.wait_ge(*squares.at(("ln2", t - 1)))
                act.activation(ln_sq, x[:, t, :], ACT.Square, accum_out=ss_ln[:, t:t + 1]).then_inc(*squares.mark(("ln2", t)))
                after(("wo", 1, t))
                if t:
                    for half in range(2):
                        to_hi(("ln2", t - 1, half), act_hi[:, 4 * half:4 * half + 4, (t - 1) * P:t * P], 4, P)
            for half in range(2):
                to_hi(("ln2", NT - 1, half), act_hi[:, 4 * half:4 * half + 4, (NT - 1) * P:], 4, P)

            for half in range(2):
                for f in range(UP_HALF):
                    key = ("up", half, f)
                    act.wait_ge(*dense_done.at(key))
                    if f >= 2 or half:
                        act.wait_ge(*sq_done.at((half, f - 2) if f >= 2 else (0, UP_HALF - 2 + f)))
                    act.activation(relu_b[:, f % 2, :], up_bank(half, f), ACT.Relu).then_inc(*relu_done.mark((half, f)))
                    after(key)
                    act.wait_ge(*sq_done.at((half, f)))
                    act.activation(a_hi[:, f, :], sq_b[:, f % 2, :], ACT.Copy).then_inc(*a_hi_done.mark((half, f)))
                for c in range(2):
                    for i in range(UP_HALF // 2):
                        after(("down", half, c, i))

        @block.vector
        def _(dve):
            def split_lo(n):
                m, width = SPLIT_AT[n], PIECES[n][2]
                dve.wait_ge(*hi_done.at(n))
                dve.tensor_tensor(w_lo[:, m % RING, 0:width], raw[:, n % RAW, 0:width],
                                  w_hi[:, m % RING, 0:width].bitcast(F32), ALU.subtract).then_inc(*lo_done.mark(n))

            def after(group):
                for n in SPLIT_AFTER.get(group, ()):
                    split_lo(n)

            def to_lo(key, dst, hi, cols):
                dve.wait_ge(*turn_hi.at(key))
                src = TD[bank_of("T", key)][:, 0:cols * P].rearrange("p (k s) -> p k s", k=cols)
                if key[0] == "mix":
                    src = backwards(src)
                dve.tensor_tensor(dst, src, hi.bitcast(F32), ALU.subtract).then_inc(*turn_lo.mark(key))

            def ln_rows(t, name, gain):
                dve.wait_ge(*rsqrt_done.at((name, t)))
                if t >= 2:
                    dve.wait_ge(*turned.at((name, t - 2, 1)))
                dve.scalar_tensor_tensor(ln_row[:, t % 2, :], x[:, t, :], rs_ln[:, t:t + 1], gain, ALU.mult, ALU.mult).then_inc(*scaled.mark((name, t)))

            def ln_lows(t, name):
                for half in range(2):
                    to_lo((name, t, half), act_lo[:, 4 * half:4 * half + 4, t * P:(t + 1) * P],
                          act_hi[:, 4 * half:4 * half + 4, t * P:(t + 1) * P], 4)

            dve.wait_ge(*gain1_in.at())
            for n in SPLITS[:2]:
                split_lo(n)
            ln_rows(0, "ln1", gain_ln1)
            ln_rows(1, "ln1", gain_ln1)
            split_lo(SPLITS[2])
            for t in range(NT):
                ln_lows(t, "ln1")
                if t + 2 < NT:
                    ln_rows(t + 2, "ln1", gain_ln1)
            for n in SPLITS[3:RING]:
                split_lo(n)
            for j in range(4):
                lo, hi = 512 * j, min(512 * (j + 1), VEC)
                dve.wait_ge(*turned.at(("vec", j)))
                dve.tensor_copy(bias_vec[:, lo:hi], TD[bank_of("T", ("vec", j))][0:8, 0:hi - lo]).then_inc(*dve_step.mark(f"vec{j}"))

            def latent_row(name, t):
                lo, hi, c = (0, Q_RANK, t) if name == "cq" else (Q_RANK, Q_RANK + KV_RANK, NT + t)
                dve.wait_ge(*rsqrt_done.at((name, t)))
                dve.wait_ge(*copied.at((name, t)))
                dve.scalar_tensor_tensor(c_row[:, t, lo:hi], c_row[:, t, lo:hi], rs_c[:, c:c + 1], gain_c[:, lo:hi],
                                         ALU.mult, ALU.mult).then_inc(*scaled.mark((name, t)))

            dve.wait_ge(*gainc_in.at())
            for t in range(NT):
                after(("cq", t))
                if t:
                    latent_row("cq", t - 1)
            latent_row("cq", NT - 1)
            for t in range(NT):
                after(("ckv", t))
                to_lo(("cq", t), c_lo[:, 0:3, t * P:(t + 1) * P], c_hi[:, 0:3, t * P:(t + 1) * P], 3)
                if t:
                    latent_row("ckv", t - 1)
            latent_row("ckv", NT - 1)
            for name, n, tab in (("uq", QK, tab_q), ("ukv", NOPE, tab_k)):
                dve.wait_ge(*pool_step.at("g_q" if name == "uq" else "g_k"))
                for t in range(NT):
                    b = t % 2
                    rs = rs_row[:, 8 * b:8 * b + 8]
                    row = qk_row[:, b, :].rearrange("p (h n) -> p h n", h=HEADS)
                    fin = qk_out.rearrange("p (h n) -> p h n", h=HEADS)
                    if name == "uq":
                        to_lo(("ckv", t), c_lo[:, 3:5, t * P:(t + 1) * P], c_hi[:, 3:5, t * P:(t + 1) * P], 2)
                    after((name, t, 0))
                    dve.wait_ge(*squares.at((name, t, 1)))
                    dve.tensor_reduce(ss_row[:, 8 * b:8 * b + 8], qk_sq[:, 0:HEADS * n].rearrange("p (h n) -> p h n", h=HEADS),
                                      AX.X, ALU.add).then_inc(*summed.mark((name, t)))
                    after((name, t, 1))
                    dve.wait_ge(*rsqrt_done.at((name, t)))
                    dve.wait_ge(*copied.at((name, t, 1)))
                    if name == "ukv":
                        dve.wait_ge(*copied.at(("kr", t)))
                        dve.tensor_tensor(row[:, :, NOPE:], kr[:, t, :].unsqueeze(1).to_broadcast([P, HEADS, ROPE]),
                                          rs.unsqueeze(2).to_broadcast([P, HEADS, ROPE]), ALU.mult)
                    dve.tensor_tensor(row[:, :, 0:n], row[:, :, 0:n], rs.unsqueeze(2).to_broadcast([P, HEADS, n]),
                                      ALU.mult).then_inc(*scaled.mark((name, t)))
                    before = (name, t - 1) if t else ("uq", NT - 1) if name == "ukv" else None
                    if before:
                        dve.wait_ge(*turned.at((*before, 1)))
                    dve.wait_ge(*scaled.at((name, t)))
                    dve.tensor_tensor(fin, row, tab[:, t, 0:QK].unsqueeze(1).to_broadcast([P, HEADS, QK]),
                                      ALU.mult).then_inc(*dve_step.mark(("gain", name, t)))

            def low_unit(n):
                kind, t, h = UNITS[n]
                b, nk = n % 2, (t + 1) * P
                bank = S[n % 2]
                dve.wait_ge(*scores.at(n))
                if n >= 2:
                    dve.wait_ge(*probs.at(n - 2))
                if kind == "cmp":
                    s = s_buf[:, b, 0:256]
                    s3 = s.rearrange("p (h c) -> p h c", h=HEADS)
                    nm = neg_max[:, (8 * out_of(n)) % 16:(8 * out_of(n)) % 16 + 8]
                    dve.tensor_tensor(s.rearrange("p (g n) -> p g n", g=2), bank[:, 0:256].rearrange("p (g n) -> p g n", g=2),
                                      bias_c[:, t, :, :], ALU.add).then_inc(*dve_step.mark(("c0", t)))
                    dve.wait_ge(*dve_step.at(("c0", t)))
                    dve.tensor_reduce(nm, s3, AX.X, ALU.min).then_inc(*dve_step.mark(("c1", t)))
                    dve.wait_ge(*dve_step.at(("c1", t)))
                    dve.tensor_scalar(nm, nm, LEAST, None, ALU.min).then_inc(*dve_step.mark(("c2", t)))
                    dve.wait_ge(*dve_step.at(("c2", t)))
                    dve.tensor_tensor(s3, s3, nm.unsqueeze(2).to_broadcast([P, HEADS, NC]), ALU.subtract).then_inc(*lows.mark(n))
                    return
                m = (h + 8 * out_of(n)) % 16
                other = const("mask")[:, SEQ - nk:] if kind == "mla" else bias[:, h, SEQ - nk:]
                dve.tensor_tensor_reduce(s_buf[:, b, 0:nk], bank[:, 0:nk], other, 1.0, LEAST, ALU.add, ALU.min,
                                         neg_max[:, m:m + 1]).then_inc(*lows.mark(n))

            def pt_out(n):
                kind, t, h = UNITS[n]
                nk = 2 * P if kind == "cmp" else (t + 1) * P
                dve.wait_ge(*turned.at(("p", n)))
                if n >= 2:
                    dve.wait_ge(*mixed.at(n - 2))
                dve.tensor_copy(pt_buf[:, n % 2, 0:nk], TD[bank_of("T", ("p", n))][:, 0:nk]).then_inc(*dve_pt.mark(n))

            def out_row(kind, t):
                m = OUTS.index((kind, t))
                bank = O[m % 2].rearrange("p (h n) -> p h n", h=HEADS)
                d, r = den[:, 8 * (m % 3):8 * (m % 3) + 8], rden[:, 8 * (m % 3):8 * (m % 3) + 8]
                n = max(i for i, u in enumerate(UNITS) if u[0] == kind and u[1] == t)
                dve.wait_ge(*probs.at(n))
                if kind == "cmp":
                    dve.wait_ge(*dve_step.at(("den", t)))
                dve.tensor_scalar(d, d, 1e-30, None, ALU.max).then_inc(*dve_step.mark(("d1", kind, t)))
                dve.wait_ge(*dve_step.at(("d1", kind, t)))
                dve.reciprocal(r, d).then_inc(*dve_step.mark(("d2", kind, t)))
                dve.wait_ge(*dve_step.at(("d2", kind, t)))
                if kind != "mla":
                    j = ("cmp", "sel", "win").index(kind)
                    dve.tensor_tensor(r, r, gates[:, t, 8 * j:8 * j + 8], ALU.mult).then_inc(*dve_step.mark(("d3", kind, t)))
                    dve.wait_ge(*dve_step.at(("d3", kind, t)))
                rb = r.unsqueeze(2).to_broadcast([P, HEADS, HD])
                dve.wait_ge(*mixed.at(n))
                if kind == "mla":
                    dve.tensor_tensor(o_mla[:, t, :].rearrange("p (h n) -> p h n", h=HEADS), bank, rb, ALU.mult).then_inc(*o_used.mark((kind, t)))
                elif kind == "sel":
                    if t >= 2:
                        dve.wait_ge(*dve_step.at(("mixrow", 1, t - 2)))
                    dve.tensor_tensor(o_nsa[:, t % 2, :].rearrange("p (h n) -> p h n", h=HEADS), bank, rb, ALU.mult).then_inc(*o_used.mark((kind, t)))
                else:
                    tmp = raw_row[:, m % 2, :]
                    dve.tensor_tensor(tmp.rearrange("p (h n) -> p h n", h=HEADS), bank, rb, ALU.mult).then_inc(*dve_step.mark(("o", kind, t)))
                    dve.wait_ge(*dve_step.at(("o", kind, t)))
                    dve.tensor_tensor(o_nsa[:, t % 2, :], o_nsa[:, t % 2, :], tmp, ALU.add).then_inc(*o_used.mark((kind, t)))

            def nsa_sum(key):
                b, t = key
                n = 8 if b == "nq" else 4
                dve.wait_ge(*squares.at(key))
                dve.tensor_reduce(ss_row[:, 8 * (t % 2):8 * (t % 2) + n], square[:, 0:n * HD].rearrange("p (h n) -> p h n", h=n),
                                  AX.X, ALU.add).then_inc(*summed.mark(key))

            def nsa_row(key):
                b, t = key
                j = t % 2
                n = 8 if b == "nq" else 4
                rs = rs_row[:, 8 * j:8 * j + n]
                row = raw_row[:, j, 0:n * HD].rearrange("p (h n) -> p h n", h=n)
                dve.wait_ge(*rsqrt_done.at(key))
                dve.wait_ge(*copied.at(key))
                dve.tensor_tensor(row, row, rs.unsqueeze(2).to_broadcast([P, n, HD]), ALU.mult).then_inc(*dve_step.mark(("nr", key)))
                dve.wait_ge(*dve_step.at(("nr", key)))
                before = (b, t - 2) if t >= 2 else ("nq", NT - 2 + t) if b == "nkv" else None
                if before:
                    dve.wait_ge(*turned.at(before))
                fin = o_nsa[:, j, :]
                if b == "nq":
                    gain = const("g_nq").unsqueeze(1).unsqueeze(1).to_broadcast([P, 2, 4, HD])
                    dve.tensor_tensor(fin.rearrange("p (r g n) -> p g r n", r=4, g=2), row.rearrange("p (g r) n -> p g r n", g=2),
                                      gain, ALU.mult).then_inc(*scaled.mark(key))
                else:
                    gain = const("g_nk")[:, HD:3 * HD].rearrange("p (b n) -> p b n", b=2).unsqueeze(2).to_broadcast([P, 2, 2, HD])
                    dve.tensor_tensor(fin[:, 0:256].rearrange("p (b g n) -> p b g n", b=2, g=2), row.rearrange("p (b g) n -> p b g n", b=2),
                                      gain, ALU.mult).then_inc(*scaled.mark(key))

            def nsa_turned(key):
                b, t = key
                k = 4 if b == "nq" else 2
                dve.wait_ge(*turned.at(key))
                dst = (n_q if b == "nq" else n_k)[:, :, t * P:(t + 1) * P]
                src = TD[bank_of("T", key)][:, 0:k * P].rearrange("p (k s) -> p k s", k=k)
                dve.tensor_copy(dst, backwards(src) if b == "nq" else src).then_inc(*dve_step.mark(("turned", key)))

            dve.wait_ge(*pool_step.at("gnq"))
            for n in range(N_MLA):
                if n - 3 >= 0 and (n - 3) % 2 == 1:
                    pt_out(n - 3)
                low_unit(n)
                if n % 8 == 5 and n >= 8:
                    out_row("mla", n // 8 - 1)
                if n % 4 == 0 and n:
                    nsa_sum(nsa_rows[n // 4 - 1])
                    after(nsa_rows[n // 4 - 1])
                if n % 4 == 2 and n >= 4:
                    nsa_row(nsa_rows[n // 4 - 1])
                if n % 4 == 0 and n >= 8:
                    nsa_turned(nsa_rows[n // 4 - 2])
                for m in SPLIT_AT_UNIT.get(n, ()):
                    split_lo(m)
            for n in range(N_MLA, N_MLA + 3):
                if (n - 3) % 2 == 1:
                    pt_out(n - 3)
                if n == N_MLA:
                    nsa_turned(nsa_rows[-2])
                    nsa_sum(nsa_rows[-1])
                    after(nsa_rows[-1])

            def low_taps(t):
                dve.wait_ge(*copied.at(("taps", t)))
                src = TD[bank_of("T", ("taps", t))][HD:P, :].rearrange("p (j s) -> p j s", j=4)
                lo = int(t == 0)
                dve.tensor_copy(taps[HD:P, :, t * P - 1 + lo:(t + 1) * P - 1], src[:, :, lo:]).then_inc(*dve_step.mark(("taps", t)))
            nsa_row(nsa_rows[-1])
            out_row("mla", NT - 1)
            nsa_turned(nsa_rows[-1])

            dve.memset(v_diag, 0.0).then_inc(*dve_step.mark("vd0"))
            dve.memset(hid_v, 0.0).then_inc(*dve_step.mark("hv0"))
            dve.memset(hid_k, 0.0).then_inc(*dve_step.mark("hk0"))
            for t in range(NT):
                dve.wait_ge(*copied.at(("cmp", t)))
                g = gates[:, t, :]
                dve.tensor_scalar(g, g, 1.0, None, ALU.add).then_inc(*dve_step.mark(("g0", t)))
                dve.wait_ge(*dve_step.at(("g0", t)))
                dve.reciprocal(g, g).then_inc(*dve_step.mark(("g1", t)))
                after(("cmp", t))
                if t:
                    low_taps(t - 1)
            low_taps(NT - 1)
            for g in range(2):
                dve.wait_ge(*turned.at(("bc", g)))
                dve.tensor_copy(bias_c[:, :, g, :], TD[bank_of("T", ("bc", g))].rearrange("p (t n) -> p t n", t=NT)).then_inc(*dve_step.mark(("bc", g)))

            dve.wait_ge(*turned.at("gt"))
            dve.tensor_copy(gate_t.rearrange("p (t s) -> p t s", t=NT),
                            backwards(TD[bank_of("T", "gt")][0:24, :].rearrange("p (t s) -> p t s", t=NT))).then_inc(*dve_step.mark("gt"))
            dve.wait_ge(*turned.at("gates"))
            dve.tensor_copy(gates, TD[bank_of("T", "gates")][:, 0:NT * 24].rearrange("p (t n) -> p t n", t=NT)).then_inc(*dve_step.mark("gates"))

            def mix_rows(g, t):
                dve.wait_ge(*rsqrt_done.at(("mix", g, t)))
                if g or t:
                    i = g * NT + t - 2
                    if i >= 0:
                        dve.wait_ge(*turned.at(("mix", i // NT, i % NT)))
                src = o_mla[:, t, :] if g == 0 else o_nsa[:, t % 2, :]
                dve.scalar_tensor_tensor(mix_row[:, (g * NT + t) % 2, :], src, rs_mix[:, g * NT + t:g * NT + t + 1],
                                         gain_grp[:, 512 * g:512 * g + 512], ALU.mult, ALU.mult).then_inc(*dve_step.mark(("mixrow", g, t)))

            def mix_lows(g, t):
                at = (slice(None), slice(4 * g, 4 * g + 4), slice(t * P, (t + 1) * P))
                to_lo(("mix", g, t), act_lo[at], act_hi[at], 4)

            for kv in range(2):
                dve.wait_ge(*turned.at(("hid", kv)))
                bank = TD[bank_of("T", ("hid", kv))]
                dve.tensor_copy(pe_col[:, kv:kv + 1], bank[:, 64:65]).then_inc(*dve_step.mark(("pe", kv)))
                dve.wait_ge(*dve_step.at(("pe", kv)))
                dve.tensor_scalar(z_buf[:, 0, kv, :], bank[:, 0:2 * N_CMP], pe_col[:, kv:kv + 1], None, ALU.add).then_inc(*dve_step.mark(("z", kv)))
            dve.wait_ge(*gaing_in.at())
            mix_rows(0, 0)
            mix_rows(0, 1)
            for kv in range(2):
                dve.wait_ge(*exp_small.at(kv))
                e = z_buf[:, 1, kv, :]
                dve.tensor_scalar(e, e, 1.0, None, ALU.add).then_inc(*dve_step.mark(("e1", kv)))
                dve.wait_ge(*dve_step.at(("e1", kv)))
                dve.reciprocal(z_buf[:, 2, kv, :], e).then_inc(*dve_step.mark(("e2", kv)))
                dve.wait_ge(*dve_step.at(("e2", kv)))
                dve.wait_ge(*dve_step.at(("z", kv)))
                z = z_buf[:, 0, kv, :].rearrange("p (g c) -> p g c", g=2)
                r = z_buf[:, 2, kv, :].rearrange("p (g c) -> p g c", g=2)
                if kv == 0:
                    dve.wait_ge(*dve_step.at("hk0"))
                    dve.tensor_tensor(hid_k.rearrange("p (g c) -> p g c", g=2)[:, :, 0:N_CMP], z, r, ALU.mult).then_inc(*dve_step.mark("hid_k"))
                else:
                    for g in range(2):
                        rep = lambda v: v[:, g, :].unsqueeze(1).to_broadcast([P, 4, N_CMP])
                        dve.tensor_tensor(hid_v[:, g, :, 0:N_CMP], rep(z), rep(r), ALU.mult).then_inc(*dve_step.mark(("hid_v", g)))
            for t in range(2):
                mix_lows(0, t)
                mix_rows(0, t + 2)
            dve.wait_ge(*turned.at("kc"))
            bank = TD[bank_of("T", "kc")]
            dve.tensor_copy(kc_row, bank[0:64, 0:HD]).then_inc(*dve_step.mark("kc0"))
            dve.wait_ge(*dve_step.at("kc0"))
            dve.tensor_tensor(kc_sq, kc_row, kc_row, ALU.mult).then_inc(*dve_step.mark("kc1"))
            dve.wait_ge(*dve_step.at("kc1"))
            dve.tensor_reduce(kc_ss[0:64, :], kc_sq, AX.X, ALU.add).then_inc(*dve_step.mark("kc_ss"))
            dve.wait_ge(*turned.at("vc"))
            bank = TD[bank_of("T", "vc")]
            for h in range(4):
                ps = slice(32 * h, 32 * h + 32)
                dve.tensor_copy(v_diag[ps, :, HD * h:HD * h + HD], bank[ps, 0:2 * HD].rearrange("p (g n) -> p g n", g=2)).then_inc(*dve_step.mark(("vd", h)))
            dve.wait_ge(*rsqrt_done.at("kc"))
            dve.scalar_tensor_tensor(kc_sq, kc_row, kc_rs[0:64, :], const("g_nk", 64)[:, 0:HD], ALU.mult, ALU.mult).then_inc(*dve_step.mark("kc2"))
            for t in range(2, NT):
                mix_lows(0, t)
            dve.wait_ge(*turned.at("kcT"))
            bank = TD[bank_of("T", "kcT")]
            dve.tensor_copy(k_cmp[0:64, :], bank[0:64, 0:NC]).then_inc(*dve_step.mark("k0"))
            dve.tensor_copy(k_cmp[64:128, :], bank[0:64, NC:2 * NC]).then_inc(*dve_step.mark("k_cmp"))

            last = len(UNITS)
            dve.wait_ge(*dve_step.at("gates"))
            dve.wait_ge(*bias_in.at())
            for n in range(N_MLA, last + 5):
                if n - 3 >= N_MLA and n - 3 < last and (n - 3) % 2 == 1:
                    pt_out(n - 3)
                if n < last:
                    low_unit(n)
                if n - 1 >= N_MLA and n - 1 < last and UNITS[n - 1][0] == "cmp":
                    t, m = UNITS[n - 1][1], out_of(n - 1)
                    dve.wait_ge(*probs.at(n - 1))
                    dve.tensor_reduce(den[:, 8 * (m % 3):8 * (m % 3) + 8], p_buf[:, (n - 1) % 2, 0:256].rearrange("p (h c) -> p h c", h=HEADS),
                                      AX.X, ALU.add).then_inc(*dve_step.mark(("den", t)))
                for m in SPLIT_AT_UNIT.get(n, ()):
                    split_lo(m)
                done = n - 5
                if done >= N_MLA and done < last:
                    kind, t, h = UNITS[done]
                    if kind == "cmp" or h == HEADS - 1:
                        out_row(kind, t)
                done = n - 8
                if done >= N_MLA and done < last and UNITS[done][0] == "cmp":
                    mix_rows(1, UNITS[done][1])
                done = n - 11
                if done >= N_MLA and done < last and UNITS[done][0] == "cmp":
                    mix_lows(1, UNITS[done][1])
            mix_rows(1, NT - 1)
            mix_lows(1, NT - 1)

            dve.wait_ge(*gain2_in.at())
            for c in range(2):
                for t in range(NT):
                    key = ("wo", c, t)
                    dve.wait_ge(*dense_done.at(key))
                    xs = x[:, t, 512 * c:512 * c + 512]
                    dve.tensor_tensor(xs, D[bank_of("D", key)], xs, ALU.add).then_inc(*x2_done.mark((c, t)))
                    after(key)
                    if c and t:
                        ln_rows(t - 1, "ln2", gain_ln2)
                    if c and t >= 2:
                        ln_lows(t - 2, "ln2")
            ln_rows(NT - 1, "ln2", gain_ln2)
            ln_lows(NT - 2, "ln2")
            ln_lows(NT - 1, "ln2")

            for half in range(2):
                for f in range(UP_HALF):
                    dve.wait_ge(*relu_done.at((half, f)))
                    if f >= 2 or half:
                        dve.wait_ge(*a_lo_done.at((half, f - 2) if f >= 2 else (0, UP_HALF - 2 + f)))
                    dve.tensor_tensor(sq_b[:, f % 2, :], relu_b[:, f % 2, :], relu_b[:, f % 2, :], ALU.mult).then_inc(*sq_done.mark((half, f)))
                    after(("up", half, f))
                    dve.wait_ge(*a_hi_done.at((half, f)))
                    dve.tensor_tensor(a_lo[:, f, :], sq_b[:, f % 2, :], a_hi[:, f, :].bitcast(F32), ALU.subtract).then_inc(*a_lo_done.mark((half, f)))
                for c in range(2):
                    for i in range(UP_HALF // 2):
                        after(("down", half, c, i))
                    for t in range(NT):
                        dve.wait_ge(*mixed.at(("down", half, c, t)))
                        xs = x[:, t, 512 * c:512 * c + 512]
                        if half:
                            dve.wait_ge(*x2_done.at(("part", c, t)))
                        done = y_done.mark((t, c)) if half else x2_done.mark(("part", c, t))
                        dve.tensor_tensor(xs, down_banks(half, c)[t], xs, ALU.add).then_inc(*done)

        @block.tensor
        def _(pe):
            bank_users = {"D": [], "T": []}

            def take(kind, key, freed_by):
                users = bank_users[kind]
                if len(users) >= 2:
                    sig, k = users[-2]
                    pe.wait_ge(*sig.at(k))
                known["bank", kind, key] = len(users) % 2
                users.append((sig_key := freed_by))
                return (D if kind == "D" else T)[(len(users) - 1) % 2]

            def three(dst, act_cols, n, w_cols, start, stop):
                a_h, a_l = act_cols
                w_h, w_l = w_cols
                pe.matmul(dst, a_h, w_h, start=start, stop=False)
                pe.matmul(dst, a_h, w_l, start=False, stop=False)
                return pe.matmul(dst, a_l, w_h, start=False, stop=stop)

            def piece(what, i):
                n = PIECE_AT[what, i]
                pe.wait_ge(*lo_done.at(n))
                m = SPLIT_AT[n] % RING
                return w_hi[:, m, :], w_lo[:, m, :]

            def used(ins, what, i):
                ins.then_inc(*piece_used.mark(PIECE_AT[what, i]))

            def turn(key, tiles, freed_by, kind="T", step=P):
                bank = take(kind, key, freed_by)
                if kind == "D":
                    known["bank", "T", key] = 2 + known["bank", "D", key]
                for i, tile in enumerate(tiles):
                    k, m = tile.shape
                    ins = pe.transpose(bank[0:m, i * step:i * step + k], tile, ident[0:k, 0:k])
                ins.then_inc(*turned.mark(key))

            def turn_ln(name, t):
                pe.wait_ge(*scaled.at((name, t)))
                for half in range(2):
                    turn((name, t, half), [ln_row[:, t % 2, (4 * half + k) * P:(4 * half + k + 1) * P] for k in range(4)],
                         (turn_lo, (name, t, half)))

            def project(block_, t, pieces=range(4)):
                n = BLOCK_COLS[block_]
                key = (block_, t)
                if pieces[0] == 0:
                    take("D", key, (copied, key))
                dst = D[known["bank", "D", key]][:, 0:n]
                if block_ == "cq":
                    pe.wait_ge(*turn_lo.at(("ln1", t, 1)))
                for i in pieces:
                    h, l = piece(block_, i)
                    for j in range(2):
                        k = 2 * i + j
                        ins = three(dst, (act_hi[:, k, t * P:(t + 1) * P], act_lo[:, k, t * P:(t + 1) * P]), n,
                                    (h[:, j * n:(j + 1) * n], l[:, j * n:(j + 1) * n]), k == 0, k == KD - 1)
                    if i < 3 and t == NT - 1:
                        used(ins, block_, i)
                if pieces[-1] == 3:
                    ins.then_inc(*dense_done.mark(key))

            def expand(name, t, c):
                k0, kn, w = (0, 3, 4 * QK) if name == "uq" else (3, 2, 4 * (NOPE + VD))
                key = (name, t, c)
                dst = take("D", key, (copied, key))[:, 0:w]
                pe.wait_ge(*turn_lo.at(("cq" if name == "uq" else "ckv", t)))
                for k in range(kn):
                    h, l = piece(name, k)
                    ins = three(dst, (c_hi[:, k0 + k, t * P:(t + 1) * P], c_lo[:, k0 + k, t * P:(t + 1) * P]), w,
                                (h[:, c * w:(c + 1) * w], l[:, c * w:(c + 1) * w]), k == 0, k == kn - 1)
                    if t == NT - 1 and c == 1 and k < kn - 1:
                        used(ins, name, k)
                ins.then_inc(*dense_done.mark(key))

            def turn_heads(name, t):
                pe.wait_ge(*roped.at((name, t)))
                for half in range(2):
                    turn((name, t, half), [qk_out[:, (4 * half + h) * QK:(4 * half + h + 1) * QK] for h in range(4)],
                         (copied, ("turned", (name, t, half))))

            pe.wait_ge(*consts_in.at())
            for t in range(NT):
                turn_ln("ln1", t)
            pe.wait_ge(*onehot_in.at("table"))
            for j in range(4):
                lo, hi = 512 * j, min(512 * (j + 1), VEC)
                bank = take("T", ("vec", j), (dve_step, f"vec{j}"))
                pe.matmul(bank[0:8, 0:hi - lo], const("rel", 33), onehot[:, lo:hi], start=True, stop=True).then_inc(*turned.mark(("vec", j)))
            for t in range(NT):
                project("cq", t)
            def turn_latent(name, t):
                lo, n = (0, 3) if name == "cq" else (Q_RANK, 2)
                pe.wait_ge(*scaled.at((name, t)))
                turn((name, t), [c_row[:, t, lo + k * P:lo + (k + 1) * P] for k in range(n)], (turn_lo, (name, t)))
            for t in range(NT):
                project("ckv", t)
                turn_latent("cq", t)
            for t in range(NT):
                turn_latent("ckv", t)
                for c in range(2):
                    expand("uq", t, c)
                if t:
                    turn_heads("uq", t - 1)
            for t in range(NT):
                for c in range(2):
                    expand("ukv", t, c)
                turn_heads(*(("ukv", t - 1) if t else ("uq", NT - 1)))
            turn_heads("ukv", NT - 1)

            def score_unit(n):
                kind, t, h = UNITS[n]
                nk = (t + 1) * P
                bank = S[n % 2]
                if n >= 2:
                    pe.wait_ge(*(dve_step.at(("c0", UNITS[n - 2][1])) if UNITS[n - 2][0] == "cmp" else lows.at(n - 2)))
                if kind == "mla":
                    ins = pe.matmul(bank[:, 0:nk], m_q[0:QK, t, h, :], m_k[0:QK, h, 0:nk], start=True, stop=True)
                elif kind == "cmp":
                    for h in range(HEADS):
                        ps = slice(64 * (h // 4), 64 * (h // 4) + 64)
                        if h == 4:
                            ins.then_inc(*half_scored.mark(n))
                            pe.wait_ge(*half_scored.at(n))
                        ins = pe.matmul(bank[:, NC * h:NC * h + NC], n_q[ps, h % 4, t * P:(t + 1) * P], k_cmp[ps, :], start=True, stop=True)
                else:
                    ps = slice(64 * (h // 4), 64 * (h // 4) + 64)
                    ins = pe.matmul(bank[:, 0:nk], n_q[ps, h % 4, t * P:(t + 1) * P], n_k[ps, int(kind == "win"), 0:nk], start=True, stop=True)
                ins.then_inc(*scores.mark(n))

            def turn_unit(n):
                kind, t, h = UNITS[n]
                pe.wait_ge(*probs.at(n))
                count = 2 if kind == "cmp" else t + 1
                turn(("p", n), [p_buf[:, n % 2, j * P:(j + 1) * P] for j in range(count)], (act_pt if n % 2 == 0 else dve_pt, n))

            def mix_unit(n):
                kind, t, h = UNITS[n]
                m = out_of(n)
                bank = O[m % 2]
                pe.wait_ge(*(act_pt if n % 2 == 0 else dve_pt).at(n))
                if m >= 2 and (h == 0 or kind == "cmp"):
                    k2, t2 = OUTS[m - 2]
                    pe.wait_ge(*(o_used.at((k2, t2)) if k2 in ("mla", "sel") else dve_step.at(("o", k2, t2))))
                if kind == "cmp":
                    for g in range(2):
                        ins = pe.matmul(bank[:, 256 * g:256 * g + 256], pt_buf[:, n % 2, g * P:(g + 1) * P], v_diag[:, g, :], start=True, stop=True)
                else:
                    for j in range(t + 1):
                        v = m_v[:, j, h * VD:(h + 1) * VD] if kind == "mla" else \
                            n_v[:, j, int(kind == "win"), HD * (h // 4):HD * (h // 4) + HD]
                        ins = pe.matmul(bank[:, 64 * h:64 * h + 64], pt_buf[:, n % 2, j * P:(j + 1) * P], v, start=j == 0, stop=j == t)
                ins.then_inc(*mixed.mark(n))

            def turn_nsa(key):
                b, t = key
                pe.wait_ge(*scaled.at(key))
                turn(key, [o_nsa[:, t % 2, k * P:(k + 1) * P] for k in range(4 if b == "nq" else 2)], (dve_step, ("turned", key)))

            for half in range(2):
                pe.wait_ge(*copied.at(("turned", ("ukv", NT - 1, half))))
            for n in range(N_MLA + 4):
                if n < N_MLA:
                    score_unit(n)
                    project(*nsa_rows[n // 4], [n % 4])
                if n - 2 >= 0 and n - 2 < N_MLA:
                    turn_unit(n - 2)
                if n - 4 >= 0:
                    mix_unit(n - 4)
                if n < N_MLA and n % 4 == 3 and n >= 4:
                    turn_nsa(nsa_rows[n // 4 - 1])
            def turn_taps(t):
                pe.wait_ge(*copied.at(("dup", t)))
                turn(("taps", t), [raw_row[:, t % 2, j * P:(j + 1) * P] for j in range(4)], (dve_step, ("taps", t)))

            for t in range(NT):
                project("cmp", t)
                if t == 0:
                    turn_nsa(nsa_rows[-1])
                if t:
                    turn_taps(t - 1)
            turn_taps(NT - 1)
            for g in range(2):
                pe.wait_ge(*biasc_in.at(HEADS - 1))
                turn(("bc", g), [bias_ct[:, g, t * P:(t + 1) * P] for t in reversed(range(NT))], (dve_step, ("bc", g)))
            pe.wait_ge(*dve_step.at(("g1", NT - 1)))
            turn("gt", [gates[:, t, :] for t in range(NT)], (dve_step, "gt"))
            pe.wait_ge(*dve_step.at("gt"))
            turn("gates", [gate_t[:, t * P:(t + 1) * P] for t in range(NT)], (dve_step, "gates"), step=24)
            for t in range(NT):
                pe.wait_ge(*dve_step.at(("taps", t)))
            for kv in range(2):
                bank = take("T", ("hid", kv), (dve_step, ("z", kv)))
                for part in range(2):
                    for lp in range(16):
                        n = PIECE_AT["w1", 2 * kv + lp // 8]
                        if part == 0 and lp % 8 == 0:
                            pe.wait_ge(*raw_in[n % RAW].at(n))
                        w = raw[:, n % RAW, (lp % 8) * P:(lp % 8 + 1) * P]
                        if part == 0:
                            tok = taps[:, 2 * kv:2 * kv + 2, 2 * lp:2 * lp + CMP_STRIDE * (N_CMP - 1) + 1:CMP_STRIDE]
                            ins = pe.matmul(bank[:, 0:2 * N_CMP], w, tok, start=lp == 0, stop=lp == 15)
                        else:
                            ins = pe.matmul(bank[:, 64:65], w, const("pe")[:, 16 * kv + lp:16 * kv + lp + 1], start=lp == 0, stop=lp == 15)
                            if lp == 7:
                                ins.then_inc(*taps_used.mark(n))
                ins.then_inc(*turned.mark(("hid", kv)))

            def turn_mix(g, t):
                pe.wait_ge(*dve_step.at(("mixrow", g, t)))
                turn(("mix", g, t), [mix_row[:, (g * NT + t) % 2, k * P:(k + 1) * P] for k in range(4)],
                     (turn_lo, ("mix", g, t)), kind="D")

            turn_mix(0, 0)
            turn_mix(0, 1)
            pe.wait_ge(*dve_step.at("hid_k"))
            bank = take("T", "kc", (dve_step, "kc0"))
            pe.matmul(bank[0:64, 0:HD], hid_k, const("w2")[:, 0:HD], start=True, stop=True).then_inc(*turned.mark("kc"))
            bank = take("T", "vc", (dve_step, ("vd", 3)))
            for g in range(2):
                pe.wait_ge(*dve_step.at(("hid_v", g)))
                ins = pe.matmul(bank[:, g * HD:(g + 1) * HD], hid_v[:, g, :, :].rearrange("p h c -> p (h c)"), const("w2")[:, HD:], start=True, stop=True)
            ins.then_inc(*turned.mark("vc"))
            for t in range(2, NT):
                turn_mix(0, t)
            pe.wait_ge(*dve_step.at("kc2"))
            turn("kcT", [kc_sq], (dve_step, "k_cmp"))

            last = len(UNITS)
            pe.wait_ge(*dve_step.at("k_cmp"))
            for n in range(N_MLA, last + 10):
                if n < last:
                    score_unit(n)
                if n - 2 >= N_MLA and n - 2 < last:
                    turn_unit(n - 2)
                if n - 4 >= N_MLA and n - 4 < last:
                    mix_unit(n - 4)
                if n - 9 >= N_MLA and n - 9 < last and UNITS[n - 9][0] == "cmp":
                    turn_mix(1, UNITS[n - 9][1])

            for c in range(2):
                for t in range(NT):
                    dst = take("D", ("wo", c, t), (x2_done, (c, t)))
                    if c == 0:
                        pe.wait_ge(*turn_lo.at(("mix", 1, t)))
                        pe.wait_ge(*turn_lo.at(("mix", 0, t)))
                    for i in range(4):
                        h, l = piece("wo", 4 * c + i)
                        for j in range(2):
                            k = 2 * i + j
                            ins = three(dst, (act_hi[:, k, t * P:(t + 1) * P], act_lo[:, k, t * P:(t + 1) * P]), 512,
                                        (h[:, j * 512:(j + 1) * 512], l[:, j * 512:(j + 1) * 512]), k == 0, k == KD - 1)
                        if i < 3 and t == NT - 1:
                            used(ins, "wo", 4 * c + i)
                    ins.then_inc(*dense_done.mark(("wo", c, t)))
                    if c and t:
                        turn_ln("ln2", t - 1)
            turn_ln("ln2", NT - 1)

            for t in range(NT):
                pe.wait_ge(*turn_lo.at(("ln2", t, 1)))
            for half in range(2):
                for f in range(UP_HALF):
                    if f >= 4:
                        pe.wait_ge(*relu_done.at((half, f - 4)))
                    elif half:
                        pe.wait_ge(*x2_done.at(("part", 0, f)))
                    dst = up_bank(half, f)
                    h, l = piece(("up", half), f)
                    for k in range(KD):
                        ws = slice(k * P, (k + 1) * P)
                        pe.matmul(dst, h[:, ws], act_hi[:, k, :], start=k == 0, stop=False)
                        pe.matmul(dst, h[:, ws], act_lo[:, k, :], start=False, stop=False)
                        ins = pe.matmul(dst, l[:, ws], act_hi[:, k, :], start=False, stop=k == KD - 1)
                    ins.then_inc(*dense_done.mark(("up", half, f)))
                for c in range(2):
                    for i in range(UP_HALF // 2):
                        h, l = piece(("down", half, c), i)
                        for t in range(NT):
                            dst = down_banks(half, c)[t]
                            if i == 0 and (half or c):
                                if c == 1:
                                    pe.wait_ge(*relu_done.at((half, UP_HALF - 4 + t)))
                                else:
                                    pe.wait_ge(*x2_done.at(("part", 1, t)))
                            for j in range(2):
                                f = 2 * i + j
                                if t == 0:
                                    pe.wait_ge(*a_lo_done.at((half, f)))
                                ins = three(dst, (a_hi[:, f, t * P:(t + 1) * P], a_lo[:, f, t * P:(t + 1) * P]), 512,
                                            (h[:, j * 512:(j + 1) * 512], l[:, j * 512:(j + 1) * 512]), f == 0, f == UP_HALF - 1)
                            if i == UP_HALF // 2 - 1:
                                ins.then_inc(*mixed.mark(("down", half, c, t)))
                            elif t == NT - 1:
                                used(ins, ("down", half, c), i)


def t5_bucket(dist):
    n = np.maximum(dist, 0)
    exact = BUCKETS // 2
    large = np.log(np.maximum(n, 1).astype(np.float32) / np.float32(exact)) / np.float32(np.log(MAX_DIST / exact))
    large = np.minimum(exact + (large * np.float32(BUCKETS - exact)).astype(np.int32), BUCKETS - 1)
    return np.where(n < exact, n, large)


def shape_constants():
    p = np.arange(P)
    mask = np.where(SEQ - 1 - p[:, None] - np.arange(SEQ)[None, :] >= 0, 0.0, MASKED).astype(np.float32)
    half = ROPE // 2
    inv = (1.0 / (np.float32(10000.0) ** (np.arange(half, dtype=np.float32) / np.float32(half)))).astype(np.float32)
    angle = (np.arange(SEQ, dtype=np.float32)[:, None] * inv[None, :]).astype(np.float32)
    c, s = np.cos(angle), np.sin(angle)
    rope = np.concatenate([c, c, -s, s], axis=1).astype(np.float32).reshape(NT, P, 64).transpose(1, 0, 2)
    dist = np.concatenate([SEQ - 1 - np.arange(NEAR), FAR - 1 - np.arange(FAR) - FAR_LEAST])
    onehot = np.zeros((BUCKETS + 1, VEC), np.float32)
    onehot[t5_bucket(dist), np.arange(VEC)] = -1.0
    onehot[:, dist < 0] = 0.0
    onehot[BUCKETS, dist < 0] = 1.0
    return np.eye(P, dtype=np.float32), mask, rope.reshape(P, -1), onehot


def kernel(**inputs):
    import concourse.bacc as bacc
    from concourse.bass_utils import run_bass_kernel_spmd

    v = {k: np.asarray(x) for k, x in inputs.items()}
    rows = lambda *gs: np.ascontiguousarray(np.broadcast_to(np.concatenate([g.reshape(-1) for g in gs])[None, :], (P, sum(g.size for g in gs))))
    chunks = lambda w: w.reshape(-1, P, w.shape[1]).transpose(1, 0, 2)
    w_in, w_up, w_down, w_o = v["w_in"][0], v["w_up"][0], v["w_down"][0], v["w_o"][0]
    weights = np.zeros((len(PIECES), P, 1024), np.float32)
    for n, (what, i, width, _) in enumerate(PIECES):
        if what in IN_BLOCKS:
            block = np.concatenate([w_in[:, lo:lo + m] for lo, m in IN_BLOCKS[what]], axis=1)
            part = chunks(block[2 * i * P:2 * (i + 1) * P])
        elif what in ("uq", "ukv"):
            part = v["mla_w_" + what][0][i * P:(i + 1) * P]
        elif what == "w1":
            part = chunks(v["nsa_cmp_w1"][0, i // 2, 8 * P * (i % 2):8 * P * (i % 2 + 1)])
        elif what == "wo":
            part = chunks(w_o[2 * (i % 4) * P:2 * (i % 4 + 1) * P, 512 * (i // 4):512 * (i // 4 + 1)])
        elif what[0] == "up":
            f = what[1] * UP_HALF + i
            part = chunks(w_up[:, f * P:(f + 1) * P])
        else:
            f = what[1] * UP_HALF + 2 * i
            part = chunks(w_down[f * P:(f + 2) * P, 512 * what[2]:512 * (what[2] + 1)])
        weights[n, :, 0:width] = part.reshape(P, width)
    ident, mask, rope, onehot = shape_constants()
    pe = v["nsa_cmp_pe"][0].reshape(2, CMP_BLOCK // 2, P).transpose(2, 0, 1).reshape(P, -1)
    w2 = v["nsa_cmp_w2"][0].transpose(1, 0, 2).reshape(P, -1)
    consts = np.concatenate([ident, mask, rope, rows(v["mla_q_gain"]), rows(v["mla_k_gain"]), rows(v["nsa_q_gain"]),
                             rows(v["nsa_k_gain"]), pe, w2], axis=1)
    assert consts.shape[1] == CONST_LOADED
    arrays = {
        "x": v["x"][0], "weights": weights, "consts": consts, "onehot": onehot, "rel_bias": v["rel_bias"],
        "gain_ln1": rows(v["ln1_g"]), "gain_c": rows(v["mla_cq_norm_g"], v["mla_ckv_norm_g"]),
        "gain_grp": rows(v["grp_norm_mla"], v["grp_norm_nsa"]), "gain_ln2": rows(v["ln2_g"]),
    }
    arrays = {k: np.ascontiguousarray(x) for k, x in arrays.items()}

    known = {}
    for _ in range(2):
        nc = bacc.Bacc("TRN2", target_bir_lowering=False, num_devices=1)
        ins = {k: nc.dram_tensor(k, x.shape, mybir.dt.from_np(x.dtype), kind="ExternalInput").ap() for k, x in arrays.items()}
        out = nc.dram_tensor("y", (SEQ, D_MODEL), F32, kind="ExternalOutput").ap()
        build(nc, ins, out, known)
    r = run_bass_kernel_spmd(nc, [arrays], core_ids=[0])
    return np.asarray(r.results[0]["y"]).reshape(1, SEQ, D_MODEL)
```

```python
from contextlib import ExitStack

import concourse.bass as bass
import numpy as np
from concourse import mybir

F32 = mybir.dt.float32
F32R = mybir.dt.float32r
ALU = mybir.AluOpType
ACT = mybir.ActivationFunctionType
AX = mybir.AxisListType

P = 128
D_MODEL, SEQ, D_FF = 1024, 512, 4096
NT = SEQ // P
KD = D_MODEL // P
HEADS = 8
NOPE, ROPE, QK, VD = 64, 32, 96, 64
Q_RANK, KV_RANK = 384, 256
HD = 64
CMP_BLOCK, CMP_STRIDE, CMP_HIDDEN = 32, 16, 128
N_CMP = SEQ // CMP_STRIDE - 1
NC = 32
BUCKETS, MAX_DIST = 32, 128
EPS = 1e-6
MASKED = 1e30
LEAST = 1e29

_KV = Q_RANK + KV_RANK + ROPE + HEADS * HD
IN_BLOCKS = {
    "cq": [(0, Q_RANK)],
    "ckv": [(Q_RANK, KV_RANK + ROPE)],
    "nq": [(Q_RANK + KV_RANK + ROPE, HEADS * HD)],
    "nkv": [(_KV + 256, 512)],
    "cmp": [(_KV, 256), (_KV + 768, 24)],
}
BLOCK_COLS = {b: sum(n for _, n in cols) for b, cols in IN_BLOCKS.items()}
UP_HALF = D_FF // P // 2


RAW, RING = 3, 5


def weight_pieces():
    out = []

    def add(what, count, width, split=True, first=0):
        out.extend((what, i, width, split) for i in range(first, count))

    add("cq", 4, 2 * BLOCK_COLS["cq"])
    add("ckv", 4, 2 * BLOCK_COLS["ckv"])
    add("uq", Q_RANK // P, HEADS * QK)
    add("ukv", KV_RANK // P, HEADS * (NOPE + VD))
    add("nq", 4, 2 * BLOCK_COLS["nq"])
    add("nkv", 4, 2 * BLOCK_COLS["nkv"])
    add("cmp", 4, 2 * BLOCK_COLS["cmp"])
    add("wo", RING, 1024)
    add("w1", 4, 1024, False)
    add("wo", 8, 1024, first=RING)
    for half in range(2):
        add(("up", half), UP_HALF, 1024)
        for c in range(2):
            add(("down", half, c), UP_HALF // 2, 1024)
    return out


PIECES = weight_pieces()
PIECE_AT = {(what, i): n for n, (what, i, _, _) in enumerate(PIECES)}
SPLIT_AT = {n: m for m, n in enumerate(n for n, p in enumerate(PIECES) if p[3])}
SPLITS = list(SPLIT_AT)

NEAR = 640
FAR = SEQ + SEQ - CMP_STRIDE
FAR_LEAST = CMP_STRIDE * (NC - 1) + CMP_BLOCK - 1
VEC = NEAR + FAR


class Signal:

    def __init__(self, nc, ctx, name, known, step=1):
        self.sem = ctx.enter_context(nc.semaphore(name))
        self.name, self.known, self.step, self.count = name, known, step, 0

    def mark(self, key=0):
        self.count += self.step
        self.known[self.name, key] = self.count
        return self.sem, self.step

    def at(self, key=0):
        return self.sem, self.known.get((self.name, key), self.step)


UNITS = [("mla", t, h) for t in range(NT) for h in range(HEADS)]
N_MLA = len(UNITS)
for _b, _t in (("sel", 3), ("win", 3), ("sel", 2), ("win", 2), ("cmp", 3), ("sel", 1), ("cmp", 2), ("win", 1), ("cmp", 1),
               ("sel", 0), ("win", 0), ("cmp", 0)):
    UNITS += [(_b, _t, h) for h in range(1 if _b == "cmp" else HEADS)]
OUTS = list(dict.fromkeys(u[0:2] for u in UNITS))

QK_ROWS = [(b, t) for b in ("uq", "ukv") for t in range(NT)]
TURN_AT = {2: QK_ROWS[-2], 5: QK_ROWS[-1]}
PARTS = [o for o in OUTS if o[0] in ("win", "cmp")]
MIXES = [(0, t) for t in range(NT)] + [(1, t) for t in reversed(range(NT))]

WO_AT = {44: (3, 0), 46: (3, 1), 48: (3, 2), 50: (3, 3), 53: (2, 0), 55: (2, 1), 57: (2, 2), 58: (2, 3),
         62: (1, 0), 63: (1, 1), 64: (1, 2), 66: (1, 3)}
WO_ADD = {51: 3, 59: 2, 67: 1}

ROWS = [(b, t) for b in ("nq", "nkv", "cmp") for t in range(NT)]


def unit_of(row, piece_):
    return 2 * (4 * row + piece_) // 3


ROW_END = [unit_of(r, 3) for r in range(len(ROWS))]

DENSE = [("cq", t) for t in range(NT)] + [("ckv", t) for t in range(NT)]
DENSE += [("uq", t, c) for t in range(NT) for c in range(2)]
DENSE += [("ukv", t, c) for t in range(NT) for c in range(2)]
DENSE += [("nq", t) for t in range(NT)] + [("nkv", t) for t in range(NT)] + [("cmp", t) for t in range(NT)]
WO = [(0, t) for t in reversed(range(NT))] + [(1, t) for t in range(NT)]
DENSE += [("wo", c, t) for c, t in WO]
for _h in range(2):
    DENSE += [("up", _h, f) for f in range(UP_HALF)]
    DENSE += [("down", _h, c, i) for c in range(2) for i in range(UP_HALF // 2)]


def last_user(piece):
    what, i, _, _ = PIECES[piece]
    if what in ("uq", "ukv"):
        return (what, NT - 1, 1)
    if what == "wo":
        return ("wo", i // 4, 0 if i < 4 else NT - 1)
    if what[0] == "up":
        return (*what, i)
    if what[0] == "down":
        return (*what, i)
    return (what, NT - 1)


SPLIT_AFTER, SPLIT_AT_UNIT = {}, {}
_early = (("cq", NT - 1), ("ckv", NT - 1), ("uq", NT - 1, 1), ("ukv", NT - 1, 1))
for _m, _n in enumerate(SPLITS[RING:]):
    _g = last_user(SPLITS[_m])
    _what = PIECES[_n][0]
    if _what == "wo" and PIECES[_n][1] < RING:
        SPLIT_AT_UNIT.setdefault(N_MLA + 1 + 2 * PIECES[_n][1], []).append(_n)
    elif _g in (("nq", NT - 1), ("nkv", NT - 1)):
        SPLIT_AT_UNIT.setdefault(1 + unit_of(ROWS.index(_g), PIECES[SPLITS[_m]][1]), []).append(_n)
    elif _g in _early:
        SPLIT_AFTER.setdefault(DENSE[DENSE.index(_g) - 1], []).append(_n)
    else:
        SPLIT_AFTER.setdefault(_g, []).append(_n)


def out_of(n):
    return OUTS.index(UNITS[n][0:2])


CONST_AT, _at = {}, 0
for _name, _n in (("ident", P), ("mask", SEQ), ("rope", NT * 64), ("g_q", QK), ("g_k", QK), ("g_nq", HD), ("g_nk", 3 * HD),
                  ("pe", 2 * CMP_BLOCK // 2), ("w2", 2 * HD), ("rel", HEADS)):
    if _name == "rel":
        CONST_LOADED = _at
    CONST_AT[_name] = (_at, _n)
    _at += _n
CONST_COLS = _at


def build(nc, a, out, known):
    with ExitStack() as ctx:
        base = (nc.sbuf_base + 63) // 64 * 64
        top = [base]

        def place(name, cols, dt=F32, at=None, parts=P):
            off = top[0] if at is None else at
            if at is None:
                top[0] += cols * 4
            assert off + cols * 4 <= nc.sbuf_usable_end, (name, off)
            return nc.alloc_sbuf_tensor_at(name, [parts, cols], dt, offset=off)[:, :]

        def psum(name):
            return ctx.enter_context(nc.psum_tensor(name, [P, 512], F32))[:, :]

        def signal(name, step=1):
            return Signal(nc, ctx, name, known, step)

        x = place("x", NT * D_MODEL).rearrange("p (t d) -> p t d", t=NT)
        raw = place("raw", RAW * 1024).rearrange("p (s n) -> p s n", s=RAW)
        w_hi = place("w_hi", RING * 1024, F32R).rearrange("p (s n) -> p s n", s=RING)
        w_lo = place("w_lo", RING * 1024, F32R).rearrange("p (s n) -> p s n", s=RING)
        act_hi = place("act_hi", KD * SEQ, F32R).rearrange("p (k s) -> p k s", k=KD)
        act_lo = place("act_lo", KD * SEQ, F32R).rearrange("p (k s) -> p k s", k=KD)
        r_mla = top[0]
        m_q = place("m_q", NT * HEADS * P).rearrange("p (t h s) -> p t h s", t=NT, h=HEADS)
        m_k = place("m_k", HEADS * SEQ).rearrange("p (h s) -> p h s", h=HEADS)
        m_v = place("m_v", NT * HEADS * VD).rearrange("p (t n) -> p t n", t=NT)
        r_nsa = top[0]
        n_q = place("n_q", 4 * SEQ).rearrange("p (r s) -> p r s", r=4)
        n_k = place("n_k", 2 * SEQ).rearrange("p (b s) -> p b s", b=2)
        n_v = place("n_v", NT * 2 * P).rearrange("p (t b n) -> p t b n", t=NT, b=2)
        r_bias = top[0]
        bias = place("bias", HEADS * SEQ).rearrange("p (h s) -> p h s", h=HEADS)
        bias_c = place("bias_c", NT * 2 * P).rearrange("p (t g n) -> p t g n", t=NT, g=2)
        r_work = top[0]
        s_buf = place("s_buf", 2 * 512).rearrange("p (b n) -> p b n", b=2)
        p_buf = place("p_buf", 2 * 512).rearrange("p (b n) -> p b n", b=2)
        pt_buf = place("pt_buf", 2 * 512).rearrange("p (b n) -> p b n", b=2)
        r_temp = top[0]
        raw_all = place("raw_row", 2 * 512)
        raw_row = raw_all.rearrange("p (b n) -> p b n", b=2)
        raw_cmp = raw_all.rearrange("p (t n) -> p t n", t=NT)
        square = place("square", 512)
        r_onsa = top[0]
        o_nsa = place("o_nsa", 2 * 512).rearrange("p (b n) -> p b n", b=2)
        consts = place("consts", CONST_COLS)
        kr = place("kr", NT * ROPE).rearrange("p (t n) -> p t n", t=NT)
        gates = place("gates", NT * 24).rearrange("p (t n) -> p t n", t=NT)
        stats = place("stats", 384)
        tab_q = place("tab_q", NT * 128, at=r_onsa).rearrange("p (t n) -> p t n", t=NT)
        tab_k = place("tab_k", NT * 128, at=r_onsa + 2048).rearrange("p (t n) -> p t n", t=NT)
        o_mla = place("o_mla", NT * 512, at=r_mla).rearrange("p (t n) -> p t n", t=NT)
        gain_ln1 = place("gain_ln1", D_MODEL, at=r_mla)
        c_row = place("c_row", NT * (Q_RANK + KV_RANK), at=r_mla + 4096).rearrange("p (t n) -> p t n", t=NT)
        r_mk = r_mla + NT * HEADS * P * 4
        gain_c = place("gain_c", Q_RANK + KV_RANK, at=r_mk)
        onehot = place("onehot", VEC, at=r_mk + 2560, parts=33)
        bias_vec = place("bias_vec", VEC, at=r_mk + 2560 + VEC * 4, parts=8)
        c_hi = place("c_hi", 5 * SEQ, F32R, at=r_bias).rearrange("p (k s) -> p k s", k=5)
        c_lo = place("c_lo", 5 * SEQ, F32R, at=r_bias + 5 * SEQ * 4).rearrange("p (k s) -> p k s", k=5)
        ln_row = place("ln_row", 2 * D_MODEL, at=r_work).rearrange("p (b n) -> p b n", b=2)
        ln_sq = place("ln_sq", D_MODEL, at=r_work + 8192)
        qk_row = place("qk_row", 2 * HEADS * QK, at=r_nsa).rearrange("p (b n) -> p b n", b=2)
        qk_out = place("qk_out", HEADS * QK, at=r_nsa + 6144)
        qk_sq = place("qk_sq", HEADS * QK, at=r_nsa + 9216)
        rope_t = place("rope_t", HEADS * ROPE, at=r_temp)
        tap_planes = place("tap_planes", 6 * SEQ, at=r_mk).rearrange("p (j s) -> p j s", j=6)
        bias_ct = tap_planes[:, 4:6, :]
        v_diag = place("v_diag", 2 * 256, at=r_mk + 12288).rearrange("p (g n) -> p g n", g=2)
        hid_v = place("hid_v", 2 * P, at=r_mk + 14336).rearrange("p (g h c) -> p g h c", g=2, h=4)
        k_cmp = place("k_cmp", NC, at=r_mk + 15360)
        hid_k = place("hid_k", 2 * NC, at=r_mk + 15488)
        kc_row = place("kc_row", HD, at=r_mk + 15744, parts=64)
        kc_sq = place("kc_sq", HD, at=r_mk + 16000, parts=64)
        r_mv = r_mk + 16384
        gain_grp = place("gain_grp", D_MODEL, at=r_mv)
        gain_ln2 = place("gain_ln2", D_MODEL, at=r_mv + 4096)
        mix_row = place("mix_row", 2 * 512, at=r_mla + 8192).rearrange("p (b n) -> p b n", b=2)
        gate_t = place("gate_t", SEQ, at=r_mla + 13824, parts=24)
        z_buf = place("z_buf", 3 * 2 * 2 * N_CMP, at=r_mla + 12288).rearrange("p (a b n) -> p a b n", a=3, b=2)
        a_hi = place("a_hi", UP_HALF * SEQ, F32R, at=r_mla).rearrange("p (f s) -> p f s", f=UP_HALF)
        a_lo = place("a_lo", UP_HALF * SEQ, F32R, at=r_mla + UP_HALF * SEQ * 4).rearrange("p (f s) -> p f s", f=UP_HALF)
        relu_b = place("relu_b", 2 * 512, at=r_work).rearrange("p (b n) -> p b n", b=2)
        sq_b = place("sq_b", 2 * 512, at=r_work + 4096).rearrange("p (b n) -> p b n", b=2)

        def const(name, parts=P):
            at, n = CONST_AT[name]
            return consts[0:parts, at:at + n]

        ident = const("ident")
        rope = const("rope").rearrange("p (t n) -> p t n", t=NT)
        stat_at = [0]

        def stat(n):
            stat_at[0] += n
            assert stat_at[0] <= 384
            return stats[:, stat_at[0] - n:stat_at[0]]

        ss_ln, rs_ln = stat(NT), stat(NT)
        ss_c, rs_c, ss_kr = stat(2 * NT), stat(2 * NT), stat(NT)
        ss_row, rs_row = stat(16), stat(16)
        neg_max = stat(8 * 2)
        den, rden = stat(8 * 4), stat(8 * 4)
        half_neg = stat(8)
        ss_mix, rs_mix = stat(2 * NT), stat(2 * NT)
        pe_col, kc_ss, kc_rs = stat(2), stat(1), stat(1)

        banks = [psum(f"bank{i}") for i in range(8)]
        D, T, S, O = banks[0:2], banks[2:4], banks[4:6], banks[6:8]
        TD = T + D

        x_in = [signal(f"x_in{t}", 16) for t in range(NT)]
        raw_in = [signal(f"raw_in{s}", 16) for s in range(RAW)]
        consts_in, gain1_in, gainc_in = signal("consts_in", 16), signal("gain1_in", 16), signal("gainc_in", 16)
        onehot_in, vec_out = signal("onehot_in", 16), signal("vec_out", 16)
        bias_in, biasc_in = signal("bias_in", 16), signal("biasc_in", 16)
        gaing_in, gain2_in, y_out = signal("gaing_in", 16), signal("gain2_in", 16), signal("y_out", 16)
        hi_done, lo_done = signal("hi_done"), signal("lo_done")
        piece_used, taps_used = signal("piece_used"), signal("taps_used")
        dense_done, turned = signal("dense_done"), signal("turned")
        scores, half_scored, mixed = signal("scores"), signal("half_scored"), signal("mixed")
        squares, copied, turn_hi = signal("squares"), signal("copied"), signal("turn_hi")
        probs, relu_done, a_hi_done = signal("probs"), signal("relu_done"), signal("a_hi_done")
        act_pt, exp_small = signal("act_pt"), signal("exp_small")
        summed, scaled, turn_lo = signal("summed"), signal("scaled"), signal("turn_lo")
        lows, dve_pt, o_used = signal("lows"), signal("dve_pt"), signal("o_used")
        mixed_last = signal("mixed_last")
        dve_step, x2_done, sq_done, a_lo_done = signal("dve_step"), signal("x2_done"), signal("sq_done"), signal("a_lo_done")
        y_done = signal("y_done")
        rsqrt_done, pool_step, roped = signal("rsqrt_done"), signal("pool_step"), signal("roped")
        o_summed, mix_done = signal("o_summed"), signal("mix_done")

        vec_dram = nc.dram_tensor("bias_by_distance", [HEADS, VEC], F32, kind="Internal").ap()

        def bank_of(kind, key):
            return known.get(("bank", kind, key), 0)

        def raw_free(n):
            what, i, _, split = PIECES[n]
            if split:
                return lo_done.at(n)
            return turned.at(("hid", i // 2)) if i % 2 else taps_used.at(n)

        def used_by(n):
            what, i, _, _ = PIECES[n]
            last = {"uq": Q_RANK // P, "ukv": KV_RANK // P}.get(what, 4)
            if what[0] == "up":
                return dense_done.at((*what, i))
            if what[0] == "down":
                return mixed.at((*what, NT - 1)) if i == UP_HALF // 2 - 1 else piece_used.at(n)
            if i % last < last - 1:
                return piece_used.at(n)
            return dense_done.at(last_user(n))

        def up_bank(half, f):
            return ((S + O) if half == 0 else (D + T))[f % 4]

        def down_banks(half, c):
            return (D + T) if (half + c) % 2 == 0 else (S + O)

        def backwards(tiles):
            return tiles[:, :, ::-1]

        block = ctx.enter_context(nc.Block())

        @block.sync
        def _(sp):
            for t in range(NT):
                sp.dma_start(x[:, t, :], a["x"][t * P:(t + 1) * P, :]).then_inc(*x_in[t].mark())
            for n, (what, i, width, split) in enumerate(PIECES):
                if n >= RAW:
                    sp.wait_ge(*raw_free(n - RAW))
                sp.dma_start(raw[:, n % RAW, 0:width], a["weights"][n, :, 0:width]).then_inc(*raw_in[n % RAW].mark(n))
            for t in range(NT):
                for c in range(2):
                    sp.wait_ge(*y_done.at((t, c)))
                    sp.dma_start(out[t * P:(t + 1) * P, c * 512:(c + 1) * 512],
                                 x[:, t, c * 512:(c + 1) * 512]).then_inc(*y_out.mark((t, c)))
            sp.wait_ge(*y_out.at((NT - 1, 1)))

        @block.gpsimd
        def _(pool):
            pool.memset(half_neg, -0.5).then_inc(*pool_step.mark("half"))
            pool.memset(consts[0:33, CONST_AT["rel"][0]:CONST_AT["rel"][0] + 8], MASKED).then_inc(*pool_step.mark("rel0"))
            pool.wait_ge(*pool_step.at("rel0"))
            pool.dma_start(const("rel", 32), a["rel_bias"]).then_inc(*onehot_in.mark("rel"))
            pool.dma_start(onehot, a["onehot"]).then_inc(*onehot_in.mark("table"))
            pool.wait_ge(*consts_in.at())
            pool.tensor_scalar(const("g_q"), const("g_q"), -float(QK) ** -0.5, 1.0, ALU.mult, ALU.mult).then_inc(*pool_step.mark("gq"))
            pool.tensor_scalar(const("g_nq"), const("g_nq"), -float(HD) ** -0.5, 1.0, ALU.mult, ALU.mult).then_inc(*pool_step.mark("gnq"))
            pool.wait_ge(*pool_step.at("gq"))
            for name, tab in (("g_q", tab_q), ("g_k", tab_k)):
                g = const(name)
                for n, lo, hi in ((0, 0, NOPE), (NOPE, NOPE, QK), (QK, NOPE + 16, QK), (QK + 16, NOPE, NOPE + 16)):
                    w = hi - lo
                    gain = g[:, lo:hi].unsqueeze(1).to_broadcast([P, NT, w])
                    if n == 0:
                        ins = pool.tensor_scalar(tab[:, :, 0:w], gain, 1.0, 1.0, ALU.mult, ALU.mult)
                    else:
                        ins = pool.tensor_tensor(tab[:, :, n:n + w], gain, rope[:, :, n - NOPE:n - NOPE + w], ALU.mult)
                ins.then_inc(*pool_step.mark(name))

            def rsqrt(key, out_, in_, width, after=None):
                pool.tensor_scalar(in_, in_, 1.0 / width, EPS, ALU.mult, ALU.add).then_inc(*pool_step.mark(("ms", key)))
                pool.wait_ge(*pool_step.at(("ms", key)))
                n = in_.shape[1]
                pool.tensor_tensor(out_, in_, half_neg[0:in_.shape[0], 0:n], ALU.pow).then_inc(*rsqrt_done.mark(key))

            pool.wait_ge(*pool_step.at("half"))
            for t in range(NT):
                pool.wait_ge(*squares.at(("ln1", t)))
                rsqrt(("ln1", t), rs_ln[:, t:t + 1], ss_ln[:, t:t + 1], D_MODEL)
            pool.wait_ge(*dve_step.at("vec3"))
            pool.dma_start(vec_dram, bias_vec).then_inc(*vec_out.mark())
            for c, (b, width) in enumerate((("cq", Q_RANK), ("ckv", KV_RANK))):
                for t in range(NT):
                    pool.wait_ge(*squares.at((b, t)))
                    rsqrt((b, t), rs_c[:, c * NT + t:c * NT + t + 1], ss_c[:, c * NT + t:c * NT + t + 1], width)

            def head_rsqrt(name, t):
                b = t % 2
                ss, rs = ss_row[:, 8 * b:8 * b + 8], rs_row[:, 8 * b:8 * b + 8]
                pool.wait_ge(*summed.at((name, t)))
                if name == "ukv":
                    pool.tensor_scalar(ss, ss, ss_kr[:, t:t + 1], 1.0, ALU.add, ALU.mult).then_inc(*pool_step.mark(("kr", t)))
                    pool.wait_ge(*pool_step.at(("kr", t)))
                rsqrt((name, t), rs, ss, QK)

            def rotate(name, t):
                tab = tab_q if name == "uq" else tab_k
                row = qk_row[:, t % 2, :].rearrange("p (h n) -> p h n", h=HEADS)
                fin = qk_out.rearrange("p (h n) -> p h n", h=HEADS)
                tmp = rope_t.rearrange("p (h n) -> p h n", h=HEADS)
                i = QK_ROWS.index((name, t))
                if i:
                    pool.wait_ge(*roped.at(QK_ROWS[i - 1]))
                pool.wait_ge(*scaled.at((name, t)))
                for lo, src in ((0, NOPE + 16), (16, NOPE)):
                    sin = tab[:, t, QK + lo:QK + lo + 16].unsqueeze(1).to_broadcast([P, HEADS, 16])
                    ins = pool.tensor_tensor(tmp[:, :, lo:lo + 16], row[:, :, src:src + 16], sin, ALU.mult)
                ins.then_inc(*pool_step.mark(("rot", name, t)))
                pool.wait_ge(*pool_step.at(("rot", name, t)))
                pool.wait_ge(*dve_step.at(("gain", name, t)))
                pool.tensor_tensor(fin[:, :, NOPE:QK], fin[:, :, NOPE:QK], tmp, ALU.add).then_inc(*roped.mark((name, t)))

            head_rsqrt(*QK_ROWS[0])
            for i, key in enumerate(QK_ROWS):
                if i + 1 < len(QK_ROWS):
                    head_rsqrt(*QK_ROWS[i + 1])
                rotate(*key)

            pool.wait_ge(*vec_out.at())
            pool.wait_ge(*dense_done.at(("ukv", NT - 1, 1)))
            pool.dma_start(bias, bass.AP(vec_dram.tensor, 0, [[1, P], [VEC, HEADS], [1, SEQ]])).then_inc(*bias_in.mark())

            for b in ("nq", "nkv"):
                for t in range(NT):
                    j = t % 2
                    n = 8 if b == "nq" else 4
                    pool.wait_ge(*summed.at((b, t)))
                    rsqrt((b, t), rs_row[:, 8 * j:8 * j + n], ss_row[:, 8 * j:8 * j + n], HD)

            pool.wait_ge(*mixed.at(N_MLA - 1))
            for h in range(HEADS):
                pool.dma_start(bias_ct[32 * (h % 4):32 * (h % 4) + 32, h // 4, :],
                               bass.AP(vec_dram.tensor, h * VEC + NEAR, [[CMP_STRIDE, NC], [1, SEQ]])
                               ).then_inc(*biasc_in.mark(h))
            pool.dma_start(gain_grp, a["gain_grp"]).then_inc(*gaing_in.mark())
            pool.dma_start(gain_ln2, a["gain_ln2"]).then_inc(*gain2_in.mark())

            def mix_row_of(g, t):
                pool.wait_ge(*squares.at(("mix", g, t)))
                at = g * NT + t
                rsqrt(("mix", g, t), rs_mix[:, at:at + 1], ss_mix[:, at:at + 1], 512)
                i = MIXES.index((g, t))
                if (g, t) == (1, 0):
                    return
                if i >= 2:
                    pool.wait_ge(*turned.at(("mix", *MIXES[i - 2])))
                pool.wait_ge(*rsqrt_done.at(("mix", g, t)))
                src = o_mla[:, t, :] if g == 0 else o_nsa[:, t % 2, :]
                pool.tensor_scalar(mix_row[:, i % 2, :], src, rs_mix[:, at:at + 1], 1.0, ALU.mult, ALU.mult).then_inc(*pool_step.mark(("scaled", g, t)))
                pool.wait_ge(*pool_step.at(("scaled", g, t)))
                pool.tensor_tensor(mix_row[:, i % 2, :], mix_row[:, i % 2, :], gain_grp[:, 512 * g:512 * g + 512], ALU.mult).then_inc(*mix_done.mark((g, t)))

            def sum_branches(kind, t):
                if kind == "cmp":
                    pool.wait_ge(*o_summed.at(("win", t)))
                pool.wait_ge(*dve_step.at(("o", kind, t)))
                pool.tensor_tensor(o_nsa[:, t % 2, :], o_nsa[:, t % 2, :], raw_row[:, PARTS.index((kind, t)) % 2, :], ALU.add).then_inc(*o_summed.mark((kind, t)))

            pool.wait_ge(*gaing_in.at())
            for t in range(NT):
                mix_row_of(0, t)
            sum_branches("win", 3)
            pool.wait_ge(*dve_step.at("kc_ss"))
            rsqrt("kc", kc_rs[0:64, :], kc_ss[0:64, :], HD)
            sum_branches("win", 2)
            for t in (3, 2):
                sum_branches("cmp", t)
                mix_row_of(1, t)
            for kind in ("win", "cmp"):
                sum_branches(kind, 1)
            mix_row_of(1, 1)
            mix_row_of(1, 0)
            for t in range(NT):
                pool.wait_ge(*squares.at(("ln2", t)))
                rsqrt(("ln2", t), rs_ln[:, t:t + 1], ss_ln[:, t:t + 1], D_MODEL)

        @block.scalar
        def _(act):
            act.dma_start(gain_ln1, a["gain_ln1"]).then_inc(*gain1_in.mark())
            act.dma_start(consts[:, 0:CONST_LOADED], a["consts"]).then_inc(*consts_in.mark())
            act.dma_start(gain_c, a["gain_c"]).then_inc(*gainc_in.mark())

            def split_hi(n):
                m, width = SPLIT_AT[n], PIECES[n][2]
                act.wait_ge(*raw_in[n % RAW].at(n))
                if m >= RING:
                    act.wait_ge(*used_by(SPLITS[m - RING]))
                act.activation(w_hi[:, m % RING, 0:width], raw[:, n % RAW, 0:width], ACT.Copy).then_inc(*hi_done.mark(n))

            def after(group):
                for n in SPLIT_AFTER.get(group, ()):
                    split_hi(n)

            def to_hi(key, dst, cols, width):
                act.wait_ge(*turned.at(key))
                src = TD[bank_of("T", key)][:, 0:cols * width].rearrange("p (k s) -> p k s", k=cols)
                if key[0] == "mix":
                    src = backwards(src)
                act.activation(dst, src, ACT.Copy).then_inc(*turn_hi.mark(key))

            for t in range(NT):
                act.wait_ge(*x_in[t].at())
                if t:
                    act.wait_ge(*squares.at(("ln1", t - 1)))
                act.activation(ln_sq, x[:, t, :], ACT.Square, accum_out=ss_ln[:, t:t + 1]).then_inc(*squares.mark(("ln1", t)))
            for n in SPLITS[:3]:
                split_hi(n)
            for t in range(NT):
                for half in range(2):
                    to_hi(("ln1", t, half), act_hi[:, 4 * half:4 * half + 4, t * P:(t + 1) * P], 4, P)
            for n in SPLITS[3:RING]:
                split_hi(n)

            for t in range(NT):
                key = ("cq", t)
                act.wait_ge(*dense_done.at(key))
                bank = D[bank_of("D", key)]
                if t:
                    act.wait_ge(*squares.at(("cq", t - 1)))
                act.activation(square[:, 0:Q_RANK], bank[:, 0:Q_RANK], ACT.Square, accum_out=ss_c[:, t:t + 1]).then_inc(*squares.mark(key))
                act.activation(c_row[:, t, 0:Q_RANK], bank[:, 0:Q_RANK], ACT.Copy).then_inc(*copied.mark(key))
                after(key)
            for t in range(NT):
                key = ("ckv", t)
                act.wait_ge(*dense_done.at(key))
                bank = D[bank_of("D", key)]
                act.wait_ge(*squares.at(("ckv", t - 1) if t else ("cq", NT - 1)))
                act.activation(square[:, KV_RANK:KV_RANK + ROPE], bank[:, KV_RANK:KV_RANK + ROPE], ACT.Square, accum_out=ss_kr[:, t:t + 1]).then_inc(*squares.mark(("kr", t)))
                act.activation(square[:, 0:KV_RANK], bank[:, 0:KV_RANK], ACT.Square, accum_out=ss_c[:, NT + t:NT + t + 1]).then_inc(*squares.mark(key))
                act.activation(kr[:, t, :], bank[:, KV_RANK:KV_RANK + ROPE], ACT.Copy).then_inc(*copied.mark(("kr", t)))
                act.activation(c_row[:, t, Q_RANK:], bank[:, 0:KV_RANK], ACT.Copy).then_inc(*copied.mark(key))
                after(key)
                to_hi(("cq", t), c_hi[:, 0:3, t * P:(t + 1) * P], 3, P)

            def turned_out(name, t, half):
                key = (name, t, half)
                act.wait_ge(*turned.at(key))
                src = TD[bank_of("T", key)][0:QK, :].rearrange("p (h s) -> p h s", h=4)
                if name == "uq":
                    src = backwards(src)
                dst = m_q[0:QK, t, 4 * half:4 * half + 4, :] if name == "uq" else m_k[0:QK, 4 * half:4 * half + 4, t * P:(t + 1) * P]
                act.activation(dst, src, ACT.Copy).then_inc(*copied.mark(("turned", key)))

            for i, (name, t) in enumerate(QK_ROWS):
                n, w = (QK, QK) if name == "uq" else (NOPE, NOPE + VD)
                row = qk_row[:, t % 2, :].rearrange("p (h n) -> p h n", h=HEADS)
                sq = qk_sq[:, 0:HEADS * n].rearrange("p (h n) -> p h n", h=HEADS)
                src = [D[bank_of("D", (name, t, c))][:, 0:4 * w].rearrange("p (h n) -> p h n", h=4) for c in range(2)]
                if (name, t) == ("ukv", 1):
                    act.wait_ge(*vec_out.at())
                if i >= 3:
                    for half in range(2):
                        turned_out(*QK_ROWS[i - 3], half)
                if name == "uq":
                    to_hi(("ckv", t), c_hi[:, 3:5, t * P:(t + 1) * P], 2, P)
                for c in range(2):
                    act.wait_ge(*dense_done.at((name, t, c)))
                    if i:
                        act.wait_ge(*summed.at(QK_ROWS[i - 1]))
                    act.activation(sq[:, 4 * c:4 * c + 4, :], src[c][:, :, 0:n], ACT.Square).then_inc(*squares.mark((name, t, c)))
                for c in range(2):
                    if i >= 2:
                        act.wait_ge(*roped.at(QK_ROWS[i - 2]))
                    if name == "ukv":
                        act.activation(m_v[:, t, 4 * c * VD:(4 * c + 4) * VD].rearrange("p (h n) -> p h n", h=4),
                                       src[c][:, :, NOPE:], ACT.Copy).then_inc(*copied.mark(("v", t, c)))
                    act.activation(row[:, 4 * c:4 * c + 4, 0:n], src[c][:, :, 0:n], ACT.Copy).then_inc(*copied.mark((name, t, c)))
                    after((name, t, c))
            for half in range(2):
                turned_out(*QK_ROWS[-3], half)

            def exp_unit(n):
                kind, t, h = UNITS[n]
                nk = 2 * P if kind == "cmp" else (t + 1) * P
                act.wait_ge(*lows.at(n))
                if n >= 2:
                    act.wait_ge(*turned.at(("p", n - 2)))
                if kind == "cmp":
                    act.activation(p_buf[:, n % 2, 0:nk], s_buf[:, n % 2, 0:nk], ACT.Exp, scale=-1.0).then_inc(*probs.mark(n))
                else:
                    m, d = (h + 8 * out_of(n)) % 16, h + 8 * (out_of(n) % 4)
                    act.activation(p_buf[:, n % 2, 0:nk], s_buf[:, n % 2, 0:nk], ACT.Exp, scale=-1.0,
                                   bias=neg_max[:, m:m + 1], accum_out=den[:, d:d + 1]).then_inc(*probs.mark(n))

            def pt_out(n):
                kind, t, h = UNITS[n]
                nk = 2 * P if kind == "cmp" else (t + 1) * P
                act.wait_ge(*turned.at(("p", n)))
                if n >= 2:
                    act.wait_ge(*mixed.at(n - 2))
                act.activation(pt_buf[:, n % 2, 0:nk], TD[bank_of("T", ("p", n))][:, 0:nk], ACT.Copy).then_inc(*act_pt.mark(n))

            def row_in(key):
                b, t = key
                act.wait_ge(*dense_done.at(key))
                bank = D[bank_of("D", key)]
                j = t % 2
                if b == "cmp":
                    act.wait_ge(*scaled.at(("nkv", NT - 2 + t // 2)))
                    act.activation(raw_cmp[:, t, :], bank[:, 0:256], ACT.Copy).then_inc(*copied.mark(("raw", t)))
                    act.activation(gates[:, t, :], bank[:, 256:280], ACT.Exp, scale=-1.0).then_inc(*copied.mark(key))
                    return
                before = (b, t - 1) if t else ("nq", NT - 1) if b == "nkv" else None
                if before:
                    act.wait_ge(*summed.at(before))
                two = (b, t - 2) if t >= 2 else ("nq", NT - 2 + t) if b == "nkv" else None
                if two:
                    act.wait_ge(*scaled.at(two))
                if b == "nq":
                    act.activation(square, bank, ACT.Square).then_inc(*squares.mark(key))
                    act.activation(raw_row[:, j, :], bank, ACT.Copy).then_inc(*copied.mark(key))
                else:
                    src = bank.rearrange("p (b v n) -> p b v n", b=2, v=2)
                    two_b = lambda r: r[:, 0:256].rearrange("p (b n) -> p b n", b=2)
                    act.activation(two_b(square), src[:, :, 0, :], ACT.Square).then_inc(*squares.mark(key))
                    act.activation(n_v[:, t, :, :], src[:, :, 1, :], ACT.Copy).then_inc(*copied.mark(("nv", t)))
                    act.activation(two_b(raw_row[:, j, :]), src[:, :, 0, :], ACT.Copy).then_inc(*copied.mark(key))

            def unit_step(n, last):
                if n - 3 >= 0 and (n - 3) % 2 == 0:
                    pt_out(n - 3)
                if n - 1 >= 0 and n - 1 < last:
                    exp_unit(n - 1)

            for n in range(N_MLA):
                unit_step(n, N_MLA)
                if n in TURN_AT:
                    for half in range(2):
                        turned_out(*TURN_AT[n], half)
                if n == 3:
                    act.wait_ge(*roped.at(QK_ROWS[-1]))
                if n - 1 in ROW_END:
                    row_in(ROWS[ROW_END.index(n - 1)])
                for m in SPLIT_AT_UNIT.get(n, ()):
                    split_hi(m)

            def top_taps(t):
                act.wait_ge(*turned.at(("taps", t)))
                bank = TD[bank_of("T", ("taps", t))][:, 0:2 * P].rearrange("p (j s) -> p j s", j=2)
                for i in range(2):
                    act.activation(tap_planes[0:HD, 2 * i:2 * i + 2, t * P:(t + 1) * P], bank[HD * i:HD * i + HD, :, :],
                                   ACT.Copy).then_inc(*copied.mark(("taps", t, i)))

            def mix_square(g, t):
                src = o_mla[:, t, :] if g == 0 else o_nsa[:, t % 2, :]
                i = MIXES.index((g, t))
                if i:
                    act.wait_ge(*squares.at(("mix", *MIXES[i - 1])))
                act.activation(square, src, ACT.Square, accum_out=ss_mix[:, g * NT + t:g * NT + t + 1]).then_inc(*squares.mark(("mix", g, t)))

            for n in range(N_MLA, N_MLA + 3):
                if (n - 3) % 2 == 0:
                    pt_out(n - 3)
                if n - 1 < N_MLA:
                    exp_unit(n - 1)
                if n == N_MLA:
                    row_in(ROWS[-1])
            last = len(UNITS)
            for n in range(N_MLA, last + 3):
                if n - 3 >= N_MLA and (n - 3) % 2 == 0:
                    pt_out(n - 3)
                if n - 1 >= N_MLA and n - 1 < last:
                    exp_unit(n - 1)
                u = n - N_MLA
                if 1 <= u < 1 + NT:
                    top_taps(u - 1)
                if u in (6, 8, 10, 12):
                    act.wait_ge(*o_used.at(("mla", u // 2 - 3)))
                    mix_square(0, u // 2 - 3)
                if u in (15, 19):
                    kv = (u - 15) // 4
                    act.wait_ge(*dve_step.at(("z", kv)))
                    act.activation(z_buf[:, 1, kv, :], z_buf[:, 0, kv, :], ACT.Exp, scale=-1.0).then_inc(*exp_small.mark(kv))
                if u in (20, 22, 24, 26):
                    t = u // 2 - 10
                    to_hi(("mix", 0, t), act_hi[:, 0:4, t * P:(t + 1) * P], 4, P)
                done = n - 5
                if done >= N_MLA and (done < last) and UNITS[done][0] == "cmp" and UNITS[done][1] > 0:
                    t = UNITS[done][1]
                    act.wait_ge(*o_summed.at(("cmp", t)))
                    mix_square(1, t)
                done = n - 10
                if done >= N_MLA and UNITS[done][0] == "cmp":
                    t = UNITS[done][1]
                    to_hi(("mix", 1, t), act_hi[:, 4:8, t * P:(t + 1) * P], 4, P)
                for m in SPLIT_AT_UNIT.get(n, ()):
                    split_hi(m)
            act.wait_ge(*o_used.at(("cmp", 0)))
            mix_square(1, 0)
            to_hi(("mix", 1, 0), act_hi[:, 4:8, 0:P], 4, P)

            after(("wo", 0, 0))
            for t in range(NT):
                act.wait_ge(*x2_done.at((1, t)))
                if t:
                    act.wait_ge(*squares.at(("ln2", t - 1)))
                act.activation(ln_sq, x[:, t, :], ACT.Square, accum_out=ss_ln[:, t:t + 1]).then_inc(*squares.mark(("ln2", t)))
                if t < NT - 1:
                    after(("wo", 1, t))
                if t:
                    for half in range(2):
                        to_hi(("ln2", t - 1, half), act_hi[:, 4 * half:4 * half + 4, (t - 1) * P:t * P], 4, P)
            for half in range(2):
                to_hi(("ln2", NT - 1, half), act_hi[:, 4 * half:4 * half + 4, (NT - 1) * P:], 4, P)
            after(("wo", 1, NT - 1))

            for half in range(2):
                for f in range(UP_HALF):
                    key = ("up", half, f)
                    act.wait_ge(*dense_done.at(key))
                    if f >= 2 or half:
                        act.wait_ge(*sq_done.at((half, f - 2) if f >= 2 else (0, UP_HALF - 2 + f)))
                    act.activation(relu_b[:, f % 2, :], up_bank(half, f), ACT.Relu).then_inc(*relu_done.mark((half, f)))
                    after(key)
                    act.wait_ge(*sq_done.at((half, f)))
                    act.activation(a_hi[:, f, :], sq_b[:, f % 2, :], ACT.Copy).then_inc(*a_hi_done.mark((half, f)))
                for c in range(2):
                    for i in range(UP_HALF // 2):
                        after(("down", half, c, i))

        @block.vector
        def _(dve):
            def split_lo(n):
                m, width = SPLIT_AT[n], PIECES[n][2]
                dve.wait_ge(*hi_done.at(n))
                dve.tensor_tensor(w_lo[:, m % RING, 0:width], raw[:, n % RAW, 0:width],
                                  w_hi[:, m % RING, 0:width].bitcast(F32), ALU.subtract).then_inc(*lo_done.mark(n))

            def after(group):
                for n in SPLIT_AFTER.get(group, ()):
                    split_lo(n)

            def to_lo(key, dst, hi, cols):
                dve.wait_ge(*turn_hi.at(key))
                src = TD[bank_of("T", key)][:, 0:cols * P].rearrange("p (k s) -> p k s", k=cols)
                if key[0] == "mix":
                    src = backwards(src)
                dve.tensor_tensor(dst, src, hi.bitcast(F32), ALU.subtract).then_inc(*turn_lo.mark(key))

            def ln_rows(t, name, gain):
                dve.wait_ge(*rsqrt_done.at((name, t)))
                if t >= 2:
                    dve.wait_ge(*turned.at((name, t - 2, 1)))
                dve.scalar_tensor_tensor(ln_row[:, t % 2, :], x[:, t, :], rs_ln[:, t:t + 1], gain, ALU.mult, ALU.mult).then_inc(*scaled.mark((name, t)))

            def ln_lows(t, name):
                for half in range(2):
                    to_lo((name, t, half), act_lo[:, 4 * half:4 * half + 4, t * P:(t + 1) * P],
                          act_hi[:, 4 * half:4 * half + 4, t * P:(t + 1) * P], 4)

            dve.wait_ge(*gain1_in.at())
            for n in SPLITS[:2]:
                split_lo(n)
            ln_rows(0, "ln1", gain_ln1)
            ln_rows(1, "ln1", gain_ln1)
            split_lo(SPLITS[2])
            for t in range(NT):
                ln_lows(t, "ln1")
                if t + 2 < NT:
                    ln_rows(t + 2, "ln1", gain_ln1)
            for n in SPLITS[3:RING]:
                split_lo(n)
            for j in range(4):
                lo, hi = 512 * j, min(512 * (j + 1), VEC)
                dve.wait_ge(*turned.at(("vec", j)))
                dve.tensor_copy(bias_vec[:, lo:hi], TD[bank_of("T", ("vec", j))][0:8, 0:hi - lo]).then_inc(*dve_step.mark(f"vec{j}"))

            def latent_row(name, t):
                lo, hi, c = (0, Q_RANK, t) if name == "cq" else (Q_RANK, Q_RANK + KV_RANK, NT + t)
                dve.wait_ge(*rsqrt_done.at((name, t)))
                dve.wait_ge(*copied.at((name, t)))
                dve.scalar_tensor_tensor(c_row[:, t, lo:hi], c_row[:, t, lo:hi], rs_c[:, c:c + 1], gain_c[:, lo:hi],
                                         ALU.mult, ALU.mult).then_inc(*scaled.mark((name, t)))

            dve.wait_ge(*gainc_in.at())
            for t in range(NT):
                after(("cq", t))
                if t:
                    latent_row("cq", t - 1)
            latent_row("cq", NT - 1)
            for t in range(NT):
                after(("ckv", t))
                to_lo(("cq", t), c_lo[:, 0:3, t * P:(t + 1) * P], c_hi[:, 0:3, t * P:(t + 1) * P], 3)
                if t:
                    latent_row("ckv", t - 1)
            latent_row("ckv", NT - 1)
            def head_sums(name, t):
                n = QK if name == "uq" else NOPE
                if name == "uq":
                    to_lo(("ckv", t), c_lo[:, 3:5, t * P:(t + 1) * P], c_hi[:, 3:5, t * P:(t + 1) * P], 2)
                after((name, t, 0))
                dve.wait_ge(*squares.at((name, t, 1)))
                dve.tensor_reduce(ss_row[:, 8 * (t % 2):8 * (t % 2) + 8], qk_sq[:, 0:HEADS * n].rearrange("p (h n) -> p h n", h=HEADS),
                                  AX.X, ALU.add).then_inc(*summed.mark((name, t)))
                after((name, t, 1))

            def head_rows(name, t):
                n, tab = (QK, tab_q) if name == "uq" else (NOPE, tab_k)
                rs = rs_row[:, 8 * (t % 2):8 * (t % 2) + 8]
                row = qk_row[:, t % 2, :].rearrange("p (h n) -> p h n", h=HEADS)
                fin = qk_out.rearrange("p (h n) -> p h n", h=HEADS)
                dve.wait_ge(*rsqrt_done.at((name, t)))
                dve.wait_ge(*copied.at((name, t, 1)))
                if name == "ukv":
                    dve.wait_ge(*copied.at(("kr", t)))
                    dve.tensor_tensor(row[:, :, NOPE:], kr[:, t, :].unsqueeze(1).to_broadcast([P, HEADS, ROPE]),
                                      rs.unsqueeze(2).to_broadcast([P, HEADS, ROPE]), ALU.mult)
                dve.tensor_tensor(row[:, :, 0:n], row[:, :, 0:n], rs.unsqueeze(2).to_broadcast([P, HEADS, n]),
                                  ALU.mult).then_inc(*scaled.mark((name, t)))
                before = (name, t - 1) if t else ("uq", NT - 1) if name == "ukv" else None
                if before:
                    dve.wait_ge(*turned.at((*before, 1)))
                if t == 0:
                    dve.wait_ge(*pool_step.at("g_q" if name == "uq" else "g_k"))
                dve.wait_ge(*scaled.at((name, t)))
                dve.tensor_tensor(fin, row, tab[:, t, 0:QK].unsqueeze(1).to_broadcast([P, HEADS, QK]),
                                  ALU.mult).then_inc(*dve_step.mark(("gain", name, t)))

            head_sums(*QK_ROWS[0])
            for i, key in enumerate(QK_ROWS):
                if i + 1 < len(QK_ROWS):
                    head_sums(*QK_ROWS[i + 1])
                if i + 1 < len(QK_ROWS):
                    head_rows(*key)

            def low_unit(n):
                kind, t, h = UNITS[n]
                b, nk = n % 2, (t + 1) * P
                bank = S[n % 2]
                dve.wait_ge(*scores.at(n))
                if n >= 2:
                    dve.wait_ge(*probs.at(n - 2))
                if kind == "cmp":
                    s = s_buf[:, b, 0:256]
                    s3 = s.rearrange("p (h c) -> p h c", h=HEADS)
                    nm = neg_max[:, (8 * out_of(n)) % 16:(8 * out_of(n)) % 16 + 8]
                    dve.tensor_tensor(s.rearrange("p (g n) -> p g n", g=2), bank[:, 0:256].rearrange("p (g n) -> p g n", g=2),
                                      bias_c[:, t, :, :], ALU.add).then_inc(*dve_step.mark(("c0", t)))
                    dve.wait_ge(*dve_step.at(("c0", t)))
                    dve.tensor_reduce(nm, s3, AX.X, ALU.min).then_inc(*dve_step.mark(("c1", t)))
                    dve.wait_ge(*dve_step.at(("c1", t)))
                    dve.tensor_scalar(nm, nm, LEAST, None, ALU.min).then_inc(*dve_step.mark(("c2", t)))
                    dve.wait_ge(*dve_step.at(("c2", t)))
                    dve.tensor_tensor(s3, s3, nm.unsqueeze(2).to_broadcast([P, HEADS, NC]), ALU.subtract).then_inc(*lows.mark(n))
                    return
                m = (h + 8 * out_of(n)) % 16
                other = const("mask")[:, SEQ - nk:] if kind == "mla" else bias[:, h, SEQ - nk:]
                dve.tensor_tensor_reduce(s_buf[:, b, 0:nk], bank[:, 0:nk], other, 1.0, LEAST, ALU.add, ALU.min,
                                         neg_max[:, m:m + 1]).then_inc(*lows.mark(n))

            def pt_out(n):
                kind, t, h = UNITS[n]
                nk = 2 * P if kind == "cmp" else (t + 1) * P
                dve.wait_ge(*turned.at(("p", n)))
                if n >= 2:
                    dve.wait_ge(*mixed.at(n - 2))
                dve.tensor_copy(pt_buf[:, n % 2, 0:nk], TD[bank_of("T", ("p", n))][:, 0:nk]).then_inc(*dve_pt.mark(n))

            def out_row(kind, t):
                m = OUTS.index((kind, t))
                bank = O[m % 2].rearrange("p (h n) -> p h n", h=HEADS)
                d, r = den[:, 8 * (m % 4):8 * (m % 4) + 8], rden[:, 8 * (m % 4):8 * (m % 4) + 8]
                n = max(i for i, u in enumerate(UNITS) if u[0] == kind and u[1] == t)
                dve.wait_ge(*probs.at(n))
                if kind == "cmp":
                    dve.wait_ge(*dve_step.at(("den", t)))
                dve.tensor_scalar(d, d, 1e-30, None, ALU.max).then_inc(*dve_step.mark(("d1", kind, t)))
                dve.wait_ge(*dve_step.at(("d1", kind, t)))
                dve.reciprocal(r, d).then_inc(*dve_step.mark(("d2", kind, t)))
                dve.wait_ge(*dve_step.at(("d2", kind, t)))
                if kind != "mla":
                    j = ("cmp", "sel", "win").index(kind)
                    dve.tensor_tensor(r, r, gates[:, t, 8 * j:8 * j + 8], ALU.mult).then_inc(*dve_step.mark(("d3", kind, t)))
                    dve.wait_ge(*dve_step.at(("d3", kind, t)))
                rb = r.unsqueeze(2).to_broadcast([P, HEADS, HD])
                dve.wait_ge(*mixed.at(n))
                if kind == "mla":
                    dve.tensor_tensor(o_mla[:, t, :].rearrange("p (h n) -> p h n", h=HEADS), bank, rb, ALU.mult).then_inc(*o_used.mark((kind, t)))
                elif kind == "sel":
                    if t < 2:
                        dve.wait_ge(*mix_done.at((1, t + 2)))
                    dve.tensor_tensor(o_nsa[:, t % 2, :].rearrange("p (h n) -> p h n", h=HEADS), bank, rb, ALU.mult).then_inc(*o_used.mark((kind, t)))
                else:
                    i = PARTS.index((kind, t))
                    tmp = raw_row[:, i % 2, :]
                    if i >= 2 and PARTS[i - 2][1]:
                        dve.wait_ge(*o_summed.at(PARTS[i - 2]))
                    elif i >= 2:
                        dve.wait_ge(*o_used.at(PARTS[i - 2]))
                    dve.tensor_tensor(tmp.rearrange("p (h n) -> p h n", h=HEADS), bank, rb, ALU.mult).then_inc(*dve_step.mark(("o", kind, t)))
                    if t == 0:
                        dve.wait_ge(*dve_step.at(("o", kind, t)))
                        dve.wait_ge(*o_used.at(("sel" if kind == "win" else "win", t)))
                        dve.tensor_tensor(o_nsa[:, t % 2, :], o_nsa[:, t % 2, :], tmp, ALU.add).then_inc(*o_used.mark((kind, t)))

            def nsa_sum(key):
                b, t = key
                n = 8 if b == "nq" else 4
                dve.wait_ge(*squares.at(key))
                dve.tensor_reduce(ss_row[:, 8 * (t % 2):8 * (t % 2) + n], square[:, 0:n * HD].rearrange("p (h n) -> p h n", h=n),
                                  AX.X, ALU.add).then_inc(*summed.mark(key))

            def nsa_row(key):
                b, t = key
                j = t % 2
                n = 8 if b == "nq" else 4
                rs = rs_row[:, 8 * j:8 * j + n]
                row = raw_row[:, j, 0:n * HD].rearrange("p (h n) -> p h n", h=n)
                dve.wait_ge(*rsqrt_done.at(key))
                dve.wait_ge(*copied.at(key))
                dve.tensor_tensor(row, row, rs.unsqueeze(2).to_broadcast([P, n, HD]), ALU.mult).then_inc(*dve_step.mark(("nr", key)))
                dve.wait_ge(*dve_step.at(("nr", key)))
                before = (b, t - 2) if t >= 2 else ("nq", NT - 2 + t) if b == "nkv" else None
                if before:
                    dve.wait_ge(*turned.at(before))
                fin = o_nsa[:, j, :]
                if b == "nq":
                    gain = const("g_nq").unsqueeze(1).unsqueeze(1).to_broadcast([P, 2, 4, HD])
                    dve.tensor_tensor(fin.rearrange("p (r g n) -> p g r n", r=4, g=2), row.rearrange("p (g r) n -> p g r n", g=2),
                                      gain, ALU.mult).then_inc(*scaled.mark(key))
                else:
                    gain = const("g_nk")[:, HD:3 * HD].rearrange("p (b n) -> p b n", b=2).unsqueeze(2).to_broadcast([P, 2, 2, HD])
                    dve.tensor_tensor(fin[:, 0:256].rearrange("p (b g n) -> p b g n", b=2, g=2), row.rearrange("p (b g) n -> p b g n", b=2),
                                      gain, ALU.mult).then_inc(*scaled.mark(key))

            def nsa_turned(key):
                b, t = key
                k = 4 if b == "nq" else 2
                dve.wait_ge(*turned.at(key))
                dst = (n_q if b == "nq" else n_k)[:, :, t * P:(t + 1) * P]
                src = TD[bank_of("T", key)][:, 0:k * P].rearrange("p (k s) -> p k s", k=k)
                dve.tensor_copy(dst, backwards(src) if b == "nq" else src).then_inc(*dve_step.mark(("turned", key)))

            def gate_row(t):
                dve.wait_ge(*copied.at(("cmp", t)))
                g = gates[:, t, :]
                dve.tensor_scalar(g, g, 1.0, None, ALU.add).then_inc(*dve_step.mark(("g0", t)))
                dve.wait_ge(*dve_step.at(("g0", t)))
                dve.reciprocal(g, g).then_inc(*dve_step.mark(("g1", t)))

            dve.wait_ge(*pool_step.at("gnq"))
            for n in range(N_MLA):
                if n - 3 >= 0 and (n - 3) % 2 == 1:
                    pt_out(n - 3)
                low_unit(n)
                if n == 1:
                    head_rows(*QK_ROWS[-1])
                if n % 8 == 5 and n >= 8:
                    out_row("mla", n // 8 - 1)
                if n - 1 in ROW_END:
                    r = ROW_END.index(n - 1)
                    if ROWS[r][0] == "cmp":
                        gate_row(ROWS[r][1])
                    else:
                        nsa_sum(ROWS[r])
                if n - 3 in ROW_END[0:8]:
                    nsa_row(ROWS[ROW_END.index(n - 3)])
                if n - 5 in ROW_END[0:8]:
                    nsa_turned(ROWS[ROW_END.index(n - 5)])
                for m in SPLIT_AT_UNIT.get(n, ()):
                    split_lo(m)
            for n in range(N_MLA, N_MLA + 3):
                if (n - 3) % 2 == 1:
                    pt_out(n - 3)
            gate_row(NT - 1)
            out_row("mla", NT - 1)

            def low_taps(t):
                bank = TD[bank_of("T", ("taps", t))][:, 0:2 * P].rearrange("p (j s) -> p j s", j=2)
                lo = int(t == 0)
                for i in range(2):
                    dve.wait_ge(*copied.at(("taps", t, i)))
                    dve.tensor_copy(tap_planes[HD:P, 2 * i:2 * i + 2, t * P - 1 + lo:(t + 1) * P - 1],
                                    bank[HD * i:HD * i + HD, :, lo:]).then_inc(*dve_step.mark(("taps", t, i)))

            def mix_lows(g, t):
                at = (slice(None), slice(4 * g, 4 * g + 4), slice(t * P, (t + 1) * P))
                to_lo(("mix", g, t), act_lo[at], act_hi[at], 4)

            def compress(u):
                if 2 <= u < 2 + NT:
                    low_taps(u - 2)
                if u == 5:
                    dve.wait_ge(*turned.at("gt"))
                    dve.tensor_copy(gate_t.rearrange("p (t s) -> p t s", t=NT),
                                    backwards(TD[bank_of("T", "gt")][0:24, :].rearrange("p (t s) -> p t s", t=NT))).then_inc(*dve_step.mark("gt"))
                if u == 7:
                    dve.wait_ge(*turned.at("gates"))
                    dve.tensor_copy(gates, TD[bank_of("T", "gates")][:, 0:NT * 24].rearrange("p (t n) -> p t n", t=NT)).then_inc(*dve_step.mark("gates"))
                    dve.memset(v_diag, 0.0).then_inc(*dve_step.mark("vd0"))
                    dve.memset(hid_v, 0.0).then_inc(*dve_step.mark("hv0"))
                    dve.memset(hid_k, 0.0).then_inc(*dve_step.mark("hk0"))
                if u in (8, 9):
                    g = u - 8
                    dve.wait_ge(*turned.at(("bc", g)))
                    dve.tensor_copy(bias_c[:, :, g, :], TD[bank_of("T", ("bc", g))].rearrange("p (t n) -> p t n", t=NT)).then_inc(*dve_step.mark(("bc", g)))
                if u == 9:
                    dve.wait_ge(*turned.at(("bc", 1)))
                    dve.tensor_copy(tap_planes[:, 4:6, 0:CMP_BLOCK:2], const("pe").rearrange("p (kv l) -> p kv l", kv=2)).then_inc(*dve_step.mark("pe_rows"))
                if u in (14, 18):
                    kv = (u - 14) // 4
                    dve.wait_ge(*turned.at(("hid", kv)))
                    bank = TD[bank_of("T", ("hid", kv))]
                    dve.tensor_copy(pe_col[:, kv:kv + 1], bank[:, 2 * N_CMP:2 * N_CMP + 1]).then_inc(*dve_step.mark(("pe", kv)))
                    dve.wait_ge(*dve_step.at(("pe", kv)))
                    dve.tensor_scalar(z_buf[:, 0, kv, :], bank[:, 0:2 * N_CMP], pe_col[:, kv:kv + 1], None, ALU.add).then_inc(*dve_step.mark(("z", kv)))
                if u in (16, 20):
                    kv = (u - 16) // 4
                    dve.wait_ge(*exp_small.at(kv))
                    e = z_buf[:, 1, kv, :]
                    dve.tensor_scalar(e, e, 1.0, None, ALU.add).then_inc(*dve_step.mark(("e1", kv)))
                    dve.wait_ge(*dve_step.at(("e1", kv)))
                    dve.reciprocal(z_buf[:, 2, kv, :], e).then_inc(*dve_step.mark(("e2", kv)))
                    dve.wait_ge(*dve_step.at(("e2", kv)))
                    z = z_buf[:, 0, kv, :].rearrange("p (g c) -> p g c", g=2)
                    r = z_buf[:, 2, kv, :].rearrange("p (g c) -> p g c", g=2)
                    if kv == 0:
                        dve.tensor_tensor(hid_k.rearrange("p (g c) -> p g c", g=2)[:, :, 0:N_CMP], z, r, ALU.mult).then_inc(*dve_step.mark("hid_k"))
                    else:
                        for g in range(2):
                            rep = lambda v: v[:, g, :].unsqueeze(1).to_broadcast([P, 4, N_CMP])
                            dve.tensor_tensor(hid_v[:, g, :, 0:N_CMP], rep(z), rep(r), ALU.mult).then_inc(*dve_step.mark(("hid_v", g)))
                if u in (21, 23, 25, 27):
                    mix_lows(0, (u - 21) // 2)
                if u == 22:
                    dve.wait_ge(*turned.at("kc"))
                    bank = TD[bank_of("T", "kc")]
                    dve.tensor_copy(kc_row, bank[0:64, 0:HD]).then_inc(*dve_step.mark("kc0"))
                    dve.wait_ge(*dve_step.at("kc0"))
                    dve.tensor_tensor(kc_sq, kc_row, kc_row, ALU.mult).then_inc(*dve_step.mark("kc1"))
                    dve.wait_ge(*dve_step.at("kc1"))
                    dve.tensor_reduce(kc_ss[0:64, :], kc_sq, AX.X, ALU.add).then_inc(*dve_step.mark("kc_ss"))
                if u == 24:
                    dve.wait_ge(*turned.at("vc"))
                    bank = TD[bank_of("T", "vc")]
                    for h in range(4):
                        ps = slice(32 * h, 32 * h + 32)
                        dve.tensor_copy(v_diag[ps, :, HD * h:HD * h + HD], bank[ps, 0:2 * HD].rearrange("p (g n) -> p g n", g=2)).then_inc(*dve_step.mark(("vd", h)))
                if u == 26:
                    dve.wait_ge(*rsqrt_done.at("kc"))
                    dve.scalar_tensor_tensor(kc_sq, kc_row, kc_rs[0:64, :], const("g_nk", 64)[:, 0:HD], ALU.mult, ALU.mult).then_inc(*dve_step.mark("kc2"))
                if u == 28:
                    dve.wait_ge(*turned.at("kcT"))
                    bank = TD[bank_of("T", "kcT")]
                    dve.tensor_copy(k_cmp[0:64, :], bank[0:64, 0:NC]).then_inc(*dve_step.mark("k0"))
                    dve.tensor_copy(k_cmp[64:128, :], bank[0:64, NC:2 * NC]).then_inc(*dve_step.mark("k_cmp"))

            def residual(c, t):
                key = ("wo", c, t)
                dve.wait_ge(*dense_done.at(key))
                xs = x[:, t, 512 * c:512 * c + 512]
                dve.tensor_tensor(xs, D[bank_of("D", key)], xs, ALU.add).then_inc(*x2_done.mark((c, t)))

            last = len(UNITS)
            dve.wait_ge(*bias_in.at())
            for n in range(N_MLA, last + 5):
                if n - 3 >= N_MLA and n - 3 < last and (n - 3) % 2 == 1:
                    pt_out(n - 3)
                if n < last:
                    low_unit(n)
                compress(n - N_MLA)
                if n - 1 >= N_MLA and n - 1 < last and UNITS[n - 1][0] == "cmp":
                    t, m = UNITS[n - 1][1], out_of(n - 1)
                    dve.wait_ge(*probs.at(n - 1))
                    dve.tensor_reduce(den[:, 8 * (m % 4):8 * (m % 4) + 8], p_buf[:, (n - 1) % 2, 0:256].rearrange("p (h c) -> p h c", h=HEADS),
                                      AX.X, ALU.add).then_inc(*dve_step.mark(("den", t)))
                for m in SPLIT_AT_UNIT.get(n, ()):
                    split_lo(m)
                if n - N_MLA in WO_ADD:
                    residual(0, WO_ADD[n - N_MLA])
                done = n - 5
                if done >= N_MLA and done < last:
                    kind, t, h = UNITS[done]
                    if kind == "cmp" or h == HEADS - 1:
                        out_row(kind, t)
                done = n - 11
                if done >= N_MLA and done < last and UNITS[done][0] == "cmp":
                    mix_lows(1, UNITS[done][1])
            dve.wait_ge(*rsqrt_done.at(("mix", 1, 0)))
            dve.wait_ge(*turned.at(("mix", 1, 2)))
            dve.scalar_tensor_tensor(mix_row[:, 1, :], o_nsa[:, 0, :], rs_mix[:, NT:NT + 1], gain_grp[:, 512:1024],
                                     ALU.mult, ALU.mult).then_inc(*mixed_last.mark())
            mix_lows(1, 0)

            dve.wait_ge(*gain2_in.at())
            after(("wo", 0, 0))
            residual(0, 0)
            for t in range(NT):
                residual(1, t)
                if t < NT - 1:
                    after(("wo", 1, t))
                if t:
                    ln_rows(t - 1, "ln2", gain_ln2)
                if t >= 2:
                    ln_lows(t - 2, "ln2")
            ln_lows(NT - 2, "ln2")
            ln_rows(NT - 1, "ln2", gain_ln2)
            ln_lows(NT - 1, "ln2")
            after(("wo", 1, NT - 1))

            for half in range(2):
                for f in range(UP_HALF):
                    dve.wait_ge(*relu_done.at((half, f)))
                    if f >= 2 or half:
                        dve.wait_ge(*a_lo_done.at((half, f - 2) if f >= 2 else (0, UP_HALF - 2 + f)))
                    dve.tensor_tensor(sq_b[:, f % 2, :], relu_b[:, f % 2, :], relu_b[:, f % 2, :], ALU.mult).then_inc(*sq_done.mark((half, f)))
                    after(("up", half, f))
                    dve.wait_ge(*a_hi_done.at((half, f)))
                    dve.tensor_tensor(a_lo[:, f, :], sq_b[:, f % 2, :], a_hi[:, f, :].bitcast(F32), ALU.subtract).then_inc(*a_lo_done.mark((half, f)))
                for c in range(2):
                    for i in range(UP_HALF // 2):
                        after(("down", half, c, i))
                    for t in range(NT):
                        dve.wait_ge(*mixed.at(("down", half, c, t)))
                        xs = x[:, t, 512 * c:512 * c + 512]
                        if half:
                            dve.wait_ge(*x2_done.at(("part", c, t)))
                        done = y_done.mark((t, c)) if half else x2_done.mark(("part", c, t))
                        dve.tensor_tensor(xs, down_banks(half, c)[t], xs, ALU.add).then_inc(*done)

        @block.tensor
        def _(pe):
            bank_users = {"D": [], "T": []}

            def take(kind, key, freed_by):
                users = bank_users[kind]
                if len(users) >= 2:
                    sig, k = users[-2]
                    pe.wait_ge(*sig.at(k))
                known["bank", kind, key] = len(users) % 2
                users.append((sig_key := freed_by))
                return (D if kind == "D" else T)[(len(users) - 1) % 2]

            def three(dst, act_cols, n, w_cols, start, stop):
                a_h, a_l = act_cols
                w_h, w_l = w_cols
                pe.matmul(dst, a_h, w_h, start=start, stop=False)
                pe.matmul(dst, a_h, w_l, start=False, stop=False)
                return pe.matmul(dst, a_l, w_h, start=False, stop=stop)

            def piece(what, i):
                n = PIECE_AT[what, i]
                pe.wait_ge(*lo_done.at(n))
                m = SPLIT_AT[n] % RING
                return w_hi[:, m, :], w_lo[:, m, :]

            def used(ins, what, i):
                ins.then_inc(*piece_used.mark(PIECE_AT[what, i]))

            def turn(key, tiles, freed_by, kind="T", step=P):
                bank = take(kind, key, freed_by)
                if kind == "D":
                    known["bank", "T", key] = 2 + known["bank", "D", key]
                for i, tile in enumerate(tiles):
                    k, m = tile.shape
                    ins = pe.transpose(bank[0:m, i * step:i * step + k], tile, ident[0:k, 0:k])
                ins.then_inc(*turned.mark(key))

            def turn_ln(name, t):
                pe.wait_ge(*scaled.at((name, t)))
                for half in range(2):
                    turn((name, t, half), [ln_row[:, t % 2, (4 * half + k) * P:(4 * half + k + 1) * P] for k in range(4)],
                         (turn_lo, (name, t, half)))

            def project(block_, t, pieces=range(4)):
                n = BLOCK_COLS[block_]
                key = (block_, t)
                if pieces[0] == 0:
                    take("D", key, (copied, key))
                dst = D[known["bank", "D", key]][:, 0:n]
                if block_ == "cq":
                    pe.wait_ge(*turn_lo.at(("ln1", t, 1)))
                for i in pieces:
                    h, l = piece(block_, i)
                    for j in range(2):
                        k = 2 * i + j
                        ins = three(dst, (act_hi[:, k, t * P:(t + 1) * P], act_lo[:, k, t * P:(t + 1) * P]), n,
                                    (h[:, j * n:(j + 1) * n], l[:, j * n:(j + 1) * n]), k == 0, k == KD - 1)
                    if i < 3 and t == NT - 1:
                        used(ins, block_, i)
                if pieces[-1] == 3:
                    ins.then_inc(*dense_done.mark(key))

            def expand(name, t, c):
                k0, kn, w = (0, 3, 4 * QK) if name == "uq" else (3, 2, 4 * (NOPE + VD))
                key = (name, t, c)
                dst = take("D", key, (copied, key))[:, 0:w]
                pe.wait_ge(*turn_lo.at(("cq" if name == "uq" else "ckv", t)))
                for k in range(kn):
                    h, l = piece(name, k)
                    ins = three(dst, (c_hi[:, k0 + k, t * P:(t + 1) * P], c_lo[:, k0 + k, t * P:(t + 1) * P]), w,
                                (h[:, c * w:(c + 1) * w], l[:, c * w:(c + 1) * w]), k == 0, k == kn - 1)
                    if t == NT - 1 and c == 1 and k < kn - 1:
                        used(ins, name, k)
                ins.then_inc(*dense_done.mark(key))

            def turn_heads(name, t):
                pe.wait_ge(*roped.at((name, t)))
                for half in range(2):
                    turn((name, t, half), [qk_out[:, (4 * half + h) * QK:(4 * half + h + 1) * QK] for h in range(4)],
                         (copied, ("turned", (name, t, half))))

            pe.wait_ge(*consts_in.at())
            for t in range(NT):
                turn_ln("ln1", t)
            pe.wait_ge(*onehot_in.at("table"))
            for j in range(4):
                lo, hi = 512 * j, min(512 * (j + 1), VEC)
                bank = take("T", ("vec", j), (dve_step, f"vec{j}"))
                pe.matmul(bank[0:8, 0:hi - lo], const("rel", 33), onehot[:, lo:hi], start=True, stop=True).then_inc(*turned.mark(("vec", j)))
            for t in range(NT):
                project("cq", t)
            def turn_latent(name, t):
                lo, n = (0, 3) if name == "cq" else (Q_RANK, 2)
                pe.wait_ge(*scaled.at((name, t)))
                turn((name, t), [c_row[:, t, lo + k * P:lo + (k + 1) * P] for k in range(n)], (turn_lo, (name, t)))
            for t in range(NT):
                project("ckv", t)
                turn_latent("cq", t)
            for i in range(len(QK_ROWS)):
                if i < NT:
                    turn_latent("ckv", i)
                for c in range(2):
                    expand(*QK_ROWS[i], c)
                if i >= 2:
                    turn_heads(*QK_ROWS[i - 2])

            def score_unit(n):
                kind, t, h = UNITS[n]
                nk = (t + 1) * P
                bank = S[n % 2]
                if n >= 2:
                    pe.wait_ge(*(dve_step.at(("c0", UNITS[n - 2][1])) if UNITS[n - 2][0] == "cmp" else lows.at(n - 2)))
                if kind == "mla":
                    if h % 4 == 0:
                        pe.wait_ge(*copied.at(("turned", ("ukv", t, h // 4))))
                    ins = pe.matmul(bank[:, 0:nk], m_q[0:QK, t, h, :], m_k[0:QK, h, 0:nk], start=True, stop=True)
                elif kind == "cmp":
                    for h in range(HEADS):
                        ps = slice(64 * (h // 4), 64 * (h // 4) + 64)
                        if h == 4:
                            ins.then_inc(*half_scored.mark(n))
                            pe.wait_ge(*half_scored.at(n))
                        ins = pe.matmul(bank[:, NC * h:NC * h + NC], n_q[ps, h % 4, t * P:(t + 1) * P], k_cmp[ps, :], start=True, stop=True)
                else:
                    ps = slice(64 * (h // 4), 64 * (h // 4) + 64)
                    ins = pe.matmul(bank[:, 0:nk], n_q[ps, h % 4, t * P:(t + 1) * P], n_k[ps, int(kind == "win"), 0:nk], start=True, stop=True)
                ins.then_inc(*scores.mark(n))

            def turn_unit(n):
                kind, t, h = UNITS[n]
                pe.wait_ge(*probs.at(n))
                count = 2 if kind == "cmp" else t + 1
                turn(("p", n), [p_buf[:, n % 2, j * P:(j + 1) * P] for j in range(count)], (act_pt if n % 2 == 0 else dve_pt, n))

            def mix_unit(n):
                kind, t, h = UNITS[n]
                m = out_of(n)
                bank = O[m % 2]
                pe.wait_ge(*(act_pt if n % 2 == 0 else dve_pt).at(n))
                if m >= 2 and (h == 0 or kind == "cmp"):
                    k2, t2 = OUTS[m - 2]
                    pe.wait_ge(*(o_used.at((k2, t2)) if k2 in ("mla", "sel") else dve_step.at(("o", k2, t2))))
                if kind == "cmp":
                    for g in range(2):
                        ins = pe.matmul(bank[:, 256 * g:256 * g + 256], pt_buf[:, n % 2, g * P:(g + 1) * P], v_diag[:, g, :], start=True, stop=True)
                else:
                    for j in range(t + 1):
                        v = m_v[:, j, h * VD:(h + 1) * VD] if kind == "mla" else \
                            n_v[:, j, int(kind == "win"), HD * (h // 4):HD * (h // 4) + HD]
                        ins = pe.matmul(bank[:, 64 * h:64 * h + 64], pt_buf[:, n % 2, j * P:(j + 1) * P], v, start=j == 0, stop=j == t)
                ins.then_inc(*mixed.mark(n))

            def turn_nsa(key):
                b, t = key
                pe.wait_ge(*scaled.at(key))
                turn(key, [o_nsa[:, t % 2, k * P:(k + 1) * P] for k in range(4 if b == "nq" else 2)], (dve_step, ("turned", key)))

            for n in range(N_MLA + 4):
                if n < N_MLA:
                    score_unit(n)
                    for r, key in enumerate(ROWS):
                        here = [i for i in range(4) if unit_of(r, i) == n]
                        if here:
                            project(*key, here)
                if n in TURN_AT:
                    turn_heads(*TURN_AT[n])
                if n - 2 >= 0 and n - 2 < N_MLA:
                    turn_unit(n - 2)
                if n - 4 >= 0:
                    mix_unit(n - 4)
                if n - 4 in ROW_END[0:8]:
                    turn_nsa(ROWS[ROW_END.index(n - 4)])

            def turn_taps(t):
                turn(("taps", t), [raw_cmp[:, t, j * P:(j + 1) * P] for j in range(2)], (dve_step, ("taps", t, 1)), kind="D")

            def hidden(kv, quarter):
                if quarter == 0:
                    take("D", ("hid", kv), (dve_step, ("z", kv)))
                    known["bank", "T", ("hid", kv)] = 2 + known["bank", "D", ("hid", kv)]
                bank = TD[known["bank", "T", ("hid", kv)]]
                n = PIECE_AT["w1", 2 * kv + quarter // 2]
                pe.wait_ge(*raw_in[n % RAW].at(n))
                for i in range(4 * (quarter % 2), 4 * (quarter % 2) + 4):
                    lp = 8 * (quarter // 2) + i
                    w = raw[:, n % RAW, i * P:(i + 1) * P]
                    tok = tap_planes[:, kv:6:2, 2 * lp:2 * lp + CMP_STRIDE * (N_CMP - 1) + 1:CMP_STRIDE]
                    ins = pe.matmul(bank[:, 0:3 * N_CMP], w, tok, start=lp == 0, stop=lp == 15)
                if quarter == 1:
                    ins.then_inc(*taps_used.mark(n))
                if quarter == 3:
                    ins.then_inc(*turned.mark(("hid", kv)))

            def turn_mix(g, t):
                pe.wait_ge(*(mixed_last.at() if (g, t) == (1, 0) else mix_done.at((g, t))))
                turn(("mix", g, t), [mix_row[:, MIXES.index((g, t)) % 2, k * P:(k + 1) * P] for k in range(4)],
                     (turn_lo, ("mix", g, t)), kind="D")

            def compress(u):
                if u == 0:
                    pe.wait_ge(*copied.at(("cmp", NT - 1)))
                if u < NT:
                    turn_taps(u)
                if u == 4:
                    pe.wait_ge(*dve_step.at(("g1", NT - 1)))
                    turn("gt", [gates[:, t, :] for t in range(NT)], (dve_step, "gt"), kind="D")
                if u == 6:
                    pe.wait_ge(*dve_step.at("gt"))
                    turn("gates", [gate_t[:, t * P:(t + 1) * P] for t in range(NT)], (dve_step, "gates"), kind="D", step=24)
                if u in (7, 8):
                    g = u - 7
                    pe.wait_ge(*biasc_in.at(HEADS - 1))
                    turn(("bc", g), [bias_ct[:, g, t * P:(t + 1) * P] for t in reversed(range(NT))], (dve_step, ("bc", g)), kind="D")
                if u == 10:
                    pe.wait_ge(*dve_step.at("pe_rows"))
                if 10 <= u < 18:
                    hidden((u - 10) // 4, (u - 10) % 4)
                if u == 21:
                    pe.wait_ge(*dve_step.at("hid_k"))
                    bank = take("T", "kc", (dve_step, "kc0"))
                    pe.matmul(bank[0:64, 0:HD], hid_k, const("w2")[:, 0:HD], start=True, stop=True).then_inc(*turned.mark("kc"))
                if u == 23:
                    pe.wait_ge(*dve_step.at(("hid_v", 1)))
                    bank = take("T", "vc", (dve_step, ("vd", 3)))
                    for g in range(2):
                        ins = pe.matmul(bank[:, g * HD:(g + 1) * HD], hid_v[:, g, :, :].rearrange("p h c -> p (h c)"), const("w2")[:, HD:], start=True, stop=True)
                    ins.then_inc(*turned.mark("vc"))
                if u in (19, 21, 23, 25):
                    turn_mix(0, (u - 19) // 2)
                if u == 27:
                    pe.wait_ge(*dve_step.at("kc2"))
                    turn("kcT", [kc_sq], (dve_step, "k_cmp"))

            def project_out(c, t, pieces=range(4)):
                key = ("wo", c, t)
                if pieces[0] == 0:
                    take("D", key, (x2_done, (c, t)))
                    if c == 0:
                        pe.wait_ge(*turn_lo.at(("mix", 0, t)))
                        pe.wait_ge(*turn_lo.at(("mix", 1, t)))
                dst = D[known["bank", "D", key]]
                for i in pieces:
                    h, l = piece("wo", 4 * c + i)
                    for j in range(2):
                        k = 2 * i + j
                        ins = three(dst, (act_hi[:, k, t * P:(t + 1) * P], act_lo[:, k, t * P:(t + 1) * P]), 512,
                                    (h[:, j * 512:(j + 1) * 512], l[:, j * 512:(j + 1) * 512]), k == 0, k == KD - 1)
                    if i < 3 and key == last_user(PIECE_AT["wo", 4 * c]):
                        used(ins, "wo", 4 * c + i)
                if pieces[-1] == 3:
                    ins.then_inc(*dense_done.mark(key))

            last = len(UNITS)
            pe.wait_ge(*dve_step.at(("turned", ROWS[7])))
            for n in range(N_MLA, last + 10):
                if n < last:
                    if UNITS[n] == ("cmp", NT - 1, 0):
                        pe.wait_ge(*dve_step.at("k_cmp"))
                    score_unit(n)
                compress(n - N_MLA)
                if n - 2 >= N_MLA and n - 2 < last:
                    turn_unit(n - 2)
                if n - 4 >= N_MLA and n - 4 < last:
                    mix_unit(n - 4)
                if n - 9 >= N_MLA and n - 9 < last and UNITS[n - 9][0] == "cmp":
                    turn_mix(1, UNITS[n - 9][1])
                if n - N_MLA in WO_AT:
                    t, i = WO_AT[n - N_MLA]
                    project_out(0, t, [i])

            for c, t in WO[NT - 1:]:
                project_out(c, t)
                if c and t:
                    turn_ln("ln2", t - 1)
            turn_ln("ln2", NT - 1)

            for t in range(NT):
                pe.wait_ge(*turn_lo.at(("ln2", t, 1)))
            for half in range(2):
                for f in range(UP_HALF):
                    if f >= 4:
                        pe.wait_ge(*relu_done.at((half, f - 4)))
                    elif half:
                        pe.wait_ge(*x2_done.at(("part", 0, f)))
                    dst = up_bank(half, f)
                    h, l = piece(("up", half), f)
                    for k in range(KD):
                        ws = slice(k * P, (k + 1) * P)
                        pe.matmul(dst, h[:, ws], act_hi[:, k, :], start=k == 0, stop=False)
                        pe.matmul(dst, h[:, ws], act_lo[:, k, :], start=False, stop=False)
                        ins = pe.matmul(dst, l[:, ws], act_hi[:, k, :], start=False, stop=k == KD - 1)
                    ins.then_inc(*dense_done.mark(("up", half, f)))
                for c in range(2):
                    for i in range(UP_HALF // 2):
                        h, l = piece(("down", half, c), i)
                        for t in range(NT):
                            dst = down_banks(half, c)[t]
                            if i == 0 and (half or c):
                                if c == 1:
                                    pe.wait_ge(*relu_done.at((half, UP_HALF - 4 + t)))
                                else:
                                    pe.wait_ge(*x2_done.at(("part", 1, t)))
                            for j in range(2):
                                f = 2 * i + j
                                if t == 0:
                                    pe.wait_ge(*a_lo_done.at((half, f)))
                                ins = three(dst, (a_hi[:, f, t * P:(t + 1) * P], a_lo[:, f, t * P:(t + 1) * P]), 512,
                                            (h[:, j * 512:(j + 1) * 512], l[:, j * 512:(j + 1) * 512]), f == 0, f == UP_HALF - 1)
                            if i == UP_HALF // 2 - 1:
                                ins.then_inc(*mixed.mark(("down", half, c, t)))
                            elif t == NT - 1:
                                used(ins, ("down", half, c), i)


def t5_bucket(dist):
    n = np.maximum(dist, 0)
    exact = BUCKETS // 2
    large = np.log(np.maximum(n, 1).astype(np.float32) / np.float32(exact)) / np.float32(np.log(MAX_DIST / exact))
    large = np.minimum(exact + (large * np.float32(BUCKETS - exact)).astype(np.int32), BUCKETS - 1)
    return np.where(n < exact, n, large)


def shape_constants():
    p = np.arange(P)
    mask = np.where(SEQ - 1 - p[:, None] - np.arange(SEQ)[None, :] >= 0, 0.0, MASKED).astype(np.float32)
    half = ROPE // 2
    inv = (1.0 / (np.float32(10000.0) ** (np.arange(half, dtype=np.float32) / np.float32(half)))).astype(np.float32)
    angle = (np.arange(SEQ, dtype=np.float32)[:, None] * inv[None, :]).astype(np.float32)
    c, s = np.cos(angle), np.sin(angle)
    rope = np.concatenate([c, c, -s, s], axis=1).astype(np.float32).reshape(NT, P, 64).transpose(1, 0, 2)
    dist = np.concatenate([SEQ - 1 - np.arange(NEAR), FAR - 1 - np.arange(FAR) - FAR_LEAST])
    onehot = np.zeros((BUCKETS + 1, VEC), np.float32)
    onehot[t5_bucket(dist), np.arange(VEC)] = -1.0
    onehot[:, dist < 0] = 0.0
    onehot[BUCKETS, dist < 0] = 1.0
    return np.eye(P, dtype=np.float32), mask, rope.reshape(P, -1), onehot


def kernel(**inputs):
    import concourse.bacc as bacc
    from concourse.bass_utils import run_bass_kernel_spmd

    v = {k: np.asarray(x) for k, x in inputs.items()}
    rows = lambda *gs: np.ascontiguousarray(np.broadcast_to(np.concatenate([g.reshape(-1) for g in gs])[None, :], (P, sum(g.size for g in gs))))
    chunks = lambda w: w.reshape(-1, P, w.shape[1]).transpose(1, 0, 2)
    w_in, w_up, w_down, w_o = v["w_in"][0], v["w_up"][0], v["w_down"][0], v["w_o"][0]
    weights = np.zeros((len(PIECES), P, 1024), np.float32)
    for n, (what, i, width, _) in enumerate(PIECES):
        if what in IN_BLOCKS:
            block = np.concatenate([w_in[:, lo:lo + m] for lo, m in IN_BLOCKS[what]], axis=1)
            part = chunks(block[2 * i * P:2 * (i + 1) * P])
        elif what in ("uq", "ukv"):
            part = v["mla_w_" + what][0][i * P:(i + 1) * P]
        elif what == "w1":
            part = chunks(v["nsa_cmp_w1"][0, i // 2, 8 * P * (i % 2):8 * P * (i % 2 + 1)])
        elif what == "wo":
            part = chunks(w_o[2 * (i % 4) * P:2 * (i % 4 + 1) * P, 512 * (i // 4):512 * (i // 4 + 1)])
        elif what[0] == "up":
            f = what[1] * UP_HALF + i
            part = chunks(w_up[:, f * P:(f + 1) * P])
        else:
            f = what[1] * UP_HALF + 2 * i
            part = chunks(w_down[f * P:(f + 2) * P, 512 * what[2]:512 * (what[2] + 1)])
        weights[n, :, 0:width] = part.reshape(P, width)
    ident, mask, rope, onehot = shape_constants()
    pe = v["nsa_cmp_pe"][0].reshape(2, CMP_BLOCK // 2, P).transpose(2, 0, 1).reshape(P, -1)
    w2 = v["nsa_cmp_w2"][0].transpose(1, 0, 2).reshape(P, -1)
    consts = np.concatenate([ident, mask, rope, rows(v["mla_q_gain"]), rows(v["mla_k_gain"]), rows(v["nsa_q_gain"]),
                             rows(v["nsa_k_gain"]), pe, w2], axis=1)
    assert consts.shape[1] == CONST_LOADED
    arrays = {
        "x": v["x"][0], "weights": weights, "consts": consts, "onehot": onehot, "rel_bias": v["rel_bias"],
        "gain_ln1": rows(v["ln1_g"]), "gain_c": rows(v["mla_cq_norm_g"], v["mla_ckv_norm_g"]),
        "gain_grp": rows(v["grp_norm_mla"], v["grp_norm_nsa"]), "gain_ln2": rows(v["ln2_g"]),
    }
    arrays = {k: np.ascontiguousarray(x) for k, x in arrays.items()}

    known = {}
    for _ in range(2):
        nc = bacc.Bacc("TRN2", target_bir_lowering=False, num_devices=1)
        ins = {k: nc.dram_tensor(k, x.shape, mybir.dt.from_np(x.dtype), kind="ExternalInput").ap() for k, x in arrays.items()}
        out = nc.dram_tensor("y", (SEQ, D_MODEL), F32, kind="ExternalOutput").ap()
        build(nc, ins, out, known)
    r = run_bass_kernel_spmd(nc, [arrays], core_ids=[0])
    return np.asarray(r.results[0]["y"]).reshape(1, SEQ, D_MODEL)
```

```python
from contextlib import ExitStack

import concourse.bass as bass
import numpy as np
from concourse import mybir

F32 = mybir.dt.float32
F32R = mybir.dt.float32r
ALU = mybir.AluOpType
ACT = mybir.ActivationFunctionType
AX = mybir.AxisListType

P = 128
D_MODEL, SEQ, D_FF = 1024, 512, 4096
NT = SEQ // P
KD = D_MODEL // P
HEADS = 8
NOPE, ROPE, QK, VD = 64, 32, 96, 64
Q_RANK, KV_RANK = 384, 256
HD = 64
CMP_BLOCK, CMP_STRIDE, CMP_HIDDEN = 32, 16, 128
N_CMP = SEQ // CMP_STRIDE - 1
NC = 32
BUCKETS, MAX_DIST = 32, 128
EPS = 1e-6
MASKED = 1e30
LEAST = 1e29

_KV = Q_RANK + KV_RANK + ROPE + HEADS * HD
IN_BLOCKS = {
    "cq": [(0, Q_RANK)],
    "ckv": [(Q_RANK, KV_RANK + ROPE)],
    "nq": [(Q_RANK + KV_RANK + ROPE, HEADS * HD)],
    "nkv": [(_KV + 256, 512)],
    "cmp": [(_KV, 256), (_KV + 768, 24)],
}
BLOCK_COLS = {b: sum(n for _, n in cols) for b, cols in IN_BLOCKS.items()}
UP_HALF = D_FF // P // 2


RAW, RING = 3, 5


def weight_pieces():
    out = []

    def add(what, count, width, split=True, first=0):
        out.extend((what, i, width, split) for i in range(first, count))

    add("cq", 4, 2 * BLOCK_COLS["cq"])
    add("ckv", 4, 2 * BLOCK_COLS["ckv"])
    add("uq", Q_RANK // P, HEADS * QK)
    add("ukv", KV_RANK // P, HEADS * (NOPE + VD))
    add("nq", 4, 2 * BLOCK_COLS["nq"])
    add("nkv", 4, 2 * BLOCK_COLS["nkv"])
    add("cmp", 4, 2 * BLOCK_COLS["cmp"])
    add("wo", RING, 1024)
    add("w1", 4, 1024, False)
    add("wo", 8, 1024, first=RING)
    for half in range(2):
        add(("up", half), UP_HALF, 1024)
        for c in range(2):
            add(("down", half, c), UP_HALF // 2, 1024)
    return out


PIECES = weight_pieces()
PIECE_AT = {(what, i): n for n, (what, i, _, _) in enumerate(PIECES)}
SPLIT_AT = {n: m for m, n in enumerate(n for n, p in enumerate(PIECES) if p[3])}
SPLITS = list(SPLIT_AT)

NEAR = 640
FAR = SEQ + SEQ - CMP_STRIDE
FAR_LEAST = CMP_STRIDE * (NC - 1) + CMP_BLOCK - 1
VEC = NEAR + FAR


class Signal:

    def __init__(self, nc, ctx, name, known, step=1):
        self.sem = ctx.enter_context(nc.semaphore(name))
        self.name, self.known, self.step, self.count = name, known, step, 0

    def mark(self, key=0):
        self.count += self.step
        self.known[self.name, key] = self.count
        return self.sem, self.step

    def at(self, key=0):
        return self.sem, self.known.get((self.name, key), self.step)


UNITS = [("mla", t, h) for t in range(NT) for h in range(HEADS)]
N_MLA = len(UNITS)
for _b, _t in (("sel", 3), ("win", 3), ("sel", 2), ("win", 2), ("cmp", 3), ("sel", 1), ("cmp", 2), ("win", 1), ("cmp", 1),
               ("sel", 0), ("win", 0), ("cmp", 0)):
    UNITS += [(_b, _t, h) for h in range(1 if _b == "cmp" else HEADS)]
OUTS = list(dict.fromkeys(u[0:2] for u in UNITS))

QK_ROWS = [(b, t) for b in ("uq", "ukv") for t in range(NT)]
TURN_AT = {2: QK_ROWS[-2], 5: QK_ROWS[-1]}
PARTS = [o for o in OUTS if o[0] in ("win", "cmp")]
MIXES = [(0, t) for t in range(NT)] + [(1, t) for t in reversed(range(NT))]

WO_JOBS = [(g, t, c) for g, t in ((0, 0), (0, 1), (0, 2), (0, 3), (1, 3), (1, 2), (1, 1), (1, 0)) for c in range(2)]
WO_UNITS = [28, 28, 29, 29, 31, 31, 32, 32, 32, 33, 33, 34, 36, 37, 38, 41, 46, 47, 49, 52, 54, 56, 56, 57, 64, 68, 70, 72]
WO_AT = {}
for _n, _u in enumerate(WO_UNITS):
    WO_AT.setdefault(_u, []).append((*WO_JOBS[_n // 2], _n % 2))
LN2_AT = {3: (56, 60, 62), 2: (62, 68, 69)}
STARTED = 3
WO_LAST = {0: NT - 1, 1: 0}
WO_SPLIT = {0: 4, 1: 6, 2: 7, 3: 9, 4: 9, 5: 44, 6: 45, 7: 46}

ROWS = [(b, t) for b in ("nq", "nkv", "cmp") for t in range(NT)]


def unit_of(row, piece_):
    return 2 * (4 * row + piece_) // 3


ROW_END = [unit_of(r, 3) for r in range(len(ROWS))]

PAIR_KEYS = {ROW_END[8 + t] + 1: t for t in range(NT)}
PAIR_QUERIES = {25: 3, N_MLA + 13: 2, N_MLA + 23: 1, N_MLA + 43: 0}

DENSE = [("cq", t) for t in range(NT)] + [("ckv", t) for t in range(NT)]
DENSE += [("uq", t, c) for t in range(NT) for c in range(2)]
DENSE += [("ukv", t, c) for t in range(NT) for c in range(2)]
DENSE += [("nq", t) for t in range(NT)] + [("nkv", t) for t in range(NT)] + [("cmp", t) for t in range(NT)]
DENSE += [("wo", *job) for job in WO_JOBS]
for _h in range(2):
    DENSE += [("up", _h, f) for f in range(UP_HALF)]
    DENSE += [("down", _h, c, i) for c in range(2) for i in range(UP_HALF // 2)]


def last_user(piece):
    what, i, _, _ = PIECES[piece]
    if what in ("uq", "ukv"):
        return (what, NT - 1, 1)
    if what == "wo":
        return ("wo", i // 4, WO_LAST[i // 4], i // 2 % 2)
    if what[0] == "up":
        return (*what, i)
    if what[0] == "down":
        return (*what, i)
    return (what, NT - 1)


SPLIT_AFTER, SPLIT_AT_UNIT = {}, {}
_early = (("cq", NT - 1), ("ckv", NT - 1), ("uq", NT - 1, 1), ("ukv", NT - 1, 1))
for _m, _n in enumerate(SPLITS[RING:]):
    _g = last_user(SPLITS[_m])
    _what = PIECES[_n][0]
    if _what == "wo":
        SPLIT_AT_UNIT.setdefault(N_MLA + WO_SPLIT[PIECES[_n][1]], []).append(_n)
    elif _g == ("wo", 0, NT - 1, 1):
        SPLIT_AT_UNIT.setdefault(N_MLA + 58, []).append(_n)
    elif _g in (("nq", NT - 1), ("nkv", NT - 1)):
        SPLIT_AT_UNIT.setdefault(1 + unit_of(ROWS.index(_g), PIECES[SPLITS[_m]][1]), []).append(_n)
    elif _g in _early:
        SPLIT_AFTER.setdefault(DENSE[DENSE.index(_g) - 1], []).append(_n)
    else:
        SPLIT_AFTER.setdefault(_g, []).append(_n)


def out_of(n):
    return OUTS.index(UNITS[n][0:2])


CONST_AT, _at = {}, 0
for _name, _n in (("ident", P), ("mask", SEQ), ("rope", NT * 64), ("g_q", QK), ("g_k", QK), ("g_nq", HD), ("g_nk", 3 * HD),
                  ("pe", 2 * CMP_BLOCK // 2), ("w2", 2 * HD), ("rel", HEADS)):
    if _name == "rel":
        CONST_LOADED = _at
    CONST_AT[_name] = (_at, _n)
    _at += _n
CONST_COLS = _at


def build(nc, a, out, known):
    with ExitStack() as ctx:
        base = (nc.sbuf_base + 63) // 64 * 64
        top = [base]

        def place(name, cols, dt=F32, at=None, parts=P):
            off = top[0] if at is None else at
            if at is None:
                top[0] += cols * 4
            assert off + cols * 4 <= nc.sbuf_usable_end, (name, off)
            return nc.alloc_sbuf_tensor_at(name, [parts, cols], dt, offset=off)[:, :]

        def psum(name):
            return ctx.enter_context(nc.psum_tensor(name, [P, 512], F32))[:, :]

        def signal(name, step=1):
            return Signal(nc, ctx, name, known, step)

        x = place("x", NT * D_MODEL).rearrange("p (t d) -> p t d", t=NT)
        raw = place("raw", RAW * 1024).rearrange("p (s n) -> p s n", s=RAW)
        w_hi = place("w_hi", RING * 1024, F32R).rearrange("p (s n) -> p s n", s=RING)
        w_lo = place("w_lo", RING * 1024, F32R).rearrange("p (s n) -> p s n", s=RING)
        act_hi = place("act_hi", KD * SEQ, F32R).rearrange("p (k s) -> p k s", k=KD)
        act_lo = place("act_lo", KD * SEQ, F32R).rearrange("p (k s) -> p k s", k=KD)
        r_mla = top[0]
        m_q = place("m_q", NT * HEADS * P).rearrange("p (t h s) -> p t h s", t=NT, h=HEADS)
        m_k = place("m_k", HEADS * SEQ).rearrange("p (h s) -> p h s", h=HEADS)
        m_v = place("m_v", NT * HEADS * VD).rearrange("p (t n) -> p t n", t=NT)
        r_nsa = top[0]
        n_q = place("n_q", 4 * SEQ).rearrange("p (r s) -> p r s", r=4)
        r_nk = top[0]
        n_k = place("n_k", 2 * SEQ).rearrange("p (b s) -> p b s", b=2)
        n_v = place("n_v", NT * 2 * P).rearrange("p (t b n) -> p t b n", t=NT, b=2)
        r_bias = top[0]
        bias = place("bias", HEADS * SEQ).rearrange("p (h s) -> p h s", h=HEADS)
        r_bias_c = top[0]
        bias_c = place("bias_c", NT * 2 * P).rearrange("p (t g n) -> p t g n", t=NT, g=2)
        r_work = top[0]
        s_buf = place("s_buf", 2 * 512).rearrange("p (b n) -> p b n", b=2)
        p_buf = place("p_buf", 2 * 512).rearrange("p (b n) -> p b n", b=2)
        pt_buf = place("pt_buf", 2 * 512).rearrange("p (b n) -> p b n", b=2)
        r_temp = top[0]
        raw_all = place("raw_row", 2 * 512)
        raw_row = raw_all.rearrange("p (b n) -> p b n", b=2)
        raw_cmp = raw_all.rearrange("p (t n) -> p t n", t=NT)
        square = place("square", 512)
        r_onsa = top[0]
        o_nsa = place("o_nsa", 2 * 512).rearrange("p (b n) -> p b n", b=2)
        r_mask = top[0] + 4 * CONST_AT["mask"][0]
        consts = place("consts", CONST_COLS)
        kr = place("kr", NT * ROPE).rearrange("p (t n) -> p t n", t=NT)
        gates = place("gates", NT * 24).rearrange("p (t n) -> p t n", t=NT)
        stats = place("stats", 384)
        tab_q = place("tab_q", NT * 128, at=r_onsa).rearrange("p (t n) -> p t n", t=NT)
        tab_k = place("tab_k", NT * 128, at=r_onsa + 2048).rearrange("p (t n) -> p t n", t=NT)
        o_mla = place("o_mla", NT * 512, at=r_mla).rearrange("p (t n) -> p t n", t=NT)
        gain_ln1 = place("gain_ln1", D_MODEL, at=r_mla)
        c_row = place("c_row", NT * (Q_RANK + KV_RANK), at=r_mla + 4096).rearrange("p (t n) -> p t n", t=NT)
        r_mk = r_mla + NT * HEADS * P * 4
        gain_c = place("gain_c", Q_RANK + KV_RANK, at=r_mk)
        onehot = place("onehot", VEC, at=r_mk + 2560, parts=33)
        bias_vec = place("bias_vec", VEC, at=r_mk + 2560 + VEC * 4, parts=8)
        c_hi = place("c_hi", 5 * SEQ, F32R, at=r_bias).rearrange("p (k s) -> p k s", k=5)
        c_lo = place("c_lo", 5 * SEQ, F32R, at=r_bias + 5 * SEQ * 4).rearrange("p (k s) -> p k s", k=5)
        ln_row = place("ln_row", 2 * D_MODEL, at=r_work).rearrange("p (b n) -> p b n", b=2)
        ln_sq = place("ln_sq", D_MODEL, at=r_work + 8192)
        ln2_row = place("ln2_row", 2 * D_MODEL, at=r_mk).rearrange("p (b n) -> p b n", b=2)
        ln2_sq = place("ln2_sq", D_MODEL, at=r_mk + 8192)
        qk_row = place("qk_row", 2 * HEADS * QK, at=r_nsa).rearrange("p (b n) -> p b n", b=2)
        qk_out = place("qk_out", HEADS * QK, at=r_nsa + 6144)
        qk_sq = place("qk_sq", HEADS * QK, at=r_nsa + 9216)
        rope_t = place("rope_t", HEADS * ROPE, at=r_temp)
        tap_planes = place("tap_planes", 6 * SEQ, at=r_mk).rearrange("p (j s) -> p j s", j=6)
        bias_ct = tap_planes[:, 4:6, :]
        v_diag = place("v_diag", 2 * 256, at=r_mk + 12288).rearrange("p (g n) -> p g n", g=2)
        hid_v = place("hid_v", 2 * P, at=r_mk + 14336).rearrange("p (g h c) -> p g h c", g=2, h=4)
        k_cmp = place("k_cmp", NC, at=r_mk + 15360)
        hid_k = place("hid_k", 2 * NC, at=r_mk + 15488)
        kc_row = place("kc_row", HD, at=r_mk + 15744, parts=64)
        kc_sq = place("kc_sq", HD, at=r_mk + 16000, parts=64)
        r_mv = r_mk + 16384
        gain_grp = place("gain_grp", D_MODEL, at=r_mv)
        gain_ln2 = place("gain_ln2", D_MODEL, at=r_nk)
        q_pairs = [place(f"q_pairs{i}", HEADS * P, F32R, at=r).rearrange("p (h s) -> p h s", h=HEADS)
                   for i, r in enumerate((r_mv + 4096, r_mla + 8192))]
        mix_row = place("mix_row", 2 * 512, at=r_mla + 12288).rearrange("p (b n) -> p b n", b=2)
        gate_t = place("gate_t", SEQ, at=r_bias_c, parts=24)
        z_buf = place("z_buf", 3 * 2 * 2 * N_CMP, at=r_mask).rearrange("p (a b n) -> p a b n", a=3, b=2)
        a_hi = place("a_hi", UP_HALF * SEQ, F32R, at=r_mla).rearrange("p (f s) -> p f s", f=UP_HALF)
        a_lo = place("a_lo", UP_HALF * SEQ, F32R, at=r_mla + UP_HALF * SEQ * 4).rearrange("p (f s) -> p f s", f=UP_HALF)
        relu_b = place("relu_b", 2 * 512, at=r_work).rearrange("p (b n) -> p b n", b=2)
        sq_b = place("sq_b", 2 * 512, at=r_work + 4096).rearrange("p (b n) -> p b n", b=2)

        def const(name, parts=P):
            at, n = CONST_AT[name]
            return consts[0:parts, at:at + n]

        ident = const("ident")
        rope = const("rope").rearrange("p (t n) -> p t n", t=NT)
        stat_at = [0]

        def stat(n):
            stat_at[0] += n
            assert stat_at[0] <= 384
            return stats[:, stat_at[0] - n:stat_at[0]]

        ss_ln, rs_ln = stat(NT), stat(NT)
        ss_c, rs_c, ss_kr = stat(2 * NT), stat(2 * NT), stat(NT)
        ss_row, rs_row = stat(16), stat(16)
        neg_max = stat(8 * 2)
        den, rden = stat(8 * 4), stat(8 * 4)
        half_neg = stat(8)
        ss_mix, rs_mix = stat(2 * NT), stat(2 * NT)
        pe_col, kc_ss, kc_rs = stat(2), stat(1), stat(1)

        banks = [psum(f"bank{i}") for i in range(8)]
        D, T, S, O = banks[0:2], banks[2:4], banks[4:6], banks[6:8]
        TD = T + D

        x_in = [signal(f"x_in{t}", 16) for t in range(NT)]
        raw_in = [signal(f"raw_in{s}", 16) for s in range(RAW)]
        ident_in = signal("ident_in", 16)
        consts_in, gain1_in, gainc_in = signal("consts_in", 16), signal("gain1_in", 16), signal("gainc_in", 16)
        onehot_in, vec_out = signal("onehot_in", 16), signal("vec_out", 16)
        bias_in, biasc_in = signal("bias_in", 16), signal("biasc_in", 16)
        gaing_in, gain2_in, y_out = signal("gaing_in", 16), signal("gain2_in", 16), signal("y_out", 16)
        hi_done, lo_done = signal("hi_done"), signal("lo_done")
        piece_used, taps_used = signal("piece_used"), signal("taps_used")
        dense_done, turned = signal("dense_done"), signal("turned")
        scores, half_scored, mixed = signal("scores"), signal("half_scored"), signal("mixed")
        pair_hi, pair_lo = signal("pair_hi"), signal("pair_lo")
        squares, copied, turn_hi = signal("squares"), signal("copied"), signal("turn_hi")
        probs, relu_done, a_hi_done = signal("probs"), signal("relu_done"), signal("a_hi_done")
        act_pt, exp_small = signal("act_pt"), signal("exp_small")
        summed, scaled, turn_lo = signal("summed"), signal("scaled"), signal("turn_lo")
        lows, dve_pt, o_used = signal("lows"), signal("dve_pt"), signal("o_used")
        mixed_last = signal("mixed_last")
        dve_step, x2_done, sq_done, a_lo_done = signal("dve_step"), signal("x2_done"), signal("sq_done"), signal("a_lo_done")
        y_done = signal("y_done")
        rsqrt_done, pool_step, roped = signal("rsqrt_done"), signal("pool_step"), signal("roped")
        o_summed, mix_done = signal("o_summed"), signal("mix_done")

        vec_dram = nc.dram_tensor("bias_by_distance", [HEADS, VEC], F32, kind="Internal").ap()

        def bank_of(kind, key):
            return known.get(("bank", kind, key), 0)

        def raw_free(n):
            what, i, _, split = PIECES[n]
            if split:
                return lo_done.at(n)
            return turned.at(("hid", i // 2)) if i % 2 else taps_used.at(n)

        def used_by(n):
            what, i, _, _ = PIECES[n]
            last = {"uq": Q_RANK // P, "ukv": KV_RANK // P, "wo": 2}.get(what, 4)
            if what[0] == "up":
                return dense_done.at((*what, i))
            if what[0] == "down":
                return mixed.at((*what, NT - 1)) if i == UP_HALF // 2 - 1 else piece_used.at(n)
            if i % last < last - 1:
                return piece_used.at(n)
            return dense_done.at(last_user(n))

        def up_bank(half, f):
            return ((S + O) if half == 0 else (D + T))[f % 4]

        def down_banks(half, c):
            return (D + T) if (half + c) % 2 == 0 else (S + O)

        def backwards(tiles):
            return tiles[:, :, ::-1]

        block = ctx.enter_context(nc.Block())

        @block.sync
        def _(sp):
            def load_x(t):
                sp.dma_start(x[:, t, :], a["x"][t * P:(t + 1) * P, :]).then_inc(*x_in[t].mark())

            load_x(0)
            load_x(1)
            for n, (what, i, width, split) in enumerate(PIECES):
                if n in (1, 2):
                    load_x(n + 1)
                if n >= RAW:
                    sp.wait_ge(*raw_free(n - RAW))
                sp.dma_start(raw[:, n % RAW, 0:width], a["weights"][n, :, 0:width]).then_inc(*raw_in[n % RAW].mark(n))
            for t in range(NT):
                for c in range(2):
                    sp.wait_ge(*y_done.at((t, c)))
                    sp.dma_start(out[t * P:(t + 1) * P, c * 512:(c + 1) * 512],
                                 x[:, t, c * 512:(c + 1) * 512]).then_inc(*y_out.mark((t, c)))
            sp.wait_ge(*y_out.at((NT - 1, 1)))

        @block.gpsimd
        def _(pool):
            pool.memset(half_neg, -0.5).then_inc(*pool_step.mark("half"))
            pool.memset(consts[0:33, CONST_AT["rel"][0]:CONST_AT["rel"][0] + 8], MASKED).then_inc(*pool_step.mark("rel0"))
            pool.wait_ge(*pool_step.at("rel0"))
            pool.dma_start(const("rel", 32), a["rel_bias"]).then_inc(*onehot_in.mark("rel"))
            pool.dma_start(onehot, a["onehot"]).then_inc(*onehot_in.mark("table"))
            def rsqrt(key, out_, in_, width, after=None):
                pool.tensor_scalar(in_, in_, 1.0 / width, EPS, ALU.mult, ALU.add).then_inc(*pool_step.mark(("ms", key)))
                pool.wait_ge(*pool_step.at(("ms", key)))
                n = in_.shape[1]
                pool.tensor_tensor(out_, in_, half_neg[0:in_.shape[0], 0:n], ALU.pow).then_inc(*rsqrt_done.mark(key))

            pool.wait_ge(*pool_step.at("half"))
            for t in range(NT):
                pool.wait_ge(*squares.at(("ln1", t)))
                rsqrt(("ln1", t), rs_ln[:, t:t + 1], ss_ln[:, t:t + 1], D_MODEL)
            pool.wait_ge(*consts_in.at())
            pool.tensor_scalar(const("g_q"), const("g_q"), -float(QK) ** -0.5, 1.0, ALU.mult, ALU.mult).then_inc(*pool_step.mark("gq"))
            pool.tensor_scalar(const("g_nq"), const("g_nq"), -float(HD) ** -0.5, 1.0, ALU.mult, ALU.mult).then_inc(*pool_step.mark("gnq"))
            pool.wait_ge(*pool_step.at("gq"))
            for name, tab in (("g_q", tab_q), ("g_k", tab_k)):
                g = const(name)
                for n, lo, hi in ((0, 0, NOPE), (NOPE, NOPE, QK), (QK, NOPE + 16, QK), (QK + 16, NOPE, NOPE + 16)):
                    w = hi - lo
                    gain = g[:, lo:hi].unsqueeze(1).to_broadcast([P, NT, w])
                    if n == 0:
                        ins = pool.tensor_scalar(tab[:, :, 0:w], gain, 1.0, 1.0, ALU.mult, ALU.mult)
                    else:
                        ins = pool.tensor_tensor(tab[:, :, n:n + w], gain, rope[:, :, n - NOPE:n - NOPE + w], ALU.mult)
                ins.then_inc(*pool_step.mark(name))

            pool.wait_ge(*dve_step.at("vec3"))
            pool.dma_start(vec_dram, bias_vec).then_inc(*vec_out.mark())
            for c, (b, width) in enumerate((("cq", Q_RANK), ("ckv", KV_RANK))):
                for t in range(NT):
                    pool.wait_ge(*squares.at((b, t)))
                    rsqrt((b, t), rs_c[:, c * NT + t:c * NT + t + 1], ss_c[:, c * NT + t:c * NT + t + 1], width)

            def head_rsqrt(name, t):
                b = t % 2
                ss, rs = ss_row[:, 8 * b:8 * b + 8], rs_row[:, 8 * b:8 * b + 8]
                pool.wait_ge(*summed.at((name, t)))
                if name == "ukv":
                    pool.tensor_scalar(ss, ss, ss_kr[:, t:t + 1], 1.0, ALU.add, ALU.mult).then_inc(*pool_step.mark(("kr", t)))
                    pool.wait_ge(*pool_step.at(("kr", t)))
                rsqrt((name, t), rs, ss, QK)

            def rotate(name, t):
                tab = tab_q if name == "uq" else tab_k
                row = qk_row[:, t % 2, :].rearrange("p (h n) -> p h n", h=HEADS)
                fin = qk_out.rearrange("p (h n) -> p h n", h=HEADS)
                tmp = rope_t.rearrange("p (h n) -> p h n", h=HEADS)
                i = QK_ROWS.index((name, t))
                if i:
                    pool.wait_ge(*roped.at(QK_ROWS[i - 1]))
                pool.wait_ge(*scaled.at((name, t)))
                for lo, src in ((0, NOPE + 16), (16, NOPE)):
                    sin = tab[:, t, QK + lo:QK + lo + 16].unsqueeze(1).to_broadcast([P, HEADS, 16])
                    ins = pool.tensor_tensor(tmp[:, :, lo:lo + 16], row[:, :, src:src + 16], sin, ALU.mult)
                ins.then_inc(*pool_step.mark(("rot", name, t)))
                pool.wait_ge(*pool_step.at(("rot", name, t)))
                pool.wait_ge(*dve_step.at(("gain", name, t)))
                pool.tensor_tensor(fin[:, :, NOPE:QK], fin[:, :, NOPE:QK], tmp, ALU.add).then_inc(*roped.mark((name, t)))

            head_rsqrt(*QK_ROWS[0])
            for i, key in enumerate(QK_ROWS):
                if i + 1 < len(QK_ROWS):
                    head_rsqrt(*QK_ROWS[i + 1])
                rotate(*key)

            pool.wait_ge(*vec_out.at())
            pool.wait_ge(*dense_done.at(("ukv", NT - 1, 1)))
            pool.dma_start(bias, bass.AP(vec_dram.tensor, 0, [[1, P], [VEC, HEADS], [1, SEQ]])).then_inc(*bias_in.mark())

            for b in ("nq", "nkv"):
                for t in range(NT):
                    j = t % 2
                    n = 8 if b == "nq" else 4
                    pool.wait_ge(*summed.at((b, t)))
                    rsqrt((b, t), rs_row[:, 8 * j:8 * j + n], ss_row[:, 8 * j:8 * j + n], HD)

            pool.wait_ge(*mixed.at(N_MLA - 1))
            for h in range(HEADS):
                pool.dma_start(bias_ct[32 * (h % 4):32 * (h % 4) + 32, h // 4, :],
                               bass.AP(vec_dram.tensor, h * VEC + NEAR, [[CMP_STRIDE, NC], [1, SEQ]])
                               ).then_inc(*biasc_in.mark(h))
            pool.dma_start(gain_grp, a["gain_grp"]).then_inc(*gaing_in.mark())

            def mix_row_of(g, t):
                pool.wait_ge(*squares.at(("mix", g, t)))
                at = g * NT + t
                rsqrt(("mix", g, t), rs_mix[:, at:at + 1], ss_mix[:, at:at + 1], 512)
                i = MIXES.index((g, t))
                if (g, t) == (1, 0):
                    return
                if i >= 2:
                    pool.wait_ge(*turned.at(("mix", *MIXES[i - 2])))
                pool.wait_ge(*rsqrt_done.at(("mix", g, t)))
                src = o_mla[:, t, :] if g == 0 else o_nsa[:, t % 2, :]
                pool.tensor_scalar(mix_row[:, i % 2, :], src, rs_mix[:, at:at + 1], 1.0, ALU.mult, ALU.mult).then_inc(*pool_step.mark(("scaled", g, t)))
                pool.wait_ge(*pool_step.at(("scaled", g, t)))
                pool.tensor_tensor(mix_row[:, i % 2, :], mix_row[:, i % 2, :], gain_grp[:, 512 * g:512 * g + 512], ALU.mult).then_inc(*mix_done.mark((g, t)))

            def sum_branches(kind, t):
                if kind == "cmp":
                    pool.wait_ge(*o_summed.at(("win", t)))
                pool.wait_ge(*dve_step.at(("o", kind, t)))
                pool.tensor_tensor(o_nsa[:, t % 2, :], o_nsa[:, t % 2, :], raw_row[:, PARTS.index((kind, t)) % 2, :], ALU.add).then_inc(*o_summed.mark((kind, t)))

            pool.wait_ge(*pair_lo.at(("k", NT - 1)))
            pool.dma_start(gain_ln2, a["gain_ln2"]).then_inc(*gain2_in.mark())
            pool.wait_ge(*gaing_in.at())
            for t in range(NT):
                mix_row_of(0, t)
            sum_branches("win", 3)
            pool.wait_ge(*dve_step.at("kc_ss"))
            rsqrt("kc", kc_rs[0:64, :], kc_ss[0:64, :], HD)
            sum_branches("win", 2)
            for t in (3, 2):
                sum_branches("cmp", t)
                mix_row_of(1, t)
            for kind in ("win", "cmp"):
                sum_branches(kind, 1)
            def ln2_rsqrt(t):
                pool.wait_ge(*squares.at(("ln2", t)))
                rsqrt(("ln2", t), rs_ln[:, t:t + 1], ss_ln[:, t:t + 1], D_MODEL)

            mix_row_of(1, 1)
            ln2_rsqrt(3)
            ln2_rsqrt(2)
            mix_row_of(1, 0)
            ln2_rsqrt(1)
            ln2_rsqrt(0)

        @block.scalar
        def _(act):
            act.dma_start(gain_ln1, a["gain_ln1"]).then_inc(*gain1_in.mark())
            act.dma_start(ident, a["consts"][:, 0:P]).then_inc(*ident_in.mark())

            def split_hi(n):
                m, width = SPLIT_AT[n], PIECES[n][2]
                act.wait_ge(*raw_in[n % RAW].at(n))
                if m >= RING:
                    act.wait_ge(*used_by(SPLITS[m - RING]))
                act.activation(w_hi[:, m % RING, 0:width], raw[:, n % RAW, 0:width], ACT.Copy).then_inc(*hi_done.mark(n))

            def after(group):
                for n in SPLIT_AFTER.get(group, ()):
                    split_hi(n)

            def to_hi(key, dst, cols, width):
                act.wait_ge(*turned.at(key))
                src = TD[bank_of("T", key)][:, 0:cols * width].rearrange("p (k s) -> p k s", k=cols)
                if key[0] == "mix":
                    src = backwards(src)
                act.activation(dst, src, ACT.Copy).then_inc(*turn_hi.mark(key))

            def ln1_square(t):
                act.wait_ge(*x_in[t].at())
                if t:
                    act.wait_ge(*squares.at(("ln1", t - 1)))
                act.activation(ln_sq, x[:, t, :], ACT.Square, accum_out=ss_ln[:, t:t + 1]).then_inc(*squares.mark(("ln1", t)))

            def ln1_his(t):
                for half in range(2):
                    to_hi(("ln1", t, half), act_hi[:, 4 * half:4 * half + 4, t * P:(t + 1) * P], 4, P)

            ln1_square(0)
            ln1_square(1)
            act.dma_start(consts[:, P:CONST_LOADED], a["consts"][:, P:]).then_inc(*consts_in.mark())
            act.dma_start(gain_c, a["gain_c"]).then_inc(*gainc_in.mark())
            split_hi(SPLITS[0])
            split_hi(SPLITS[1])
            ln1_his(0)
            ln1_square(2)
            split_hi(SPLITS[2])
            ln1_his(1)
            split_hi(SPLITS[3])
            ln1_square(3)
            ln1_his(2)
            ln1_his(3)
            split_hi(SPLITS[4])

            for t in range(NT):
                key = ("cq", t)
                act.wait_ge(*dense_done.at(key))
                bank = D[bank_of("D", key)]
                if t:
                    act.wait_ge(*squares.at(("cq", t - 1)))
                act.activation(square[:, 0:Q_RANK], bank[:, 0:Q_RANK], ACT.Square, accum_out=ss_c[:, t:t + 1]).then_inc(*squares.mark(key))
                act.activation(c_row[:, t, 0:Q_RANK], bank[:, 0:Q_RANK], ACT.Copy).then_inc(*copied.mark(key))
                after(key)
            for t in range(NT):
                key = ("ckv", t)
                act.wait_ge(*dense_done.at(key))
                bank = D[bank_of("D", key)]
                act.wait_ge(*squares.at(("ckv", t - 1) if t else ("cq", NT - 1)))
                act.activation(square[:, KV_RANK:KV_RANK + ROPE], bank[:, KV_RANK:KV_RANK + ROPE], ACT.Square, accum_out=ss_kr[:, t:t + 1]).then_inc(*squares.mark(("kr", t)))
                act.activation(square[:, 0:KV_RANK], bank[:, 0:KV_RANK], ACT.Square, accum_out=ss_c[:, NT + t:NT + t + 1]).then_inc(*squares.mark(key))
                act.activation(kr[:, t, :], bank[:, KV_RANK:KV_RANK + ROPE], ACT.Copy).then_inc(*copied.mark(("kr", t)))
                act.activation(c_row[:, t, Q_RANK:], bank[:, 0:KV_RANK], ACT.Copy).then_inc(*copied.mark(key))
                after(key)
                to_hi(("cq", t), c_hi[:, 0:3, t * P:(t + 1) * P], 3, P)

            def turned_out(name, t, half):
                key = (name, t, half)
                act.wait_ge(*turned.at(key))
                src = TD[bank_of("T", key)][0:QK, :].rearrange("p (h s) -> p h s", h=4)
                if name == "uq":
                    src = backwards(src)
                dst = m_q[0:QK, t, 4 * half:4 * half + 4, :] if name == "uq" else m_k[0:QK, 4 * half:4 * half + 4, t * P:(t + 1) * P]
                act.activation(dst, src, ACT.Copy).then_inc(*copied.mark(("turned", key)))

            for i, (name, t) in enumerate(QK_ROWS):
                n, w = (QK, QK) if name == "uq" else (NOPE, NOPE + VD)
                row = qk_row[:, t % 2, :].rearrange("p (h n) -> p h n", h=HEADS)
                sq = qk_sq[:, 0:HEADS * n].rearrange("p (h n) -> p h n", h=HEADS)
                src = [D[bank_of("D", (name, t, c))][:, 0:4 * w].rearrange("p (h n) -> p h n", h=4) for c in range(2)]
                if (name, t) == ("ukv", 1):
                    act.wait_ge(*vec_out.at())
                if i >= 3:
                    for half in range(2):
                        turned_out(*QK_ROWS[i - 3], half)
                if name == "uq":
                    to_hi(("ckv", t), c_hi[:, 3:5, t * P:(t + 1) * P], 2, P)
                for c in range(2):
                    act.wait_ge(*dense_done.at((name, t, c)))
                    if i:
                        act.wait_ge(*summed.at(QK_ROWS[i - 1]))
                    act.activation(sq[:, 4 * c:4 * c + 4, :], src[c][:, :, 0:n], ACT.Square).then_inc(*squares.mark((name, t, c)))
                for c in range(2):
                    if i >= 2:
                        act.wait_ge(*roped.at(QK_ROWS[i - 2]))
                    if name == "ukv":
                        act.activation(m_v[:, t, 4 * c * VD:(4 * c + 4) * VD].rearrange("p (h n) -> p h n", h=4),
                                       src[c][:, :, NOPE:], ACT.Copy).then_inc(*copied.mark(("v", t, c)))
                    act.activation(row[:, 4 * c:4 * c + 4, 0:n], src[c][:, :, 0:n], ACT.Copy).then_inc(*copied.mark((name, t, c)))
                    after((name, t, c))
            for half in range(2):
                turned_out(*QK_ROWS[-3], half)

            def exp_unit(n):
                kind, t, h = UNITS[n]
                nk = 2 * P if kind == "cmp" else (t + 1) * P
                act.wait_ge(*lows.at(n))
                if n >= 2:
                    act.wait_ge(*turned.at(("p", n - 2)))
                if kind == "cmp":
                    act.activation(p_buf[:, n % 2, 0:nk], s_buf[:, n % 2, 0:nk], ACT.Exp, scale=-1.0).then_inc(*probs.mark(n))
                else:
                    m, d = (h + 8 * out_of(n)) % 16, h + 8 * (out_of(n) % 4)
                    act.activation(p_buf[:, n % 2, 0:nk], s_buf[:, n % 2, 0:nk], ACT.Exp, scale=-1.0,
                                   bias=neg_max[:, m:m + 1], accum_out=den[:, d:d + 1]).then_inc(*probs.mark(n))

            def pt_out(n):
                kind, t, h = UNITS[n]
                nk = 2 * P if kind == "cmp" else (t + 1) * P
                act.wait_ge(*turned.at(("p", n)))
                if n >= 2:
                    act.wait_ge(*mixed.at(n - 2))
                act.activation(pt_buf[:, n % 2, 0:nk], TD[bank_of("T", ("p", n))][:, 0:nk], ACT.Copy).then_inc(*act_pt.mark(n))

            def row_in(key):
                b, t = key
                act.wait_ge(*dense_done.at(key))
                bank = D[bank_of("D", key)]
                j = t % 2
                if b == "cmp":
                    act.wait_ge(*scaled.at(("nkv", NT - 2 + t // 2)))
                    act.activation(raw_cmp[:, t, :], bank[:, 0:256], ACT.Copy).then_inc(*copied.mark(("raw", t)))
                    act.activation(gates[:, t, :], bank[:, 256:280], ACT.Exp, scale=-1.0).then_inc(*copied.mark(key))
                    return
                before = (b, t - 1) if t else ("nq", NT - 1) if b == "nkv" else None
                if before:
                    act.wait_ge(*summed.at(before))
                two = (b, t - 2) if t >= 2 else ("nq", NT - 2 + t) if b == "nkv" else None
                if two:
                    act.wait_ge(*scaled.at(two))
                if b == "nq":
                    act.activation(square, bank, ACT.Square).then_inc(*squares.mark(key))
                    act.activation(raw_row[:, j, :], bank, ACT.Copy).then_inc(*copied.mark(key))
                else:
                    src = bank.rearrange("p (b v n) -> p b v n", b=2, v=2)
                    two_b = lambda r: r[:, 0:256].rearrange("p (b n) -> p b n", b=2)
                    act.activation(two_b(square), src[:, :, 0, :], ACT.Square).then_inc(*squares.mark(key))
                    act.activation(n_v[:, t, :, :], src[:, :, 1, :], ACT.Copy).then_inc(*copied.mark(("nv", t)))
                    act.activation(two_b(raw_row[:, j, :]), src[:, :, 0, :], ACT.Copy).then_inc(*copied.mark(key))

            def unit_step(n, last):
                if n - 3 >= 0 and (n - 3) % 2 == 0:
                    pt_out(n - 3)
                if n - 1 >= 0 and n - 1 < last:
                    exp_unit(n - 1)

            def pair_his(n):
                if n in PAIR_KEYS:
                    t = PAIR_KEYS[n]
                    cols = slice(t * P, (t + 1) * P)
                    act.wait_ge(*dense_done.at(("cmp", t)))
                    act.wait_ge(*dve_step.at(("turned", ("nkv", t))))
                    for g in range(2):
                        for half in range(2):
                            ins = act.activation(act_hi[64 * half:64 * half + 64, 4 + g:8:2, cols], n_k[64 * g:64 * g + 64, :, cols], ACT.Copy)
                    ins.then_inc(*pair_hi.mark(("k", t)))
                if n in PAIR_QUERIES:
                    t = PAIR_QUERIES[n]
                    dst = q_pairs[t % 2]
                    if n >= N_MLA:
                        act.wait_ge(*(mixed.at(N_MLA - 1) if t == 2 else scores.at(UNITS.index(("win", t + 2, HEADS - 1)))))
                    act.wait_ge(*dve_step.at(("turned", ("nq", t))))
                    act.activation(dst[0:64, 0:4, :], n_q[0:64, :, t * P:(t + 1) * P], ACT.Copy)
                    act.activation(dst[0:64, 4:8, :], n_q[64:128, :, t * P:(t + 1) * P], ACT.Copy)
                    act.activation(dst[64:128, 4:8, :], n_q[64:128, :, t * P:(t + 1) * P], ACT.Copy).then_inc(*pair_hi.mark(("q", t)))

            for n in range(N_MLA):
                unit_step(n, N_MLA)
                pair_his(n)
                if n in TURN_AT:
                    for half in range(2):
                        turned_out(*TURN_AT[n], half)
                if n == 3:
                    act.wait_ge(*roped.at(QK_ROWS[-1]))
                if n - 1 in ROW_END:
                    row_in(ROWS[ROW_END.index(n - 1)])
                for m in SPLIT_AT_UNIT.get(n, ()):
                    split_hi(m)

            def top_taps(t):
                act.wait_ge(*turned.at(("taps", t)))
                bank = TD[bank_of("T", ("taps", t))][:, 0:2 * P].rearrange("p (j s) -> p j s", j=2)
                for i in range(2):
                    act.activation(tap_planes[0:HD, 2 * i:2 * i + 2, t * P:(t + 1) * P], bank[HD * i:HD * i + HD, :, :],
                                   ACT.Copy).then_inc(*copied.mark(("taps", t, i)))

            def mix_square(g, t):
                src = o_mla[:, t, :] if g == 0 else o_nsa[:, t % 2, :]
                i = MIXES.index((g, t))
                if i:
                    act.wait_ge(*squares.at(("mix", *MIXES[i - 1])))
                act.activation(square, src, ACT.Square, accum_out=ss_mix[:, g * NT + t:g * NT + t + 1]).then_inc(*squares.mark(("mix", g, t)))

            for n in range(N_MLA, N_MLA + 3):
                if (n - 3) % 2 == 0:
                    pt_out(n - 3)
                if n - 1 < N_MLA:
                    exp_unit(n - 1)
                if n == N_MLA:
                    row_in(ROWS[-1])
                    pair_his(n)
            def ln_square(t):
                act.wait_ge(*x2_done.at((1, t, 1)))
                if t < NT - 1:
                    act.wait_ge(*squares.at(("ln2", t + 1)))
                act.activation(ln2_sq, x[:, t, :], ACT.Square, accum_out=ss_ln[:, t:t + 1]).then_inc(*squares.mark(("ln2", t)))

            def ln_his(t):
                for half in range(2):
                    to_hi(("ln2", t, half), act_hi[:, 4 * half:4 * half + 4, t * P:(t + 1) * P], 4, P)

            last = len(UNITS)
            for n in range(N_MLA, last + 6):
                if n - 3 >= N_MLA and n - 3 < last and (n - 3) % 2 == 0:
                    pt_out(n - 3)
                if n - 1 >= N_MLA and n - 1 < last:
                    exp_unit(n - 1)
                u = n - N_MLA
                if u:
                    pair_his(n)
                if u in (1, 3, 5, 7):
                    top_taps(u // 2)
                if u in (6, 8, 10, 12):
                    act.wait_ge(*o_used.at(("mla", u // 2 - 3)))
                    mix_square(0, u // 2 - 3)
                if u in (15, 19):
                    kv = (u - 15) // 4
                    act.wait_ge(*dve_step.at(("z", kv)))
                    act.activation(z_buf[:, 1, kv, :], z_buf[:, 0, kv, :], ACT.Exp, scale=-1.0).then_inc(*exp_small.mark(kv))
                if u in (20, 22, 24, 26):
                    t = u // 2 - 10
                    to_hi(("mix", 0, t), act_hi[:, 0:4, t * P:(t + 1) * P], 4, P)
                done = n - 5
                if done >= N_MLA and (done < last) and UNITS[done][0] == "cmp" and UNITS[done][1] > 0:
                    t = UNITS[done][1]
                    act.wait_ge(*o_summed.at(("cmp", t)))
                    mix_square(1, t)
                done = n - 10
                if done >= N_MLA and UNITS[done][0] == "cmp" and UNITS[done][1]:
                    t = UNITS[done][1]
                    to_hi(("mix", 1, t), act_hi[:, 4:8, t * P:(t + 1) * P], 4, P)
                for m in SPLIT_AT_UNIT.get(n, ()):
                    split_hi(m)
                for t in (3, 2):
                    if u == LN2_AT[t][0]:
                        ln_square(t)
                    if u == LN2_AT[t][2]:
                        ln_his(t)
            act.wait_ge(*o_used.at(("cmp", 0)))
            mix_square(1, 0)

            ln_square(1)
            to_hi(("mix", 1, 0), act_hi[:, 4:8, 0:P], 4, P)
            ln_his(1)
            after(("wo", 1, 0, 0))
            ln_square(0)
            after(("wo", 1, 0, 1))
            ln_his(0)

            for half in range(2):
                for f in range(UP_HALF):
                    key = ("up", half, f)
                    act.wait_ge(*dense_done.at(key))
                    if f >= 2 or half:
                        act.wait_ge(*sq_done.at((half, f - 2) if f >= 2 else (0, UP_HALF - 2 + f)))
                    act.activation(relu_b[:, f % 2, :], up_bank(half, f), ACT.Relu).then_inc(*relu_done.mark((half, f)))
                    after(key)
                    act.wait_ge(*sq_done.at((half, f)))
                    act.activation(a_hi[:, f, :], sq_b[:, f % 2, :], ACT.Copy).then_inc(*a_hi_done.mark((half, f)))
                for c in range(2):
                    for i in range(UP_HALF // 2):
                        after(("down", half, c, i))

        @block.vector
        def _(dve):
            def split_lo(n):
                m, width = SPLIT_AT[n], PIECES[n][2]
                dve.wait_ge(*hi_done.at(n))
                dve.tensor_tensor(w_lo[:, m % RING, 0:width], raw[:, n % RAW, 0:width],
                                  w_hi[:, m % RING, 0:width].bitcast(F32), ALU.subtract).then_inc(*lo_done.mark(n))

            def after(group):
                for n in SPLIT_AFTER.get(group, ()):
                    split_lo(n)

            def to_lo(key, dst, hi, cols):
                dve.wait_ge(*turn_hi.at(key))
                src = TD[bank_of("T", key)][:, 0:cols * P].rearrange("p (k s) -> p k s", k=cols)
                if key[0] == "mix":
                    src = backwards(src)
                dve.tensor_tensor(dst, src, hi.bitcast(F32), ALU.subtract).then_inc(*turn_lo.mark(key))

            def ln_rows(t, name, gain):
                dve.wait_ge(*rsqrt_done.at((name, t)))
                rows_ = ln_row if name == "ln1" else ln2_row
                before = t - 2 if name == "ln1" else t + 2
                if before in range(NT):
                    dve.wait_ge(*turned.at((name, before, 1)))
                dve.scalar_tensor_tensor(rows_[:, t % 2, :], x[:, t, :], rs_ln[:, t:t + 1], gain, ALU.mult, ALU.mult).then_inc(*scaled.mark((name, t)))

            def ln_lows(t, name):
                for half in range(2):
                    to_lo((name, t, half), act_lo[:, 4 * half:4 * half + 4, t * P:(t + 1) * P],
                          act_hi[:, 4 * half:4 * half + 4, t * P:(t + 1) * P], 4)

            dve.wait_ge(*gain1_in.at())
            ln_rows(0, "ln1", gain_ln1)
            split_lo(SPLITS[0])
            ln_rows(1, "ln1", gain_ln1)
            split_lo(SPLITS[1])
            ln_lows(0, "ln1")
            split_lo(SPLITS[2])
            ln_rows(2, "ln1", gain_ln1)
            ln_lows(1, "ln1")
            split_lo(SPLITS[3])
            ln_rows(3, "ln1", gain_ln1)
            ln_lows(2, "ln1")
            ln_lows(3, "ln1")
            split_lo(SPLITS[4])
            for j in range(4):
                lo, hi = 512 * j, min(512 * (j + 1), VEC)
                dve.wait_ge(*turned.at(("vec", j)))
                dve.tensor_copy(bias_vec[:, lo:hi], TD[bank_of("T", ("vec", j))][0:8, 0:hi - lo]).then_inc(*dve_step.mark(f"vec{j}"))

            def latent_row(name, t):
                lo, hi, c = (0, Q_RANK, t) if name == "cq" else (Q_RANK, Q_RANK + KV_RANK, NT + t)
                dve.wait_ge(*rsqrt_done.at((name, t)))
                dve.wait_ge(*copied.at((name, t)))
                dve.scalar_tensor_tensor(c_row[:, t, lo:hi], c_row[:, t, lo:hi], rs_c[:, c:c + 1], gain_c[:, lo:hi],
                                         ALU.mult, ALU.mult).then_inc(*scaled.mark((name, t)))

            dve.wait_ge(*gainc_in.at())
            for t in range(NT):
                after(("cq", t))
                if t:
                    latent_row("cq", t - 1)
            latent_row("cq", NT - 1)
            for t in range(NT):
                after(("ckv", t))
                to_lo(("cq", t), c_lo[:, 0:3, t * P:(t + 1) * P], c_hi[:, 0:3, t * P:(t + 1) * P], 3)
                if t:
                    latent_row("ckv", t - 1)
            latent_row("ckv", NT - 1)
            def head_sums(name, t):
                n = QK if name == "uq" else NOPE
                if name == "uq":
                    to_lo(("ckv", t), c_lo[:, 3:5, t * P:(t + 1) * P], c_hi[:, 3:5, t * P:(t + 1) * P], 2)
                after((name, t, 0))
                dve.wait_ge(*squares.at((name, t, 1)))
                dve.tensor_reduce(ss_row[:, 8 * (t % 2):8 * (t % 2) + 8], qk_sq[:, 0:HEADS * n].rearrange("p (h n) -> p h n", h=HEADS),
                                  AX.X, ALU.add).then_inc(*summed.mark((name, t)))
                after((name, t, 1))

            def head_rows(name, t):
                n, tab = (QK, tab_q) if name == "uq" else (NOPE, tab_k)
                rs = rs_row[:, 8 * (t % 2):8 * (t % 2) + 8]
                row = qk_row[:, t % 2, :].rearrange("p (h n) -> p h n", h=HEADS)
                fin = qk_out.rearrange("p (h n) -> p h n", h=HEADS)
                dve.wait_ge(*rsqrt_done.at((name, t)))
                dve.wait_ge(*copied.at((name, t, 1)))
                if name == "ukv":
                    dve.wait_ge(*copied.at(("kr", t)))
                    dve.tensor_tensor(row[:, :, NOPE:], kr[:, t, :].unsqueeze(1).to_broadcast([P, HEADS, ROPE]),
                                      rs.unsqueeze(2).to_broadcast([P, HEADS, ROPE]), ALU.mult)
                dve.tensor_tensor(row[:, :, 0:n], row[:, :, 0:n], rs.unsqueeze(2).to_broadcast([P, HEADS, n]),
                                  ALU.mult).then_inc(*scaled.mark((name, t)))
                before = (name, t - 1) if t else ("uq", NT - 1) if name == "ukv" else None
                if before:
                    dve.wait_ge(*turned.at((*before, 1)))
                if t == 0:
                    dve.wait_ge(*pool_step.at("g_q" if name == "uq" else "g_k"))
                dve.wait_ge(*scaled.at((name, t)))
                dve.tensor_tensor(fin, row, tab[:, t, 0:QK].unsqueeze(1).to_broadcast([P, HEADS, QK]),
                                  ALU.mult).then_inc(*dve_step.mark(("gain", name, t)))

            head_sums(*QK_ROWS[0])
            for i, key in enumerate(QK_ROWS):
                if i + 1 < len(QK_ROWS):
                    head_sums(*QK_ROWS[i + 1])
                if i + 1 < len(QK_ROWS):
                    head_rows(*key)

            def low_unit(n):
                kind, t, h = UNITS[n]
                b, nk = n % 2, (t + 1) * P
                bank = S[n % 2]
                dve.wait_ge(*scores.at(n))
                if n >= 2:
                    dve.wait_ge(*probs.at(n - 2))
                if kind == "cmp":
                    s = s_buf[:, b, 0:256]
                    s3 = s.rearrange("p (h c) -> p h c", h=HEADS)
                    nm = neg_max[:, (8 * out_of(n)) % 16:(8 * out_of(n)) % 16 + 8]
                    dve.tensor_tensor(s.rearrange("p (g n) -> p g n", g=2), bank[:, 0:256].rearrange("p (g n) -> p g n", g=2),
                                      bias_c[:, t, :, :], ALU.add).then_inc(*dve_step.mark(("c0", t)))
                    dve.wait_ge(*dve_step.at(("c0", t)))
                    dve.tensor_reduce(nm, s3, AX.X, ALU.min).then_inc(*dve_step.mark(("c1", t)))
                    dve.wait_ge(*dve_step.at(("c1", t)))
                    dve.tensor_scalar(nm, nm, LEAST, None, ALU.min).then_inc(*dve_step.mark(("c2", t)))
                    dve.wait_ge(*dve_step.at(("c2", t)))
                    dve.tensor_tensor(s3, s3, nm.unsqueeze(2).to_broadcast([P, HEADS, NC]), ALU.subtract).then_inc(*lows.mark(n))
                    return
                m = (h + 8 * out_of(n)) % 16
                other = const("mask")[:, SEQ - nk:] if kind == "mla" else bias[:, h, SEQ - nk:]
                dve.tensor_tensor_reduce(s_buf[:, b, 0:nk], bank[:, 0:nk], other, 1.0, LEAST, ALU.add, ALU.min,
                                         neg_max[:, m:m + 1]).then_inc(*lows.mark(n))

            def pt_out(n):
                kind, t, h = UNITS[n]
                nk = 2 * P if kind == "cmp" else (t + 1) * P
                dve.wait_ge(*turned.at(("p", n)))
                if n >= 2:
                    dve.wait_ge(*mixed.at(n - 2))
                dve.tensor_copy(pt_buf[:, n % 2, 0:nk], TD[bank_of("T", ("p", n))][:, 0:nk]).then_inc(*dve_pt.mark(n))

            def out_row(kind, t):
                m = OUTS.index((kind, t))
                bank = O[m % 2].rearrange("p (h n) -> p h n", h=HEADS)
                d, r = den[:, 8 * (m % 4):8 * (m % 4) + 8], rden[:, 8 * (m % 4):8 * (m % 4) + 8]
                n = max(i for i, u in enumerate(UNITS) if u[0] == kind and u[1] == t)
                dve.wait_ge(*probs.at(n))
                if kind == "cmp":
                    dve.wait_ge(*dve_step.at(("den", t)))
                dve.tensor_scalar(d, d, 1e-30, None, ALU.max).then_inc(*dve_step.mark(("d1", kind, t)))
                dve.wait_ge(*dve_step.at(("d1", kind, t)))
                dve.reciprocal(r, d).then_inc(*dve_step.mark(("d2", kind, t)))
                dve.wait_ge(*dve_step.at(("d2", kind, t)))
                if kind != "mla":
                    j = ("cmp", "sel", "win").index(kind)
                    dve.tensor_tensor(r, r, gates[:, t, 8 * j:8 * j + 8], ALU.mult).then_inc(*dve_step.mark(("d3", kind, t)))
                    dve.wait_ge(*dve_step.at(("d3", kind, t)))
                rb = r.unsqueeze(2).to_broadcast([P, HEADS, HD])
                dve.wait_ge(*mixed.at(n))
                if kind == "mla":
                    dve.tensor_tensor(o_mla[:, t, :].rearrange("p (h n) -> p h n", h=HEADS), bank, rb, ALU.mult).then_inc(*o_used.mark((kind, t)))
                elif kind == "sel":
                    if t < 2:
                        dve.wait_ge(*mix_done.at((1, t + 2)))
                    dve.tensor_tensor(o_nsa[:, t % 2, :].rearrange("p (h n) -> p h n", h=HEADS), bank, rb, ALU.mult).then_inc(*o_used.mark((kind, t)))
                else:
                    i = PARTS.index((kind, t))
                    tmp = raw_row[:, i % 2, :]
                    if i >= 2 and PARTS[i - 2][1]:
                        dve.wait_ge(*o_summed.at(PARTS[i - 2]))
                    elif i >= 2:
                        dve.wait_ge(*o_used.at(PARTS[i - 2]))
                    dve.tensor_tensor(tmp.rearrange("p (h n) -> p h n", h=HEADS), bank, rb, ALU.mult).then_inc(*dve_step.mark(("o", kind, t)))
                    if t == 0:
                        dve.wait_ge(*dve_step.at(("o", kind, t)))
                        dve.wait_ge(*o_used.at(("sel" if kind == "win" else "win", t)))
                        dve.tensor_tensor(o_nsa[:, t % 2, :], o_nsa[:, t % 2, :], tmp, ALU.add).then_inc(*o_used.mark((kind, t)))

            def nsa_sum(key):
                b, t = key
                n = 8 if b == "nq" else 4
                dve.wait_ge(*squares.at(key))
                dve.tensor_reduce(ss_row[:, 8 * (t % 2):8 * (t % 2) + n], square[:, 0:n * HD].rearrange("p (h n) -> p h n", h=n),
                                  AX.X, ALU.add).then_inc(*summed.mark(key))

            def nsa_row(key):
                b, t = key
                j = t % 2
                n = 8 if b == "nq" else 4
                rs = rs_row[:, 8 * j:8 * j + n]
                row = raw_row[:, j, 0:n * HD].rearrange("p (h n) -> p h n", h=n)
                dve.wait_ge(*rsqrt_done.at(key))
                dve.wait_ge(*copied.at(key))
                dve.tensor_tensor(row, row, rs.unsqueeze(2).to_broadcast([P, n, HD]), ALU.mult).then_inc(*dve_step.mark(("nr", key)))
                dve.wait_ge(*dve_step.at(("nr", key)))
                before = (b, t - 2) if t >= 2 else ("nq", NT - 2 + t) if b == "nkv" else None
                if before:
                    dve.wait_ge(*turned.at(before))
                fin = o_nsa[:, j, :]
                if b == "nq":
                    gain = const("g_nq").unsqueeze(1).unsqueeze(1).to_broadcast([P, 2, 4, HD])
                    dve.tensor_tensor(fin.rearrange("p (r g n) -> p g r n", r=4, g=2), row.rearrange("p (g r) n -> p g r n", g=2),
                                      gain, ALU.mult).then_inc(*scaled.mark(key))
                else:
                    gain = const("g_nk")[:, HD:3 * HD].rearrange("p (b n) -> p b n", b=2).unsqueeze(2).to_broadcast([P, 2, 2, HD])
                    dve.tensor_tensor(fin[:, 0:256].rearrange("p (b g n) -> p b g n", b=2, g=2), row.rearrange("p (b g) n -> p b g n", b=2),
                                      gain, ALU.mult).then_inc(*scaled.mark(key))

            def nsa_turned(key):
                b, t = key
                k = 4 if b == "nq" else 2
                dve.wait_ge(*turned.at(key))
                dst = (n_q if b == "nq" else n_k)[:, :, t * P:(t + 1) * P]
                src = TD[bank_of("T", key)][:, 0:k * P].rearrange("p (k s) -> p k s", k=k)
                dve.tensor_copy(dst, backwards(src) if b == "nq" else src).then_inc(*dve_step.mark(("turned", key)))

            def gate_row(t):
                dve.wait_ge(*copied.at(("cmp", t)))
                g = gates[:, t, :]
                dve.tensor_scalar(g, g, 1.0, None, ALU.add).then_inc(*dve_step.mark(("g0", t)))
                dve.wait_ge(*dve_step.at(("g0", t)))
                dve.reciprocal(g, g).then_inc(*dve_step.mark(("g1", t)))

            def pair_los(n):
                if n - 1 in PAIR_KEYS:
                    t = PAIR_KEYS[n - 1]
                    cols = slice(t * P, (t + 1) * P)
                    dve.wait_ge(*pair_hi.at(("k", t)))
                    for g in range(2):
                        ps = slice(64 * g, 64 * g + 64)
                        for half in range(2):
                            ins = dve.tensor_tensor(act_lo[64 * half:64 * half + 64, 4 + g:8:2, cols], n_k[ps, :, cols],
                                                    act_hi[ps, 4 + g:8:2, cols].bitcast(F32), ALU.subtract)
                    ins.then_inc(*pair_lo.mark(("k", t)))
                if n - 1 in PAIR_QUERIES:
                    t = PAIR_QUERIES[n - 1]
                    dst = q_pairs[t % 2]
                    cols = slice(t * P, (t + 1) * P)
                    dve.wait_ge(*pair_hi.at(("q", t)))
                    dve.tensor_tensor(dst[64:128, 0:4, :], n_q[0:64, :, cols], dst[0:64, 0:4, :].bitcast(F32), ALU.subtract)
                    dve.tensor_tensor(dst[64:128, 4:8, :], n_q[64:128, :, cols], dst[64:128, 4:8, :].bitcast(F32),
                                      ALU.subtract).then_inc(*pair_lo.mark(("q", t)))

            dve.wait_ge(*pool_step.at("gnq"))
            for n in range(N_MLA):
                if n - 3 >= 0 and (n - 3) % 2 == 1:
                    pt_out(n - 3)
                low_unit(n)
                pair_los(n)
                if n == 1:
                    head_rows(*QK_ROWS[-1])
                if n % 8 == 5 and n >= 8:
                    out_row("mla", n // 8 - 1)
                if n - 1 in ROW_END:
                    r = ROW_END.index(n - 1)
                    if ROWS[r][0] == "cmp":
                        gate_row(ROWS[r][1])
                    else:
                        nsa_sum(ROWS[r])
                if n - 3 in ROW_END[0:8]:
                    nsa_row(ROWS[ROW_END.index(n - 3)])
                if n - 5 in ROW_END[0:8]:
                    nsa_turned(ROWS[ROW_END.index(n - 5)])
                for m in SPLIT_AT_UNIT.get(n, ()):
                    split_lo(m)
            for n in range(N_MLA, N_MLA + 3):
                if (n - 3) % 2 == 1:
                    pt_out(n - 3)
            gate_row(NT - 1)
            pair_los(N_MLA)
            pair_los(N_MLA + 1)
            out_row("mla", NT - 1)

            def low_taps(t):
                bank = TD[bank_of("T", ("taps", t))][:, 0:2 * P].rearrange("p (j s) -> p j s", j=2)
                lo = int(t == 0)
                for i in range(2):
                    dve.wait_ge(*copied.at(("taps", t, i)))
                    dve.tensor_copy(tap_planes[HD:P, 2 * i:2 * i + 2, t * P - 1 + lo:(t + 1) * P - 1],
                                    bank[HD * i:HD * i + HD, :, lo:]).then_inc(*dve_step.mark(("taps", t, i)))

            def mix_lows(g, t):
                at = (slice(None), slice(4 * g, 4 * g + 4), slice(t * P, (t + 1) * P))
                to_lo(("mix", g, t), act_lo[at], act_hi[at], 4)

            def compress(u):
                if u in (1, 3, 5, 7):
                    low_taps(u // 2)
                if u == 4:
                    dve.wait_ge(*turned.at("gt"))
                    dve.tensor_copy(gate_t.rearrange("p (t s) -> p t s", t=NT),
                                    backwards(TD[bank_of("T", "gt")][0:24, :].rearrange("p (t s) -> p t s", t=NT))).then_inc(*dve_step.mark("gt"))
                if u == 6:
                    dve.wait_ge(*turned.at("gates"))
                    dve.tensor_copy(gates, TD[bank_of("T", "gates")][:, 0:NT * 24].rearrange("p (t n) -> p t n", t=NT)).then_inc(*dve_step.mark("gates"))
                    dve.memset(v_diag, 0.0).then_inc(*dve_step.mark("vd0"))
                    dve.memset(hid_v, 0.0).then_inc(*dve_step.mark("hv0"))
                    dve.memset(hid_k, 0.0).then_inc(*dve_step.mark("hk0"))
                if u in (8, 9):
                    g = u - 8
                    dve.wait_ge(*turned.at(("bc", g)))
                    dve.tensor_copy(bias_c[:, :, g, :], TD[bank_of("T", ("bc", g))].rearrange("p (t n) -> p t n", t=NT)).then_inc(*dve_step.mark(("bc", g)))
                if u == 9:
                    dve.wait_ge(*turned.at(("bc", 1)))
                    dve.tensor_copy(tap_planes[:, 4:6, 0:CMP_BLOCK:2], const("pe").rearrange("p (kv l) -> p kv l", kv=2)).then_inc(*dve_step.mark("pe_rows"))
                if u in (14, 18):
                    kv = (u - 14) // 4
                    dve.wait_ge(*turned.at(("hid", kv)))
                    bank = TD[bank_of("T", ("hid", kv))]
                    dve.tensor_copy(pe_col[:, kv:kv + 1], bank[:, 2 * N_CMP:2 * N_CMP + 1]).then_inc(*dve_step.mark(("pe", kv)))
                    dve.wait_ge(*dve_step.at(("pe", kv)))
                    dve.tensor_scalar(z_buf[:, 0, kv, :], bank[:, 0:2 * N_CMP], pe_col[:, kv:kv + 1], None, ALU.add).then_inc(*dve_step.mark(("z", kv)))
                if u in (16, 21):
                    kv = (u - 16) // 5
                    dve.wait_ge(*exp_small.at(kv))
                    e = z_buf[:, 1, kv, :]
                    dve.tensor_scalar(e, e, 1.0, None, ALU.add).then_inc(*dve_step.mark(("e1", kv)))
                    dve.wait_ge(*dve_step.at(("e1", kv)))
                    dve.reciprocal(z_buf[:, 2, kv, :], e).then_inc(*dve_step.mark(("e2", kv)))
                    dve.wait_ge(*dve_step.at(("e2", kv)))
                    z = z_buf[:, 0, kv, :].rearrange("p (g c) -> p g c", g=2)
                    r = z_buf[:, 2, kv, :].rearrange("p (g c) -> p g c", g=2)
                    if kv == 0:
                        dve.tensor_tensor(hid_k.rearrange("p (g c) -> p g c", g=2)[:, :, 0:N_CMP], z, r, ALU.mult).then_inc(*dve_step.mark("hid_k"))
                    else:
                        for g in range(2):
                            rep = lambda v: v[:, g, :].unsqueeze(1).to_broadcast([P, 4, N_CMP])
                            dve.tensor_tensor(hid_v[:, g, :, 0:N_CMP], rep(z), rep(r), ALU.mult).then_inc(*dve_step.mark(("hid_v", g)))
                if u in (21, 23, 25, 27):
                    mix_lows(0, (u - 21) // 2)
                if u == 22:
                    dve.wait_ge(*turned.at("kc"))
                    bank = TD[bank_of("T", "kc")]
                    dve.tensor_copy(kc_row, bank[0:64, 0:HD]).then_inc(*dve_step.mark("kc0"))
                    dve.wait_ge(*dve_step.at("kc0"))
                    dve.tensor_tensor(kc_sq, kc_row, kc_row, ALU.mult).then_inc(*dve_step.mark("kc1"))
                    dve.wait_ge(*dve_step.at("kc1"))
                    dve.tensor_reduce(kc_ss[0:64, :], kc_sq, AX.X, ALU.add).then_inc(*dve_step.mark("kc_ss"))
                if u == 24:
                    dve.wait_ge(*turned.at("vc"))
                    bank = TD[bank_of("T", "vc")]
                    for h in range(4):
                        ps = slice(32 * h, 32 * h + 32)
                        dve.tensor_copy(v_diag[ps, :, HD * h:HD * h + HD], bank[ps, 0:2 * HD].rearrange("p (g n) -> p g n", g=2)).then_inc(*dve_step.mark(("vd", h)))
                if u == 26:
                    dve.wait_ge(*rsqrt_done.at("kc"))
                    dve.scalar_tensor_tensor(kc_sq, kc_row, kc_rs[0:64, :], const("g_nk", 64)[:, 0:HD], ALU.mult, ALU.mult).then_inc(*dve_step.mark("kc2"))
                if u == 28:
                    dve.wait_ge(*turned.at("kcT"))
                    bank = TD[bank_of("T", "kcT")]
                    dve.tensor_copy(k_cmp[0:64, :], bank[0:64, 0:NC]).then_inc(*dve_step.mark("k0"))
                    dve.tensor_copy(k_cmp[64:128, :], bank[0:64, NC:2 * NC]).then_inc(*dve_step.mark("k_cmp"))

            def residual(g, t, c):
                dve.wait_ge(*dense_done.at(("wo", g, t, c)))
                if g:
                    dve.wait_ge(*x2_done.at((0, t, c)))
                xs = x[:, t, 512 * c:512 * c + 512]
                dve.tensor_tensor(xs, D[bank_of("D", ("wo", g, t, c))], xs, ALU.add).then_inc(*x2_done.mark((g, t, c)))

            last = len(UNITS)
            dve.wait_ge(*bias_in.at())
            for n in range(N_MLA, last + 9):
                if n - 3 >= N_MLA and n - 3 < last and (n - 3) % 2 == 1:
                    pt_out(n - 3)
                if n < last:
                    low_unit(n)
                compress(n - N_MLA)
                if n > N_MLA + 1:
                    pair_los(n)
                if n - 1 >= N_MLA and n - 1 < last and UNITS[n - 1][0] == "cmp":
                    t, m = UNITS[n - 1][1], out_of(n - 1)
                    dve.wait_ge(*probs.at(n - 1))
                    dve.tensor_reduce(den[:, 8 * (m % 4):8 * (m % 4) + 8], p_buf[:, (n - 1) % 2, 0:256].rearrange("p (h c) -> p h c", h=HEADS),
                                      AX.X, ALU.add).then_inc(*dve_step.mark(("den", t)))
                done = n - 5
                if done >= N_MLA and done < last:
                    kind, t, h = UNITS[done]
                    if kind == "cmp" or h == HEADS - 1:
                        out_row(kind, t)
                for m in SPLIT_AT_UNIT.get(n, ()):
                    split_lo(m)
                for g, t, c, j in WO_AT.get(n - N_MLA, ()):
                    if j:
                        residual(g, t, c)
                done = n - 11
                if done >= N_MLA and done < last and UNITS[done][0] == "cmp":
                    mix_lows(1, UNITS[done][1])
                for t in (3, 2):
                    if n - N_MLA == LN2_AT[t][1]:
                        dve.wait_ge(*gain2_in.at())
                        ln_rows(t, "ln2", gain_ln2)
                    if n - N_MLA == LN2_AT[t][2]:
                        ln_lows(t, "ln2")
            dve.wait_ge(*rsqrt_done.at(("mix", 1, 0)))
            dve.wait_ge(*turned.at(("mix", 1, 2)))
            dve.scalar_tensor_tensor(mix_row[:, 1, :], o_nsa[:, 0, :], rs_mix[:, NT:NT + 1], gain_grp[:, 512:1024],
                                     ALU.mult, ALU.mult).then_inc(*mixed_last.mark())

            ln_rows(1, "ln2", gain_ln2)
            mix_lows(1, 0)
            ln_lows(1, "ln2")
            residual(1, 0, 0)
            after(("wo", 1, 0, 0))
            residual(1, 0, 1)
            ln_rows(0, "ln2", gain_ln2)
            after(("wo", 1, 0, 1))
            ln_lows(0, "ln2")

            for half in range(2):
                for f in range(UP_HALF):
                    dve.wait_ge(*relu_done.at((half, f)))
                    if f >= 2 or half:
                        dve.wait_ge(*a_lo_done.at((half, f - 2) if f >= 2 else (0, UP_HALF - 2 + f)))
                    dve.tensor_tensor(sq_b[:, f % 2, :], relu_b[:, f % 2, :], relu_b[:, f % 2, :], ALU.mult).then_inc(*sq_done.mark((half, f)))
                    after(("up", half, f))
                    dve.wait_ge(*a_hi_done.at((half, f)))
                    dve.tensor_tensor(a_lo[:, f, :], sq_b[:, f % 2, :], a_hi[:, f, :].bitcast(F32), ALU.subtract).then_inc(*a_lo_done.mark((half, f)))
                for c in range(2):
                    for i in range(UP_HALF // 2):
                        after(("down", half, c, i))
                    for t in range(NT):
                        dve.wait_ge(*mixed.at(("down", half, c, t)))
                        xs = x[:, t, 512 * c:512 * c + 512]
                        if half:
                            dve.wait_ge(*x2_done.at(("part", c, t)))
                        done = y_done.mark((t, c)) if half else x2_done.mark(("part", c, t))
                        dve.tensor_tensor(xs, down_banks(half, c)[t], xs, ALU.add).then_inc(*done)

        @block.tensor
        def _(pe):
            bank_users = {"D": [], "T": []}

            def take(kind, key, freed_by):
                users = bank_users[kind]
                if len(users) >= 2:
                    sig, k = users[-2]
                    pe.wait_ge(*sig.at(k))
                known["bank", kind, key] = len(users) % 2
                users.append((sig_key := freed_by))
                return (D if kind == "D" else T)[(len(users) - 1) % 2]

            def three(dst, act_cols, n, w_cols, start, stop):
                a_h, a_l = act_cols
                w_h, w_l = w_cols
                pe.matmul(dst, a_h, w_h, start=start, stop=False)
                pe.matmul(dst, a_h, w_l, start=False, stop=False)
                return pe.matmul(dst, a_l, w_h, start=False, stop=stop)

            def piece(what, i):
                n = PIECE_AT[what, i]
                pe.wait_ge(*lo_done.at(n))
                m = SPLIT_AT[n] % RING
                return w_hi[:, m, :], w_lo[:, m, :]

            def used(ins, what, i):
                ins.then_inc(*piece_used.mark(PIECE_AT[what, i]))

            def turn(key, tiles, freed_by, kind="T", step=P):
                bank = take(kind, key, freed_by)
                if kind == "D":
                    known["bank", "T", key] = 2 + known["bank", "D", key]
                for i, tile in enumerate(tiles):
                    k, m = tile.shape
                    ins = pe.transpose(bank[0:m, i * step:i * step + k], tile, ident[0:k, 0:k])
                ins.then_inc(*turned.mark(key))

            def turn_ln(name, t, kind="T"):
                pe.wait_ge(*scaled.at((name, t)))
                rows_ = ln_row if name == "ln1" else ln2_row
                for half in range(2):
                    turn((name, t, half), [rows_[:, t % 2, (4 * half + k) * P:(4 * half + k + 1) * P] for k in range(4)],
                         (turn_lo, (name, t, half)), kind=kind)

            def project(block_, t, pieces=range(4)):
                n = BLOCK_COLS[block_]
                key = (block_, t)
                if pieces[0] == 0:
                    take("D", key, (copied, key))
                dst = D[known["bank", "D", key]][:, 0:n]
                if block_ == "cq":
                    pe.wait_ge(*turn_lo.at(("ln1", t, 1)))
                for i in pieces:
                    h, l = piece(block_, i)
                    for j in range(2):
                        k = 2 * i + j
                        ins = three(dst, (act_hi[:, k, t * P:(t + 1) * P], act_lo[:, k, t * P:(t + 1) * P]), n,
                                    (h[:, j * n:(j + 1) * n], l[:, j * n:(j + 1) * n]), k == 0, k == KD - 1)
                    if i < 3 and t == NT - 1:
                        used(ins, block_, i)
                if pieces[-1] == 3:
                    ins.then_inc(*dense_done.mark(key))

            def expand(name, t, c):
                k0, kn, w = (0, 3, 4 * QK) if name == "uq" else (3, 2, 4 * (NOPE + VD))
                key = (name, t, c)
                dst = take("D", key, (copied, key))[:, 0:w]
                pe.wait_ge(*turn_lo.at(("cq" if name == "uq" else "ckv", t)))
                for k in range(kn):
                    h, l = piece(name, k)
                    ins = three(dst, (c_hi[:, k0 + k, t * P:(t + 1) * P], c_lo[:, k0 + k, t * P:(t + 1) * P]), w,
                                (h[:, c * w:(c + 1) * w], l[:, c * w:(c + 1) * w]), k == 0, k == kn - 1)
                    if t == NT - 1 and c == 1 and k < kn - 1:
                        used(ins, name, k)
                ins.then_inc(*dense_done.mark(key))

            def turn_heads(name, t):
                pe.wait_ge(*roped.at((name, t)))
                for half in range(2):
                    turn((name, t, half), [qk_out[:, (4 * half + h) * QK:(4 * half + h + 1) * QK] for h in range(4)],
                         (copied, ("turned", (name, t, half))))

            pe.wait_ge(*ident_in.at())
            turn_ln("ln1", 0)
            turn_ln("ln1", 1)
            project("cq", 0)
            turn_ln("ln1", 2)
            project("cq", 1)
            turn_ln("ln1", 3)
            pe.wait_ge(*onehot_in.at("table"))
            for j in range(4):
                lo, hi = 512 * j, min(512 * (j + 1), VEC)
                bank = take("T", ("vec", j), (dve_step, f"vec{j}"))
                pe.matmul(bank[0:8, 0:hi - lo], const("rel", 33), onehot[:, lo:hi], start=True, stop=True).then_inc(*turned.mark(("vec", j)))
            project("cq", 2)
            project("cq", 3)
            def turn_latent(name, t):
                lo, n = (0, 3) if name == "cq" else (Q_RANK, 2)
                pe.wait_ge(*scaled.at((name, t)))
                turn((name, t), [c_row[:, t, lo + k * P:lo + (k + 1) * P] for k in range(n)], (turn_lo, (name, t)))
            for t in range(NT):
                project("ckv", t)
                turn_latent("cq", t)
            for i in range(len(QK_ROWS)):
                if i < NT:
                    turn_latent("ckv", i)
                for c in range(2):
                    expand(*QK_ROWS[i], c)
                if i >= 2:
                    turn_heads(*QK_ROWS[i - 2])

            def score_unit(n):
                kind, t, h = UNITS[n]
                nk = (t + 1) * P
                bank = S[n % 2]
                if n >= 2:
                    pe.wait_ge(*(dve_step.at(("c0", UNITS[n - 2][1])) if UNITS[n - 2][0] == "cmp" else lows.at(n - 2)))
                if kind == "mla":
                    if h % 4 == 0:
                        pe.wait_ge(*copied.at(("turned", ("ukv", t, h // 4))))
                    ins = pe.matmul(bank[:, 0:nk], m_q[0:QK, t, h, :], m_k[0:QK, h, 0:nk], start=True, stop=True)
                elif kind == "cmp":
                    for h in range(HEADS):
                        ps = slice(64 * (h // 4), 64 * (h // 4) + 64)
                        if h == 4:
                            ins.then_inc(*half_scored.mark(n))
                            pe.wait_ge(*half_scored.at(n))
                        ins = pe.matmul(bank[:, NC * h:NC * h + NC], n_q[ps, h % 4, t * P:(t + 1) * P], k_cmp[ps, :], start=True, stop=True)
                else:
                    if kind == "sel" and h == 0:
                        pe.wait_ge(*pair_lo.at(("q", t)))
                        pe.wait_ge(*pair_lo.at(("k", t)))
                    at = 4 + 2 * int(kind == "win") + h // 4
                    pe.matmul(bank[:, 0:nk], q_pairs[t % 2][:, h, :], act_hi[:, at, 0:nk], start=True, stop=False)
                    ins = pe.matmul(bank[:, 0:nk], q_pairs[t % 2][:, h, :], act_lo[:, at, 0:nk], start=False, stop=True)
                ins.then_inc(*scores.mark(n))

            def turn_unit(n):
                kind, t, h = UNITS[n]
                pe.wait_ge(*probs.at(n))
                count = 2 if kind == "cmp" else t + 1
                turn(("p", n), [p_buf[:, n % 2, j * P:(j + 1) * P] for j in range(count)], (act_pt if n % 2 == 0 else dve_pt, n))

            def mix_unit(n):
                kind, t, h = UNITS[n]
                m = out_of(n)
                bank = O[m % 2]
                pe.wait_ge(*(act_pt if n % 2 == 0 else dve_pt).at(n))
                if m >= 2 and (h == 0 or kind == "cmp"):
                    k2, t2 = OUTS[m - 2]
                    pe.wait_ge(*(o_used.at((k2, t2)) if k2 in ("mla", "sel") else dve_step.at(("o", k2, t2))))
                if kind == "cmp":
                    for g in range(2):
                        ins = pe.matmul(bank[:, 256 * g:256 * g + 256], pt_buf[:, n % 2, g * P:(g + 1) * P], v_diag[:, g, :], start=True, stop=True)
                else:
                    for j in range(t + 1):
                        v = m_v[:, j, h * VD:(h + 1) * VD] if kind == "mla" else \
                            n_v[:, j, int(kind == "win"), HD * (h // 4):HD * (h // 4) + HD]
                        ins = pe.matmul(bank[:, 64 * h:64 * h + 64], pt_buf[:, n % 2, j * P:(j + 1) * P], v, start=j == 0, stop=j == t)
                ins.then_inc(*mixed.mark(n))

            def turn_nsa(key):
                b, t = key
                pe.wait_ge(*scaled.at(key))
                turn(key, [o_nsa[:, t % 2, k * P:(k + 1) * P] for k in range(4 if b == "nq" else 2)], (dve_step, ("turned", key)))

            for n in range(N_MLA + 4):
                if n < N_MLA:
                    score_unit(n)
                    for r, key in enumerate(ROWS):
                        here = [i for i in range(4) if unit_of(r, i) == n]
                        if here:
                            project(*key, here)
                if n in TURN_AT:
                    turn_heads(*TURN_AT[n])
                if n - 2 >= 0 and n - 2 < N_MLA:
                    turn_unit(n - 2)
                if n - 4 >= 0:
                    mix_unit(n - 4)
                if n - 4 in ROW_END[0:8]:
                    turn_nsa(ROWS[ROW_END.index(n - 4)])

            def turn_taps(t):
                turn(("taps", t), [raw_cmp[:, t, j * P:(j + 1) * P] for j in range(2)], (dve_step, ("taps", t, 1)), kind="D")

            def hidden(kv, quarter):
                if quarter == 0:
                    take("D", ("hid", kv), (dve_step, ("z", kv)))
                    known["bank", "T", ("hid", kv)] = 2 + known["bank", "D", ("hid", kv)]
                bank = TD[known["bank", "T", ("hid", kv)]]
                n = PIECE_AT["w1", 2 * kv + quarter // 2]
                pe.wait_ge(*raw_in[n % RAW].at(n))
                for i in range(4 * (quarter % 2), 4 * (quarter % 2) + 4):
                    lp = 8 * (quarter // 2) + i
                    w = raw[:, n % RAW, i * P:(i + 1) * P]
                    tok = tap_planes[:, kv:6:2, 2 * lp:2 * lp + CMP_STRIDE * (N_CMP - 1) + 1:CMP_STRIDE]
                    ins = pe.matmul(bank[:, 0:3 * N_CMP], w, tok, start=lp == 0, stop=lp == 15)
                if quarter == 1:
                    ins.then_inc(*taps_used.mark(n))
                if quarter == 3:
                    ins.then_inc(*turned.mark(("hid", kv)))

            def turn_mix(g, t):
                pe.wait_ge(*(mixed_last.at() if (g, t) == (1, 0) else mix_done.at((g, t))))
                turn(("mix", g, t), [mix_row[:, MIXES.index((g, t)) % 2, k * P:(k + 1) * P] for k in range(4)],
                     (turn_lo, ("mix", g, t)), kind="D")

            def compress(u):
                if u == 0:
                    pe.wait_ge(*copied.at(("cmp", NT - 1)))
                if u in (0, 2, 4, 6):
                    turn_taps(u // 2)
                if u == 3:
                    pe.wait_ge(*dve_step.at(("g1", NT - 1)))
                    turn("gt", [gates[:, t, :] for t in range(NT)], (dve_step, "gt"), kind="D")
                if u == 5:
                    pe.wait_ge(*dve_step.at("gt"))
                    turn("gates", [gate_t[:, t * P:(t + 1) * P] for t in range(NT)], (dve_step, "gates"), kind="D", step=24)
                if u in (7, 8):
                    g = u - 7
                    pe.wait_ge(*biasc_in.at(HEADS - 1))
                    turn(("bc", g), [bias_ct[:, g, t * P:(t + 1) * P] for t in reversed(range(NT))], (dve_step, ("bc", g)), kind="D")
                if u == 10:
                    pe.wait_ge(*dve_step.at("pe_rows"))
                if 10 <= u < 18:
                    hidden((u - 10) // 4, (u - 10) % 4)
                if u == 21:
                    pe.wait_ge(*dve_step.at("hid_k"))
                    bank = take("T", "kc", (dve_step, "kc0"))
                    pe.matmul(bank[0:64, 0:HD], hid_k, const("w2")[:, 0:HD], start=True, stop=True).then_inc(*turned.mark("kc"))
                if u == 23:
                    pe.wait_ge(*dve_step.at(("hid_v", 1)))
                    bank = take("T", "vc", (dve_step, ("vd", 3)))
                    for g in range(2):
                        ins = pe.matmul(bank[:, g * HD:(g + 1) * HD], hid_v[:, g, :, :].rearrange("p h c -> p (h c)"), const("w2")[:, HD:], start=True, stop=True)
                    ins.then_inc(*turned.mark("vc"))
                if u in (19, 21, 23, 25):
                    turn_mix(0, (u - 19) // 2)
                if u == 27:
                    pe.wait_ge(*dve_step.at("kc2"))
                    turn("kcT", [kc_sq], (dve_step, "k_cmp"))

            def project_out(g, t, c, j):
                key = ("wo", g, t, c)
                if j == 0:
                    take("D", key, (x2_done, (g, t, c)))
                    pe.wait_ge(*turn_lo.at(("mix", g, t)))
                dst = D[known["bank", "D", key]]
                i = 4 * g + 2 * c + j
                h, l = piece("wo", i)
                for k in range(2):
                    chunk = 4 * g + 2 * j + k
                    ins = three(dst, (act_hi[:, chunk, t * P:(t + 1) * P], act_lo[:, chunk, t * P:(t + 1) * P]), 512,
                                (h[:, k * 512:(k + 1) * 512], l[:, k * 512:(k + 1) * 512]), j == 0 and k == 0, j == 1 and k == 1)
                if j:
                    ins.then_inc(*dense_done.mark(key))
                elif t == WO_LAST[g]:
                    used(ins, "wo", i)

            def up(half, f, cols):
                dst = up_bank(half, f)[:, cols]
                h, l = piece(("up", half), f)
                for k in range(KD):
                    ws = slice(k * P, (k + 1) * P)
                    pe.matmul(dst, h[:, ws], act_hi[:, k, cols], start=k == 0, stop=False)
                    pe.matmul(dst, h[:, ws], act_lo[:, k, cols], start=False, stop=False)
                    ins = pe.matmul(dst, l[:, ws], act_hi[:, k, cols], start=False, stop=k == KD - 1)
                return ins

            last = len(UNITS)
            pe.wait_ge(*dve_step.at(("turned", ROWS[7])))
            for n in range(N_MLA, last + 10):
                if n < last:
                    if UNITS[n] == ("cmp", NT - 1, 0):
                        pe.wait_ge(*dve_step.at("k_cmp"))
                    score_unit(n)
                compress(n - N_MLA)
                if n - 2 >= N_MLA and n - 2 < last:
                    turn_unit(n - 2)
                if n - 4 >= N_MLA and n - 4 < last:
                    mix_unit(n - 4)
                if n - 9 >= N_MLA and n - 9 < last and UNITS[n - 9][0] == "cmp":
                    turn_mix(1, UNITS[n - 9][1])
                for job in WO_AT.get(n - N_MLA, ()):
                    project_out(*job)
                for t in (3, 2):
                    if n - N_MLA == LN2_AT[t][2]:
                        turn_ln("ln2", t, kind="D")
                if n == last + 6:
                    pe.wait_ge(*turn_lo.at(("ln2", 2, 1)))
                    up(0, 0, slice(2 * P, SEQ))

            turn_ln("ln2", 1)
            for c in range(2):
                for j in range(2):
                    project_out(1, 0, c, j)
            pe.wait_ge(*turn_lo.at(("ln2", 1, 1)))
            up(0, 0, slice(P, 2 * P))
            up(0, 1, slice(P, SEQ))
            turn_ln("ln2", 0)
            up(0, 2, slice(P, SEQ))
            pe.wait_ge(*turn_lo.at(("ln2", 0, 1)))
            for f in range(STARTED):
                up(0, f, slice(0, P)).then_inc(*dense_done.mark(("up", 0, f)))

            for half in range(2):
                for f in range(0 if half else STARTED, UP_HALF):
                    if f >= 4:
                        pe.wait_ge(*relu_done.at((half, f - 4)))
                    elif half:
                        pe.wait_ge(*x2_done.at(("part", 0, f)))
                    up(half, f, slice(0, SEQ)).then_inc(*dense_done.mark(("up", half, f)))
                for c in range(2):
                    for i in range(UP_HALF // 2):
                        h, l = piece(("down", half, c), i)
                        for t in range(NT):
                            dst = down_banks(half, c)[t]
                            if i == 0 and (half or c):
                                if c == 1:
                                    pe.wait_ge(*relu_done.at((half, UP_HALF - 4 + t)))
                                else:
                                    pe.wait_ge(*x2_done.at(("part", 1, t)))
                            for j in range(2):
                                f = 2 * i + j
                                if t == 0:
                                    pe.wait_ge(*a_lo_done.at((half, f)))
                                ins = three(dst, (a_hi[:, f, t * P:(t + 1) * P], a_lo[:, f, t * P:(t + 1) * P]), 512,
                                            (h[:, j * 512:(j + 1) * 512], l[:, j * 512:(j + 1) * 512]), f == 0, f == UP_HALF - 1)
                            if i == UP_HALF // 2 - 1:
                                ins.then_inc(*mixed.mark(("down", half, c, t)))
                            elif t == NT - 1:
                                used(ins, ("down", half, c), i)


def t5_bucket(dist):
    n = np.maximum(dist, 0)
    exact = BUCKETS // 2
    large = np.log(np.maximum(n, 1).astype(np.float32) / np.float32(exact)) / np.float32(np.log(MAX_DIST / exact))
    large = np.minimum(exact + (large * np.float32(BUCKETS - exact)).astype(np.int32), BUCKETS - 1)
    return np.where(n < exact, n, large)


def shape_constants():
    p = np.arange(P)
    mask = np.where(SEQ - 1 - p[:, None] - np.arange(SEQ)[None, :] >= 0, 0.0, MASKED).astype(np.float32)
    half = ROPE // 2
    inv = (1.0 / (np.float32(10000.0) ** (np.arange(half, dtype=np.float32) / np.float32(half)))).astype(np.float32)
    angle = (np.arange(SEQ, dtype=np.float32)[:, None] * inv[None, :]).astype(np.float32)
    c, s = np.cos(angle), np.sin(angle)
    rope = np.concatenate([c, c, -s, s], axis=1).astype(np.float32).reshape(NT, P, 64).transpose(1, 0, 2)
    dist = np.concatenate([SEQ - 1 - np.arange(NEAR), FAR - 1 - np.arange(FAR) - FAR_LEAST])
    onehot = np.zeros((BUCKETS + 1, VEC), np.float32)
    onehot[t5_bucket(dist), np.arange(VEC)] = -1.0
    onehot[:, dist < 0] = 0.0
    onehot[BUCKETS, dist < 0] = 1.0
    return np.eye(P, dtype=np.float32), mask, rope.reshape(P, -1), onehot


def kernel(**inputs):
    import concourse.bacc as bacc
    from concourse.bass_utils import run_bass_kernel_spmd

    v = {k: np.asarray(x) for k, x in inputs.items()}
    rows = lambda *gs: np.ascontiguousarray(np.broadcast_to(np.concatenate([g.reshape(-1) for g in gs])[None, :], (P, sum(g.size for g in gs))))
    chunks = lambda w: w.reshape(-1, P, w.shape[1]).transpose(1, 0, 2)
    w_in, w_up, w_down, w_o = v["w_in"][0], v["w_up"][0], v["w_down"][0], v["w_o"][0]
    weights = np.zeros((len(PIECES), P, 1024), np.float32)
    for n, (what, i, width, _) in enumerate(PIECES):
        if what in IN_BLOCKS:
            block = np.concatenate([w_in[:, lo:lo + m] for lo, m in IN_BLOCKS[what]], axis=1)
            part = chunks(block[2 * i * P:2 * (i + 1) * P])
        elif what in ("uq", "ukv"):
            part = v["mla_w_" + what][0][i * P:(i + 1) * P]
        elif what == "w1":
            part = chunks(v["nsa_cmp_w1"][0, i // 2, 8 * P * (i % 2):8 * P * (i % 2 + 1)])
        elif what == "wo":
            k, c = 4 * (i // 4) + 2 * (i % 2), i // 2 % 2
            part = chunks(w_o[k * P:(k + 2) * P, 512 * c:512 * (c + 1)])
        elif what[0] == "up":
            f = what[1] * UP_HALF + i
            part = chunks(w_up[:, f * P:(f + 1) * P])
        else:
            f = what[1] * UP_HALF + 2 * i
            part = chunks(w_down[f * P:(f + 2) * P, 512 * what[2]:512 * (what[2] + 1)])
        weights[n, :, 0:width] = part.reshape(P, width)
    ident, mask, rope, onehot = shape_constants()
    pe = v["nsa_cmp_pe"][0].reshape(2, CMP_BLOCK // 2, P).transpose(2, 0, 1).reshape(P, -1)
    w2 = v["nsa_cmp_w2"][0].transpose(1, 0, 2).reshape(P, -1)
    consts = np.concatenate([ident, mask, rope, rows(v["mla_q_gain"]), rows(v["mla_k_gain"]), rows(v["nsa_q_gain"]),
                             rows(v["nsa_k_gain"]), pe, w2], axis=1)
    assert consts.shape[1] == CONST_LOADED
    arrays = {
        "x": v["x"][0], "weights": weights, "consts": consts, "onehot": onehot, "rel_bias": v["rel_bias"],
        "gain_ln1": rows(v["ln1_g"]), "gain_c": rows(v["mla_cq_norm_g"], v["mla_ckv_norm_g"]),
        "gain_grp": rows(v["grp_norm_mla"], v["grp_norm_nsa"]), "gain_ln2": rows(v["ln2_g"]),
    }
    arrays = {k: np.ascontiguousarray(x) for k, x in arrays.items()}

    known = {}
    for _ in range(2):
        nc = bacc.Bacc("TRN2", target_bir_lowering=False, num_devices=1)
        ins = {k: nc.dram_tensor(k, x.shape, mybir.dt.from_np(x.dtype), kind="ExternalInput").ap() for k, x in arrays.items()}
        out = nc.dram_tensor("y", (SEQ, D_MODEL), F32, kind="ExternalOutput").ap()
        build(nc, ins, out, known)
    r = run_bass_kernel_spmd(nc, [arrays], core_ids=[0])
    return np.asarray(r.results[0]["y"]).reshape(1, SEQ, D_MODEL)
```
